# Optimizing a Trainium2 kernel written in Bass

```python
import math
import jax, jax.numpy as jnp
from jax import lax
import numpy as np

D_MODEL = 1024
BATCH = 1
SEQ = 256
DEPTH = 2

GRID_W = 64
CTX_LEN = 256
N_MIXERS = 2
EPS = 1e-6
MLA_HEADS = 16
Q_LORA = 512
KV_LORA = 256
QK_NOPE = 64
QK_ROPE = 32
V_HEAD = 64
ROPE_THETA = 10000.0
Q_BLOCK = 128
SSD_EXPAND = 2
SSD_INNER = SSD_EXPAND * D_MODEL
SSD_HEADDIM = 64
SSD_HEADS = SSD_INNER // SSD_HEADDIM
SSD_GROUPS = 4
SSD_STATE = 128
SSD_CONV = 5
SSD_CONV_DIM = SSD_INNER + 2 * SSD_GROUPS * SSD_STATE
SSD_IN_DIM = SSD_INNER + SSD_CONV_DIM + 2 * SSD_HEADS
CHUNK = 128
FFN_HIDDEN = ((8 * D_MODEL // 3 + 255) // 256) * 256

kernel_name = "hybrid_mla_ssd_diffusion_block"

def rms_norm(x, g):
    xf = x.astype(jnp.float32)
    y = xf * lax.rsqrt(jnp.mean(xf * xf, axis=-1, keepdims=True) + EPS)
    return (y * g.astype(jnp.float32)).astype(x.dtype)

def rope_1d(x, pos):
    d = x.shape[-1]
    half = d // 2
    inv = ROPE_THETA ** (-jnp.arange(half, dtype=jnp.float32) * 2.0 / d)
    ang = pos.astype(jnp.float32)[:, None] * inv[None, :]
    cos = jnp.cos(ang)[None, :, None, :]
    sin = jnp.sin(ang)[None, :, None, :]
    xf = x.astype(jnp.float32)
    x1, x2 = xf[..., :half], xf[..., half:]
    return jnp.concatenate([x1 * cos - x2 * sin, x2 * cos + x1 * sin], axis=-1).astype(x.dtype)

def rope_2d(x, row, col):
    h = x.shape[-1] // 2
    return jnp.concatenate([rope_1d(x[..., :h], row), rope_1d(x[..., h:], col)], axis=-1)

def sdpa(q, k, v):
    s = jnp.einsum('bqhd,bshd->bhqs', q, k).astype(jnp.float32) * (1.0 / math.sqrt(q.shape[-1]))
    p = jax.nn.softmax(s, axis=-1).astype(v.dtype)
    return jnp.einsum('bhqs,bshd->bqhd', p, v)

def blocked_sdpa(q, k, v):
    bsz, L, H, dk = q.shape
    nb = L // Q_BLOCK
    qb = q.reshape(bsz, nb, Q_BLOCK, H, dk).transpose(1, 0, 2, 3, 4)
    out = lax.map(lambda blk: sdpa(blk, k, v), qb)
    return out.transpose(1, 0, 2, 3, 4).reshape(bsz, L, H * v.shape[-1])

def mla_mixer(hx, hc, row, col, w_in, q_norm, w_uq, kv_norm, w_ukv, w_o, need_ctx):
    bsz, Lc = hc.shape[0], hc.shape[1]
    h = jnp.concatenate([hc, hx], axis=1)
    T = h.shape[1]
    proj = h @ w_in
    cq, ckv, kr = jnp.split(proj, [Q_LORA, Q_LORA + KV_LORA], axis=-1)
    q = (rms_norm(cq, q_norm) @ w_uq).reshape(bsz, T, MLA_HEADS, QK_NOPE + QK_ROPE)
    kv = (rms_norm(ckv, kv_norm) @ w_ukv).reshape(bsz, T, MLA_HEADS, QK_NOPE + V_HEAD)
    k_nope, v = kv[..., :QK_NOPE], kv[..., QK_NOPE:]
    q_nope, q_rope = q[..., :QK_NOPE], q[..., QK_NOPE:]
    q_rope = jnp.concatenate([q_rope[:, :Lc], rope_2d(q_rope[:, Lc:], row, col)], axis=1)
    kr = kr[:, :, None, :]
    kr = jnp.concatenate([kr[:, :Lc], rope_2d(kr[:, Lc:], row, col)], axis=1)
    k = jnp.concatenate([k_nope, jnp.broadcast_to(kr, (bsz, T, MLA_HEADS, QK_ROPE))], axis=-1)
    q = jnp.concatenate([q_nope, q_rope], axis=-1)
    out_x = blocked_sdpa(q[:, Lc:], k, v) @ w_o
    out_c = None
    if need_ctx:
        out_c = sdpa(q[:, :Lc], k[:, :Lc], v[:, :Lc]).reshape(bsz, Lc, MLA_HEADS * V_HEAD) @ w_o
    return out_x, out_c

def dw_conv(u, w, b):
    C = u.shape[-1]
    K = w.shape[0]
    y = lax.conv_general_dilated(u, w[:, None, :].astype(u.dtype), window_strides=(1,),
                                 padding=[(K // 2, K // 2)], dimension_numbers=('NWC', 'WIO', 'NWC'),
                                 feature_group_count=C)
    return y + b

def ssd_chunked(xs, dt, A, bm, cm, h0):
    bsz, L, H, P = xs.shape
    G, N = bm.shape[2], bm.shape[3]
    Hg = H // G
    nc = L // CHUNK
    xc = xs.reshape(bsz, nc, CHUNK, G, Hg, P)
    dtc = dt.reshape(bsz, nc, CHUNK, G, Hg)
    bc = bm.reshape(bsz, nc, CHUNK, G, N)
    cc = cm.reshape(bsz, nc, CHUNK, G, N)
    cum = jnp.cumsum(dtc * A.reshape(G, Hg), axis=2)
    lower = jnp.tril(jnp.ones((CHUNK, CHUNK), dtype=bool))[None, None, :, :, None, None]
    seg = cum[:, :, :, None] - cum[:, :, None, :]
    decay = jnp.exp(jnp.where(lower, seg, -jnp.inf))
    cb = jnp.einsum('bcqgn,bckgn->bcqkg', cc, bc).astype(jnp.float32)
    w = cb[..., None] * decay * dtc[:, :, None]
    y_diag = jnp.einsum('bcqkgh,bckghp->bcqghp', w, xc)
    to_end = jnp.exp(cum[:, :, -1:] - cum) * dtc
    states = jnp.einsum('bcqgn,bcqgh,bcqghp->bcghpn', bc, to_end, xc)
    chunk_decay = jnp.exp(cum[:, :, -1])

    def step(h, inp):
        s, d = inp
        return d[..., None, None] * h + s, h

    h_last, h_start = lax.scan(step, h0.reshape(bsz, G, Hg, P, N),
                               (jnp.moveaxis(states, 1, 0), jnp.moveaxis(chunk_decay, 1, 0)))
    h_start = jnp.moveaxis(h_start, 0, 1)
    y_off = jnp.einsum('bcqgn,bcghpn,bcqgh->bcqghp', cc, h_start, jnp.exp(cum))
    y = (y_diag + y_off).reshape(bsz, L, H, P).astype(xs.dtype)
    return y, h_last.reshape(bsz, H, P, N)

def ssd_mixer(hx, hc, w_in, conv_w, conv_b, dt_bias, a_log, d_skip, norm_g, w_o, need_ctx):
    bsz, Lc = hc.shape[0], hc.shape[1]
    proj = jnp.concatenate([hc, hx], axis=1) @ w_in
    T = proj.shape[1]
    z, xbc, dt_raw = jnp.split(proj, [SSD_INNER, SSD_INNER + SSD_CONV_DIM], axis=-1)
    xbc = jax.nn.silu(jnp.concatenate([dw_conv(xbc[:, :Lc], conv_w, conv_b),
                                       dw_conv(xbc[:, Lc:], conv_w, conv_b)], axis=1))
    xs, bm, cm = jnp.split(xbc, [SSD_INNER, SSD_INNER + SSD_GROUPS * SSD_STATE], axis=-1)
    xs = xs.reshape(bsz, T, SSD_HEADS, SSD_HEADDIM)
    bm = bm.reshape(bsz, T, SSD_GROUPS, SSD_STATE)
    cm = cm.reshape(bsz, T, SSD_GROUPS, SSD_STATE)
    dt = jax.nn.softplus(dt_raw.reshape(bsz, T, 2, SSD_HEADS).astype(jnp.float32)
                         + dt_bias.astype(jnp.float32))
    A = -jnp.exp(a_log.astype(jnp.float32))
    h0 = jnp.zeros((bsz, SSD_HEADS, SSD_HEADDIM, SSD_STATE), jnp.float32)
    fl = lambda a: jnp.flip(a, axis=1)
    xs_c, xs_x = xs[:, :Lc], xs[:, Lc:]
    bm_c, bm_x = bm[:, :Lc], bm[:, Lc:]
    cm_c, cm_x = cm[:, :Lc], cm[:, Lc:]
    dt_c, dt_x = dt[:, :Lc], dt[:, Lc:]
    yc_f, hcf = ssd_chunked(xs_c, dt_c[:, :, 0], A[0], bm_c, cm_c, h0)
    yx_f, _ = ssd_chunked(xs_x, dt_x[:, :, 0], A[0], bm_x, cm_x, hcf)
    yc_b, hcb = ssd_chunked(fl(xs_c), fl(dt_c[:, :, 1]), A[1], fl(bm_c), fl(cm_c), h0)
    yx_b, _ = ssd_chunked(fl(xs_x), fl(dt_x[:, :, 1]), A[1], fl(bm_x), fl(cm_x), hcb)
    dsk = d_skip[:, None]

    def gate_out(y, zz):
        y = y.reshape(bsz, y.shape[1], SSD_INNER)
        return rms_norm(y * jax.nn.silu(zz), norm_g) @ w_o

    out_x = gate_out(yx_f + fl(yx_b) + dsk * xs_x, z[:, Lc:])
    out_c = None
    if need_ctx:
        out_c = gate_out(yc_f + fl(yc_b) + dsk * xs_c, z[:, :Lc])
    return out_x, out_c

def swiglu(h, w1, w3, w2):
    return (jax.nn.silu(h @ w1) * (h @ w3)) @ w2

def setup_inputs(seed: int = 0) -> dict:
    key = jax.random.key(seed)
    ks = jax.random.split(key, 32)
    NA = (DEPTH + 1) // 2
    NB = DEPTH // 2
    f32 = jnp.float32
    nrm = lambda k, shape, s: jax.random.normal(k, shape, f32) * s
    gain = lambda k, shape: 1.0 + 0.02 * jax.random.normal(k, shape, f32)
    dt0 = jnp.exp(jax.random.uniform(ks[22], (NB, 2, SSD_HEADS), f32, math.log(1e-3), math.log(1e-1)))
    return {
        "x": nrm(ks[0], (BATCH, SEQ, D_MODEL), 1.0),
        "c": nrm(ks[1], (BATCH, D_MODEL), 1.0),
        "ctx": nrm(ks[2], (BATCH, CTX_LEN, D_MODEL), 1.0),
        "c_ctx": nrm(ks[3], (D_MODEL,), 1.0),
        "ada_w": nrm(ks[4], (DEPTH, D_MODEL, 6 * D_MODEL), D_MODEL ** -0.5),
        "ada_b": nrm(ks[5], (DEPTH, 6 * D_MODEL), 0.02),
        "norm_mix": gain(ks[6], (DEPTH, D_MODEL)),
        "norm_ffn": gain(ks[7], (DEPTH, D_MODEL)),
        "ffn_w1": nrm(ks[8], (DEPTH, D_MODEL, FFN_HIDDEN), D_MODEL ** -0.5),
        "ffn_w3": nrm(ks[9], (DEPTH, D_MODEL, FFN_HIDDEN), D_MODEL ** -0.5),
        "ffn_w2": nrm(ks[10], (DEPTH, FFN_HIDDEN, D_MODEL), FFN_HIDDEN ** -0.5),
        "mla_w_in": nrm(ks[11], (NA, D_MODEL, Q_LORA + KV_LORA + QK_ROPE), D_MODEL ** -0.5),
        "mla_q_norm": gain(ks[12], (NA, Q_LORA)),
        "mla_w_uq": nrm(ks[13], (NA, Q_LORA, MLA_HEADS * (QK_NOPE + QK_ROPE)), Q_LORA ** -0.5),
        "mla_kv_norm": gain(ks[14], (NA, KV_LORA)),
        "mla_w_ukv": nrm(ks[15], (NA, KV_LORA, MLA_HEADS * (QK_NOPE + V_HEAD)), KV_LORA ** -0.5),
        "mla_w_o": nrm(ks[16], (NA, MLA_HEADS * V_HEAD, D_MODEL), (MLA_HEADS * V_HEAD) ** -0.5),
        "ssd_w_in": nrm(ks[17], (NB, D_MODEL, SSD_IN_DIM), D_MODEL ** -0.5),
        "ssd_conv_w": nrm(ks[18], (NB, SSD_CONV, SSD_CONV_DIM), SSD_CONV ** -0.5),
        "ssd_conv_b": nrm(ks[19], (NB, SSD_CONV_DIM), 0.02),
        "ssd_dt_bias": dt0 + jnp.log(-jnp.expm1(-dt0)),
        "ssd_a_log": jnp.log(jax.random.uniform(ks[20], (NB, 2, SSD_HEADS), f32, 1.0, 16.0)),
        "ssd_d": gain(ks[21], (NB, SSD_HEADS)),
        "ssd_norm": gain(ks[23], (NB, SSD_INNER)),
        "ssd_w_o": nrm(ks[24], (NB, SSD_INNER, D_MODEL), SSD_INNER ** -0.5),
        "final_norm": gain(ks[25], (D_MODEL,)),
    }

def reference(x, c, ctx, c_ctx, ada_w, ada_b, norm_mix, norm_ffn, ffn_w1, ffn_w3, ffn_w2,
              mla_w_in, mla_q_norm, mla_w_uq, mla_kv_norm, mla_w_ukv, mla_w_o,
              ssd_w_in, ssd_conv_w, ssd_conv_b, ssd_dt_bias, ssd_a_log, ssd_d, ssd_norm, ssd_w_o,
              final_norm):
    L = x.shape[1]
    rows = L // GRID_W
    row = jnp.repeat(jnp.arange(rows), GRID_W)
    col = jnp.tile(jnp.arange(GRID_W), rows)
    sc = jax.nn.silu(c)
    scc = jax.nn.silu(c_ctx)
    for i in range(DEPTH):
        need_ctx = i < DEPTH - 1
        mod_x = jnp.split((sc @ ada_w[i] + ada_b[i])[:, None, :], 6, axis=-1)
        mod_c = jnp.split((scc @ ada_w[i] + ada_b[i])[None, None, :], 6, axis=-1)
        hx = rms_norm(x, norm_mix[i]) * (1.0 + mod_x[1]) + mod_x[0]
        hc = rms_norm(ctx, norm_mix[i]) * (1.0 + mod_c[1]) + mod_c[0]
        j = i // N_MIXERS
        if i % N_MIXERS == 0:
            out_x, out_c = mla_mixer(hx, hc, row, col, mla_w_in[j], mla_q_norm[j], mla_w_uq[j],
                                     mla_kv_norm[j], mla_w_ukv[j], mla_w_o[j], need_ctx)
        else:
            out_x, out_c = ssd_mixer(hx, hc, ssd_w_in[j], ssd_conv_w[j], ssd_conv_b[j], ssd_dt_bias[j],
                                     ssd_a_log[j], ssd_d[j], ssd_norm[j], ssd_w_o[j], need_ctx)
        x = x + mod_x[2] * out_x
        hx = rms_norm(x, norm_ffn[i]) * (1.0 + mod_x[4]) + mod_x[3]
        x = x + mod_x[5] * swiglu(hx, ffn_w1[i], ffn_w3[i], ffn_w2[i])
        if need_ctx:
            ctx = ctx + mod_c[2] * out_c
            hc = rms_norm(ctx, norm_ffn[i]) * (1.0 + mod_c[4]) + mod_c[3]
            ctx = ctx + mod_c[5] * swiglu(hc, ffn_w1[i], ffn_w3[i], ffn_w2[i])
    return rms_norm(x, final_norm)


_drawn_inputs = setup_inputs


def setup_inputs(seed=0):
    import zlib

    import numpy as np

    out = dict(_drawn_inputs(seed))
    spreads = {}
    factors = {'norm_mix': 4.543,
     'norm_ffn': 2.882,
     'mla_q_norm': 8.0,
     'mla_kv_norm': 8.0,
     'ssd_conv_b': 25.156,
     'ssd_d': 64.0,
     'ssd_norm': 36.174,
     'final_norm': 8.308}
    for name, (base, spread) in spreads.items():
        noise = np.random.default_rng([zlib.crc32(name.encode()), seed]).standard_normal(out[name].shape)
        drawn = base * np.exp(spread * noise) if base else spread * noise
        out[name] = __import__('jax').numpy.asarray(drawn.astype(out[name].dtype))
    for name, factor in factors.items():
        out[name] = (out[name] * factor).astype(out[name].dtype)
    return out
```

```python
import numpy as np


D = 1024
CTX = 256
LAT = 256
TOK = CTX + LAT
KD = D // 128
HEADS = 16
ROPE = 32
QKD = 96
KQ = 512 // 128
KKV = 256 // 128
HID = 2816
KH = HID // 128
SH = 32
GH = 8
GROUPS = 4
GW = GH * 64
INNER = 2048
KI = INNER // 128
EPS = 1e-6
GRID_W = 64

PAR = {}
_at = 0
for _name, _n in (("c", 8), ("cctx", 8), ("ada_b", 96), ("norm_mix", 16), ("norm_ffn", 16), ("q_norm", 4),
                  ("kv_norm", 2), ("conv_w", 120), ("conv_b", 24), ("ssd_norm", 16), ("final", 8)):
    PAR[_name] = _at
    _at += _n
NPAR = _at
TAB = {"ident": 0, "gt": 128, "lt": 256, "le": 384, "ge": 512, "cos": 640, "sin": 896}
NTAB = 1152

A0 = 0
IN = A0 + 16
HP = IN + 7
HL = HP + 2
WO = HL + 4 * 15 + 2
F0 = WO + 8
AR = F0 + 4 * KH
G0 = AR + 4
BC = G0 + 3 * KD
DT = BC + 8
XS = DT + 1
ZS = XS + 16
SO = ZS + 16
F1 = SO + 2 * KD
G1 = F1 + 2 * KH
NBLK = G1 + 3 * KD
RING = 4


def block_cols():
    cols = [1024] * NBLK
    for i in range(-1, 15):
        n = HP if i < 0 else HL + 4 * i
        cols[n], cols[n + 1] = 512, 256
    cols[DT] = 512
    return cols


COLS = block_cols()
NORM_K = [8, 4, 2, 8, 8, 16, 8, 8]
NB = [sum(NORM_K[:w]) for w in range(len(NORM_K) + 1)]


def late(t, k):
    return t >= k if isinstance(t, int) else True


def program(nc, a, out):
    import concourse.bass as bass
    from concourse import mybir
    from contextlib import ExitStack

    f32, f32r = mybir.dt.float32, mybir.dt.float32r
    ALU, ACT, AX = mybir.AluOpType, mybir.ActivationFunctionType, mybir.AxisListType
    MUL, ADD, SUB = ALU.mult, ALU.add, ALU.subtract
    ds = bass.ds

    with ExitStack() as fixed:
        def sb(name, shape, dt=f32, stack=fixed):
            return stack.enter_context(nc.sbuf_tensor(name, shape, dt))

        def sem(name):
            return fixed.enter_context(nc.semaphore(name))

        X = sb("residual", [128, KD, TOK])
        raw = [sb(f"raw{i}", [128, 1024]) for i in range(RING)]
        wh = [sb(f"w_hi{i}", [128, 1024], f32r) for i in range(RING)]
        wl = [sb(f"w_lo{i}", [128, 1024], f32r) for i in range(RING)]
        T = sb("scratch", [128, 8, 512])
        par = sb("par", [128, NPAR])
        rows = sb("rows", [128, 160])
        tab = sb("tab", [128, NTAB])
        ones = sb("ones", [128, 128])
        eps = sb("eps", [128, 1])
        sc = sb("silu_c", [128, 2, 8])
        smov = sb("silu_c_parts", [128, 8, 2, 2], f32r)
        mod = [sb(f"mod{i}", [128, 48, 2]) for i in range(2)]
        gain = [sb(f"gain{i}", [128, 8, 2]) for i in range(4)]
        bank = [fixed.enter_context(nc.psum_tensor(f"bank{i}", [128, 512], f32)) for i in range(8)]

        def tabv(name, n=128):
            return tab[:, TAB[name]:TAB[name] + n]

        with ExitStack() as ph:
            Hmh, Hml = (sb(f"mla_h_{p}", [128, KD, TOK], f32r, ph) for p in ("hi", "lo"))
            Oh, Ol = Hmh, Hml
            cq = sb("cq", [128, KQ + KKV, TOK], f32, ph)
            kf = sb("k_rope", [128, TOK], f32, ph)
            cnh, cnl = (sb(f"c_normed_{p}", [128, KQ + KKV, TOK], f32r, ph) for p in ("hi", "lo"))
            qf = sb("q_f32", [128, TOK], f32, ph)
            qh, ql = (sb(f"q_{p}", [128, TOK], f32r, ph) for p in ("hi", "lo"))
            kh, kl = (sb(f"k_{p}", [128, TOK], f32r, ph) for p in ("hi", "lo"))
            vh, vl = (sb(f"v_{p}", [128, 2, 4, 64], f32r, ph) for p in ("hi", "lo"))
            P = sb("probs", [128, 3, 512], f32, ph)
            PTh, PTl = (sb(f"probs_t_{p}", [128, 6, 256], f32r, ph) for p in ("hi", "lo"))
            rtmp = sb("rope_tmp", [128, LAT], f32, ph)
            mx, nm, ssum, rs_ = (sb(f"softmax_{p}", [128, 4], f32, ph) for p in ("max", "negmax", "sum", "inv"))
        with ExitStack() as ph:
            H0h, H0l = (sb(f"ffn0_h_{p}", [128, KD, TOK], f32r, ph) for p in ("hi", "lo"))
            U0h, U0l = (sb(f"ffn0_hidden_{p}", [128, KH, TOK], f32r, ph) for p in ("hi", "lo"))
        with ExitStack() as ph:
            xtok = sb("x_tok", [128, 4, INNER], f32, ph)
            Bth, Btl = (sb(f"B_tok_{p}", [128, 4, GROUPS, 128], f32r, ph) for p in ("hi", "lo"))
            CTh, CTl = (sb(f"C_T_{p}", [128, GROUPS, LAT], f32r, ph) for p in ("hi", "lo"))
            zs = sb("z_gate", [128, KI, LAT], f32, ph)
            dt = sb("dt", [128, 4, 64], f32, ph)
            dtA = sb("dtA", [128, 4, 64], f32, ph)
            dtAh, dtAl = (sb(f"dtA_{p}", [128, 2, 64], f32, ph) for p in ("hi", "lo"))
            w6 = sb("state_w", [128, 6, SH], f32, ph)
            et = sb("exp_sums", [128, 384], f32, ph)
            maskr = sb("masks_r", [128, 2, 128], f32r, ph)
            with ExitStack() as ph2:
                H1h, H1l = (sb(f"ssd_h_{p}", [128, KD, TOK], f32r, ph2) for p in ("hi", "lo"))
                up = sb("conv_in", [128, 2, 2, 260], f32, ph2)
                dtw = sb("dt_work", [128, 6, 256], f32, ph2)
                BTh, BTl = (sb(f"B_T_{p}", [128, GROUPS, LAT], f32r, ph2) for p in ("hi", "lo"))
            with ExitStack() as ph2:
                xsh, xsl = (sb(f"xs_{p}", [128, 2, GW], f32r, ph2) for p in ("hi", "lo"))
                hh, hl = (sb(f"state_{p}", [128, 2, GW], f32r, ph2) for p in ("hi", "lo"))
                mh, ml = (sb(f"dtA_mask_{p}", [128, GH, 128], f32r, ph2) for p in ("hi", "lo"))
                E = sb("decay", [128, GH, 128], f32, ph2)
                xgh, xgl = (sb(f"x_group_{p}", [128, 2, GW], f32r, ph2) for p in ("hi", "lo"))
                Y = sb("y_tok", [128, 2, GW], f32, ph2)
                Wh, Wl = (sb(f"W_{p}", [128, GH, 128], f32r, ph2) for p in ("hi", "lo"))
                cb = sb("CB", [128, 2, GROUPS, 128], f32, ph2)
            with ExitStack() as ph2:
                Hyh, Hyl = (sb(f"y_{p}", [128, KI, LAT], f32r, ph2) for p in ("hi", "lo"))
        with ExitStack() as ph:
            H2h, H2l = (sb(f"ffn1_h_{p}", [128, KD, LAT], f32r, ph) for p in ("hi", "lo"))
            U1h, U1l = (sb(f"ffn1_hidden_{p}", [128, KH, LAT], f32r, ph) for p in ("hi", "lo"))
            yout = sb("y_out", [128, KD, LAT], f32, ph)

        raw_loaded = [sem(f"raw_loaded{i}") for i in range(RING)]
        w_hi, w_lo, w_used = sem("w_hi"), sem("w_lo"), sem("w_used")
        par_in, inputs_in = sem("par_in"), sem("inputs_in")
        ones_set, silu_c, sc_hi, sc_lo = sem("ones_set"), sem("silu_c_done"), sem("sc_hi"), sem("sc_lo")
        mod_step, mod_done = sem("mod_step"), sem("mod_done")
        sq_ready, sq_used, root, inv = sem("sq_ready"), sem("sq_used"), sem("rms_root"), sem("rms_inv")
        nv, nhi, nlo = sem("normed"), sem("normed_hi"), sem("normed_lo")
        proj_out = sem("proj_out")
        kr_part, kr_done, kr_hi, kr_lo = sem("kr_part"), sem("kr_done"), sem("kr_hi"), sem("kr_lo")
        q_cp, rope_part, q_rope, q_hi, q_lo = sem("q_copied"), sem("rope_part"), sem("q_roped"), sem("q_hi_"), sem("q_lo_")
        k_hi, k_lo, v_hi, v_lo = sem("k_hi_"), sem("k_lo_"), sem("v_hi_"), sem("v_lo_")
        s_mm, maxed, nmax, exp_done, rcp, p_norm = (sem(x) for x in ("scores_mm", "maxed", "negmax", "exp_done", "sum_inv", "p_norm"))
        pt_mm, pt_hi, pt_lo, o_mm, o_hi, o_lo = (sem(x) for x in ("pt_mm", "pt_hi", "pt_lo", "o_mm", "o_hi_", "o_lo_"))
        added = sem("added")
        silu_done, hid_f, hid_hi, hid_lo = (sem(x) for x in ("silu_done", "hid_f", "hid_hi", "hid_lo"))
        up_zero, conv_up, conv_init, conv_tap, conv_y, conv_tr, conv_ev, conv_hi, ct_hi, ct_lo = (sem(x) for x in (
            "up_zero", "conv_up", "conv_init", "conv_tap", "conv_y", "conv_tr", "conv_ev", "conv_hi", "ct_hi", "ct_lo"))
        dt_dve, dt_act, cum_mm, cum_exp = (sem(x) for x in ("dt_dve", "dt_act", "cum_mm", "cum_exp"))
        masks_r, dta_hi, w6_done = sem("masks_r_done"), sem("dta_parts"), sem("state_w_done")
        cb_mm, cb_done = sem("cb_mm"), sem("cb_done")
        xs_f, xs_hi, xs_lo, st_mm = (sem(x) for x in ("xs_f", "xs_hi_", "xs_lo_", "states_mm"))
        st_hi, st_dec, st_sum, st_lo, off_mm = (sem(x) for x in ("st_hi", "st_dec", "st_sum", "st_lo", "off_mm"))
        mk, dec_mm, dec_exp, gb, g_step, wf, W_hi, W_lo = (sem(x) for x in ("masked", "dec_mm", "dec_exp", "gb", "g_step", "wf", "W_hi_", "W_lo_"))
        xg_hi, xg_lo, dg_mm, dx, y_step, y_done, yt_mm, yt_done = (sem(x) for x in (
            "xg_hi_", "xg_lo_", "diag_mm", "dx", "y_step", "y_done", "yt_mm", "yt_done"))
        out_done, stored = sem("out_done"), sem("stored")

        block = fixed.enter_context(nc.Block())

        @block.sync
        def _(sp):
            def load(n, s, dst_cols, src):
                if late(n, RING):
                    sp.wait_ge(w_lo, n - RING + 1)
                sp.dma_start(raw[s % RING][:, 0:dst_cols], src).then_inc(raw_loaded[s % RING], 16)

            def ada(n, s, layer, t):
                load(n, s, 1024, a["ada_w"][ds(48 * layer + t, 1), :, :].rearrange("o p n -> (o p) n"))

            def one(name, t):
                return a[name][ds(t, 1), :, :].rearrange("o p n -> (o p) n")

            sp.dma_start(par[:, :], a["par"]).then_inc(par_in, 16)
            for t in range(4):
                ada(A0 + t, A0 + t, 0, t)
            sp.dma_start(X[:, :, :], a["xT"]).then_inc(inputs_in, 16)
            sp.dma_start(tab[:, :], a["tab"]).then_inc(inputs_in, 16)
            sp.dma_start(rows[:, :], a["rows"]).then_inc(inputs_in, 16)
            for t in range(4, 16):
                ada(A0 + t, A0 + t, 0, t)
            for t in range(7):
                load(IN + t, IN + t, 1024, one("w_in", t))
            load(HP, HP, 512, one("w_uq", 0))
            load(HP + 1, HP + 1, 256, one("w_ukv", 0))

            def head(i, u):
                n, s = HL + 4 * i, HL + 4 * u
                load(n, s, 512, one("w_uq", i + 1))
                load(n + 1, s + 1, 256, one("w_ukv", i + 1))
                ada(n + 2, s + 2, 0, 16 + 2 * i)
                ada(n + 3, s + 3, 0, 17 + 2 * i)

            with sp.Fori(0, 15) as i:
                head(i, 0)
            ada(WO - 2, WO - 2, 0, 46)
            ada(WO - 1, WO - 1, 0, 47)
            for t in range(8):
                load(WO + t, WO + t, 1024, one("w_o", t))
            with sp.Fori(0, KH) as j:
                load(F0 + 4 * j, F0, 1024, one("w1", j))
                load(F0 + 4 * j + 1, F0 + 1, 1024, one("w3", j))
                ada(F0 + 4 * j + 2, F0 + 2, 1, 2 * j)
                ada(F0 + 4 * j + 3, F0 + 3, 1, 2 * j + 1)
            for t in range(4):
                ada(AR + t, AR + t, 1, 44 + t)

            def w2(layer, base):
                with sp.Fori(0, 2) as i:
                    for u in range(4):
                        src = one("w2", 8 * layer + 4 * i + u)
                        for r, (k0, k1) in enumerate(((0, 8), (8, 16), (16, KH))):
                            load(base + 12 * i + 3 * u + r, base + 3 * u + r, 128 * (k1 - k0), src[:, 128 * k0:128 * k1])

            w2(0, G0)
            for t in range(8):
                load(BC + t, BC + t, 1024, one("w_xbc", t))
            load(DT, DT, 512, a["w_dt"])
            with sp.Fori(0, 4) as i:
                for u in range(4):
                    load(XS + 4 * i + u, XS + u, 1024, one("w_xbc", 8 + 4 * i + u))
            with sp.Fori(0, 4) as i:
                for u in range(4):
                    load(ZS + 4 * i + u, ZS + u, 1024, one("w_z", 4 * i + u))
            with sp.Fori(0, 4) as i:
                for u in range(4):
                    load(SO + 4 * i + u, SO + u, 1024, one("w_so", 4 * i + u))
            with sp.Fori(0, KH // 2) as i:
                for u in range(2):
                    load(F1 + 4 * i + 2 * u, F1 + 2 * u, 1024, one("w1", KH + 2 * i + u))
                    load(F1 + 4 * i + 2 * u + 1, F1 + 2 * u + 1, 1024, one("w3", KH + 2 * i + u))
            w2(1, G1)
            for k in range(KD):
                sp.wait_ge(out_done, k + 1)
                sp.dma_start(out[:, k, :], yout[:, k, :]).then_inc(stored, 16)
            sp.wait_ge(stored, 16 * KD)

        @block.gpsimd
        def _(pool):
            nc.gpsimd.memset(ones[:, :], 1.0).then_inc(ones_set, 1)
            nc.gpsimd.memset(eps[:, :], EPS).then_inc(ones_set, 1)

            def scale_probs(i):
                for p in range(3):
                    pool.wait_ge(rcp, 3 * i + p + 1)
                    if p < 2:
                        nc.gpsimd.tensor_tensor(P[:, p, :], P[:, p, :], rs_[:, p:p + 1].to_broadcast([128, 512]), MUL).then_inc(p_norm, 1)
                    else:
                        nc.gpsimd.tensor_tensor(P[:, 2, 0:256], P[:, 2, 0:256], rs_[:, 2:3].to_broadcast([128, 256]), MUL)
                        nc.gpsimd.tensor_tensor(P[:, 2, 256:512], P[:, 2, 256:512], rs_[:, 3:4].to_broadcast([128, 256]), MUL).then_inc(p_norm, 1)

            with pool.Fori(0, HEADS) as i:
                scale_probs(i)

            pool.wait_ge(added, 16)
            pool.wait_ge(w_used, BC)
            for u in range(2):
                nc.gpsimd.memset(up[:, u, :, 0:2], 0.0).then_inc(up_zero, 1)
                nc.gpsimd.memset(up[:, u, :, 258:260], 0.0).then_inc(up_zero, 1)

            for g in range(GROUPS):
                hs = slice(GH * g, GH * g + GH)
                if g == 0:
                    pool.wait_ge(w_used, SO)
                    pool.wait_ge(w6_done, 3)
                    pool.wait_ge(conv_ev, 20)
                for s, (tt, row) in enumerate(((0, 0), (1, 2), (0, 1), (1, 3), (2, 4), (3, 5))):
                    m = 6 * g + s
                    if m >= 2:
                        pool.wait_ge(xs_lo, m - 1)
                    nc.gpsimd.tensor_tensor(
                        T[:, s % 2, :].rearrange("p (h d) -> p h d", d=64),
                        xtok[:, tt, GW * g:GW * g + GW].rearrange("p (h d) -> p h d", d=64),
                        w6[:, row, hs].unsqueeze(2).to_broadcast([128, GH, 64]), MUL).then_inc(xs_f, 1)
                if g == 0:
                    pool.wait_ge(dta_hi, 2)
                for c in range(2):
                    for d_, name in ((0, "le"), (1, "ge")):
                        m = 4 * g + 2 * c + d_
                        if m >= 1:
                            pool.wait_ge(dec_mm, m)
                        for dst, src in ((mh, dtAh), (ml, dtAl)):
                            last = nc.gpsimd.tensor_tensor(
                                dst[:, :, :], tabv(name).unsqueeze(1).to_broadcast([128, GH, 128]),
                                src[:, c, 32 * d_ + GH * g:32 * d_ + GH * g + GH].unsqueeze(2).to_broadcast([128, GH, 128]), MUL)
                        last.then_inc(mk, 1)
                    if 2 * g + c >= 1:
                        pool.wait_ge(wf, 3 * (2 * g + c))
                    nc.gpsimd.tensor_tensor(
                        T[:, 4:6, :].rearrange("p a (h q) -> p (a h) q", q=128),
                        tabv("ge").unsqueeze(1).to_broadcast([128, GH, 128]),
                        dt[:, 2 + c, 32 + GH * g:32 + GH * g + GH].unsqueeze(2).to_broadcast([128, GH, 128]), MUL).then_inc(gb, 1)
                    if 2 * g + c >= 1:
                        pool.wait_ge(y_done, 2 * g + c)
                    nc.gpsimd.tensor_tensor(
                        T[:, 7, :].rearrange("p (h d) -> p h d", d=64),
                        xtok[:, 2 + c, GW * g:GW * g + GW].rearrange("p (h d) -> p h d", d=64),
                        rows[:, 128 + GH * g:128 + GH * g + GH].unsqueeze(2).to_broadcast([128, GH, 64]), MUL).then_inc(dx, 1)

        @block.scalar
        def _(act):
            A = nc.scalar.activation

            def hi(n, s):
                if isinstance(n, int) and n >= NBLK:
                    return
                act.wait_ge(raw_loaded[s % RING], 4 * (n - s % RING) + 16)
                if late(n, RING):
                    act.wait_ge(w_used, n - RING + 1)
                c = COLS[s]
                A(wh[s % RING][:, 0:c], raw[s % RING][:, 0:c], ACT.Copy).then_inc(w_hi, 1)

            def norm(w, src, nk, groups, dim, hdst, shift):
                b = NB[w]
                t0, t1 = groups[0][1], groups[-1][2]
                for k in range(nk):
                    if k >= 2:
                        act.wait_ge(sq_used, b + k - 1)
                    A(T[:, k % 2, 0:t1 - t0], src(k, t0, t1), ACT.Square).then_inc(sq_ready, 1)
                act.wait_ge(sq_used, b + nk)
                if w >= 1:
                    act.wait_ge(inv, w)
                A(T[:, 4, 0:t1 - t0], bank[6][:, 0:t1 - t0], ACT.Sqrt, bias=eps[:, 0:1], scale=1.0 / dim).then_inc(root, 1)
                if hdst is None:
                    return
                for k in range(nk):
                    act.wait_ge(nv, b + k + 1)
                    for g, (m, c0, c1) in enumerate(groups):
                        v = T[:, 2 + k % 2, c0 - t0:c1 - t0]
                        if shift is None:
                            ins = A(hdst(k, c0, c1), v, ACT.Copy)
                        else:
                            ins = A(hdst(k, c0, c1), v, ACT.Identity, bias=shift(k, m))
                    ins.then_inc(nhi, 1)

            act.wait_ge(par_in, 16)
            A(sc[:, :, :], par[:, 0:16].rearrange("p (s k) -> p s k", s=2), ACT.Silu).then_inc(silu_c, 1)
            act.wait_ge(silu_c, 1)
            A(smov[:, :, :, 0], sc[:, :, :].rearrange("p s k -> p k s"), ACT.Copy).then_inc(sc_hi, 1)
            for n in range(RING):
                hi(n, n)
            for t in range(16):
                hi(A0 + t + RING, A0 + t + RING)
            act.wait_ge(inputs_in, 48)
            act.wait_ge(ones_set, 2)
            both = [(1, 0, CTX), (0, CTX, TOK)]
            norm(0, lambda k, c0, c1: X[:, k, c0:c1], 8, both, D, lambda k, c0, c1: Hmh[:, k, c0:c1],
                 lambda k, m: mod[0][:, k, m:m + 1])

            for t in range(6):
                act.wait_ge(w_used, IN + t + 1)
                A(cq[:, t, :], bank[t % 2][:, :], ACT.Copy).then_inc(proj_out, 1)
                hi(IN + t + RING, IN + t + RING)
            act.wait_ge(w_used, IN + 7)
            A(kf[64:96, :], bank[0][64:96, :], ACT.Copy).then_inc(proj_out, 1)
            hi(IN + 6 + RING, IN + 6 + RING)
            act.wait_ge(kr_done, 1)
            A(kh[64:96, :], kf[64:96, :], ACT.Copy).then_inc(kr_hi, 1)
            whole = [(0, 0, TOK)]
            norm(1, lambda k, c0, c1: cq[:, k, c0:c1], KQ, whole, 512, lambda k, c0, c1: cnh[:, k, c0:c1], None)
            norm(2, lambda k, c0, c1: cq[:, KQ + k, c0:c1], KKV, whole, 256, lambda k, c0, c1: cnh[:, KQ + k, c0:c1], None)

            def project(i, n, s, u):
                act.wait_ge(w_used, n + 1)
                if late(i, 1):
                    act.wait_ge(q_lo, i)
                    act.wait_ge(s_mm, 3 * i)
                A(qf[0:QKD, :], bank[0][0:QKD, :], ACT.Copy).then_inc(q_cp, 1)
                act.wait_ge(w_used, n + 2)
                A(kh[0:64, :], bank[1][0:64, :], ACT.Copy).then_inc(k_hi, 1)
                if late(i, 2):
                    act.wait_ge(o_mm, i - 1)
                A(vh[:, u, :, :], bank[2][:, 0:256].rearrange("p (t d) -> p t d", d=64), ACT.Copy).then_inc(v_hi, 1)
                act.wait_ge(q_rope, i + 1)
                A(qh[0:QKD, :], qf[0:QKD, :], ACT.Copy).then_inc(q_hi, 1)
                hi(n + 4, s + 4)
                hi(n + 5, s + 5)

            def exps(i, p):
                act.wait_ge(nmax, 3 * i + p + 1)
                if late(i, 1):
                    act.wait_ge(pt_mm, 3 * i - 2 + p)
                    act.wait_ge(rcp, 3 * i - 2 + p)
                scale = float(QKD) ** -0.5
                if p < 2:
                    A(P[:, p, :], bank[p][:, :], ACT.Exp, bias=nm[:, p:p + 1], scale=scale,
                      accum_out=ssum[:, p:p + 1]).then_inc(exp_done, 1)
                else:
                    for t in range(2):
                        A(P[:, 2, 256 * t:256 * t + 256], bank[4][:, 256 * t:256 * t + 256], ACT.Exp,
                          bias=nm[:, 2 + t:3 + t], scale=scale, accum_out=ssum[:, 2 + t:3 + t]).then_inc(exp_done, 1)

            def pt_split(i, p, u):
                act.wait_ge(pt_mm, 3 * i + p + 1)
                if late(i, 1):
                    act.wait_ge(o_mm, i)
                b = bank[5 + (3 * u + p) % 2]
                if p < 2:
                    dst, src = PTh[:, 0:4, 128 * p:128 * p + 128], b[:, :].rearrange("p (k q) -> p k q", q=128)
                else:
                    dst, src = PTh[:, 4:6, :], b[:, :].rearrange("p (k q) -> p k q", q=256)
                A(dst, src, ACT.Copy).then_inc(pt_hi, 1)

            def head(i, j, u):
                n, s = HL + 4 * i, HL + 4 * (i if isinstance(i, int) else u)
                more = not isinstance(i, int) or i < 15
                if more:
                    project(i + 1, n, s, 1 - u)
                for p in range(3):
                    pt_split(i, p, u)
                    if more:
                        exps(i + 1, p)
                act.wait_ge(o_mm, i + 1)
                A(Oh[64 * u:64 * u + 64, ds(j, 1), :].rearrange("p o t -> p (o t)"), bank[3][0:64, :], ACT.Copy).then_inc(o_hi, 1)
                if more:
                    n, s = n + 2, s + 2
                hi(n + 4, s + 4)
                hi(n + 5, s + 5)

            project(0, HP, HP, 0)
            for p in range(3):
                exps(0, p)
            head(0, 0, 0)
            head(1, 0, 1)
            with act.Fori(1, 7) as j:
                head(2 * j, j, 0)
                head(2 * j + 1, j, 1)
            head(14, 7, 0)
            head(15, 7, 1)
            for t in range(8):
                hi(WO + t + RING, WO + t + RING)
            act.wait_ge(added, 8)
            norm(3, lambda k, c0, c1: X[:, k, c0:c1], 8, both, D, lambda k, c0, c1: H0h[:, k, c0:c1],
                 lambda k, m: mod[0][:, 24 + k, m:m + 1])

            def hidden(j, g, u, nt, U, n, s, splits):
                act.wait_ge(w_used, n + 1)
                if late(g, 2):
                    act.wait_ge(hid_f, g - 1)
                A(T[:, u, 0:nt], bank[2 + 2 * u][:, 0:nt], ACT.Silu).then_inc(silu_done, 1)
                hi(n + 4, s + 4)
                hi(n + 5, s + 5)
                act.wait_ge(hid_f, g + 1)
                A(U[:, ds(j, 1), :].rearrange("p o t -> p (o t)"), T[:, 2 + u, 0:nt], ACT.Copy).then_inc(hid_hi, 1)
                for r in range(6, splits):
                    hi(n + r, s + r)

            for j in range(2):
                hidden(j, j, j % 2, TOK, U0h, F0 + 4 * j, F0 + 4 * j, 8)
            with act.Fori(1, KH // 2) as i:
                for u in range(2):
                    hidden(2 * i + u, 2 * i + u, u, TOK, U0h, F0 + 8 * i + 4 * u, F0 + 4 * u, 8)
            for t in range(4):
                hi(AR + t + RING, AR + t + RING)
            for t in range(24):
                hi(G0 + t + RING, G0 + t + RING)

            act.wait_ge(added, 16)
            act.wait_ge(mod_done, 6)
            norm(4, lambda k, c0, c1: X[:, k, c0:c1], 8, both, D, lambda k, c0, c1: H1h[:, k, c0:c1],
                 lambda k, m: mod[1][:, k, m:m + 1])
            act.wait_ge(up_zero, 4)

            def conv(t, n, s, u, kind):
                seg = slice(1, 2) if kind == "C" else slice(0, 2)
                act.wait_ge(w_used, n + 1)
                if late(t, 2):
                    act.wait_ge(conv_tap, 4 * t - 4)
                if kind == "C":
                    A(up[:, u, 1, 2:258], bank[u][:, 256:512], ACT.Copy).then_inc(conv_up, 1)
                else:
                    A(up[:, u, :, 2:258], bank[u][:, :].rearrange("p (s t) -> p s t", s=2), ACT.Copy).then_inc(conv_up, 1)
                act.wait_ge(conv_up, t + 1)
                acc = T[:, u, :].rearrange("p (s t) -> p s t", s=2)[:, seg, :]
                A(acc, up[:, u, seg, 0:256], ACT.Identity, bias=par[:, ds(PAR["conv_b"] + t, 1)],
                  scale=par[:, ds(PAR["conv_w"] + 5 * t, 1)]).then_inc(conv_init, 1)
                hi(n + 4, s + 4)
                act.wait_ge(conv_tap, 4 * t + 4)
                if kind == "x" and late(t, 10):
                    act.wait_ge(conv_tr, t - 5)
                if kind == "B" and t >= 2:
                    act.wait_ge(conv_tr, t - 1)
                    act.wait_ge(ct_lo, t - 1)
                if kind == "C":
                    act.wait_ge(ct_lo, t - 1)
                    act.wait_ge(conv_tr, min(4, t - 1))
                if kind == "x" and isinstance(t, int) and t < 10:
                    act.wait_ge(ct_lo, t - 1)
                y = T[:, 2 + u, :].rearrange("p (s t) -> p s t", s=2)[:, seg, :]
                A(y, acc, ACT.Silu).then_inc(conv_y, 1)
                if kind in "BC":
                    g, dst = t % 4, BTh if kind == "B" else CTh
                    act.wait_ge(conv_y, t + 1)
                    A(dst[:, g, :], T[:, 2 + u, 256:512], ACT.Copy).then_inc(ct_hi, 1)
                if kind == "B":
                    act.wait_ge(conv_tr, t + 1)
                    A(Bth[:, :, t, :], bank[2 + u][:, :].rearrange("p (t n) -> p t n", n=128), ACT.Copy).then_inc(conv_hi, 1)

            for t in range(8):
                conv(t, BC + t, BC + t, t % 2, "BC"[t // 4])
            hi(DT + RING, DT + RING)
            W = dtw
            act.wait_ge(dt_dve, 2)
            A(W[:, 2, :], W[:, 1, :], ACT.Exp, scale=-1.0).then_inc(dt_act, 1)
            A(rows[:, 64:128], rows[:, 64:128], ACT.Exp).then_inc(dt_act, 1)
            act.wait_ge(dt_dve, 3)
            A(W[:, 4, :], W[:, 3, :], ACT.Ln).then_inc(dt_act, 1)
            act.wait_ge(masks_r, 2)

            for u in range(4):
                conv(8 + u, XS + u, XS + u, u % 2, "x")
            with act.Fori(1, 4) as i:
                for u in range(4):
                    conv(8 + 4 * i + u, XS + 4 * i + u, XS + u, u % 2, "x")
            with act.Fori(0, 4) as i:
                for u in range(4):
                    act.wait_ge(w_used, ZS + 4 * i + u + 1)
                    A(zs[:, ds(4 * i + u, 1), :].rearrange("p o t -> p (o t)"), bank[4 + u % 2][:, 0:LAT], ACT.Silu).then_inc(conv_y, 1)
                    hi(ZS + 4 * i + u + 4, ZS + u + 4)
            act.wait_ge(cum_mm, 1)
            A(et[:, :], bank[6][:, 0:384], ACT.Exp).then_inc(cum_exp, 1)

            act.wait_ge(cb_mm, 2)
            for c in range(2):
                A(cb[:, c, :, :], bank[2 + c][:, :].rearrange("p (g q) -> p g q", q=128), ACT.Copy).then_inc(cb_done, 1)
            for g in range(GROUPS):
                for s in range(6):
                    m = 6 * g + s
                    act.wait_ge(xs_f, m + 1)
                    if m >= 2:
                        act.wait_ge(st_mm, m - 1)
                    A(xsh[:, s % 2, :], T[:, s % 2, :], ACT.Copy).then_inc(xs_hi, 1)
                if g == 0:
                    act.wait_ge(conv_ev, 20)
                else:
                    act.wait_ge(dg_mm, 2 * g)
                A(xgh[:, :, :], xtok[:, 2:4, GW * g:GW * g + GW], ACT.Copy).then_inc(xg_hi, 1)
                for d_ in range(2):
                    m = 4 * g + 2 * d_
                    act.wait_ge(st_mm, 6 * g + 6)
                    if m >= 2:
                        act.wait_ge(off_mm, m)
                    A(hh[:, 0, :], bank[d_][:, :], ACT.Copy).then_inc(st_hi, 1)
                    act.wait_ge(st_sum, 2 * g + d_ + 1)
                    A(hh[:, 1, :], T[:, 6, :], ACT.Copy).then_inc(st_hi, 1)
                for c in range(2):
                    m = 2 * g + c
                    act.wait_ge(dec_mm, 2 * m + 2)
                    if m >= 1:
                        act.wait_ge(W_lo, m)
                    for b in range(2):
                        A(E[:, 4 * b:4 * b + 4, :], bank[6 + b][:, :].rearrange("p (h q) -> p h q", q=128), ACT.Exp).then_inc(dec_exp, 1)
                    act.wait_ge(wf, 3 * m + 3)
                    if m >= 1:
                        act.wait_ge(dg_mm, m)
                    A(Wh[:, :, :], E[:, :, :], ACT.Copy).then_inc(W_hi, 1)
            act.wait_ge(yt_done, 8)
            lat = [(0, 0, LAT)]
            norm(5, lambda k, c0, c1: zs[:, k, :], KI, lat, INNER, lambda k, c0, c1: Hyh[:, k, :], None)
            with act.Fori(0, 4) as i:
                for u in range(4):
                    hi(SO + 4 * i + u + 4, SO + u + 4)
            xlat = [(0, CTX, TOK)]
            act.wait_ge(added, 24)
            norm(6, lambda k, c0, c1: X[:, k, c0:c1], 8, xlat, D, lambda k, c0, c1: H2h[:, k, :],
                 lambda k, m: mod[1][:, 24 + k, m:m + 1])
            with act.Fori(0, KH // 2) as i:
                for u in range(2):
                    hidden(2 * i + u, KH + 2 * i + u, u, LAT, U1h, F1 + 4 * i + 2 * u, F1 + 2 * u, 0)
            for t in range(24):
                hi(G1 + t + RING, G1 + t + RING)
            act.wait_ge(added, 32)
            norm(7, lambda k, c0, c1: X[:, k, c0:c1], 8, xlat, D, None, None)

        @block.vector
        def _(dve):
            V = nc.vector

            def lo(n, s):
                if isinstance(n, int) and n >= NBLK:
                    return
                dve.wait_ge(w_hi, n + 1)
                c = COLS[s]
                V.tensor_tensor(wl[s % RING][:, 0:c], raw[s % RING][:, 0:c], wh[s % RING][:, 0:c].bitcast(f32), SUB).then_inc(w_lo, 1)

            def norm(w, src, nk, groups, gn, hdst, ldst, shift):
                b = NB[w]
                t0, t1 = groups[0][1], groups[-1][2]
                dve.wait_ge(root, w + 1)
                V.reciprocal(T[:, 5, 0:t1 - t0], T[:, 4, 0:t1 - t0]).then_inc(inv, 1)
                dve.wait_ge(inv, w + 1)

                def value(k):
                    if k >= 2:
                        dve.wait_ge(nhi, b + k - 1)
                        dve.wait_ge(nlo, b + k - 1)
                    for m, c0, c1 in groups:
                        ins = V.scalar_tensor_tensor(T[:, 2 + k % 2, c0 - t0:c1 - t0], src(k, c0, c1), gn(k, m),
                                                     T[:, 5, c0 - t0:c1 - t0], MUL, MUL)
                    ins.then_inc(nv, 1)

                def low(k):
                    dve.wait_ge(nhi, b + k + 1)
                    for m, c0, c1 in groups:
                        v, h = T[:, 2 + k % 2, c0 - t0:c1 - t0], hdst(k, c0, c1).bitcast(f32)
                        if shift is None:
                            ins = V.tensor_tensor(ldst(k, c0, c1), v, h, SUB)
                        else:
                            ins = V.scalar_tensor_tensor(ldst(k, c0, c1), v, shift(k, m), h, ADD, SUB)
                    ins.then_inc(nlo, 1)

                value(0)
                for k in range(1, nk):
                    value(k)
                    low(k - 1)
                low(nk - 1)

            def mods(layer, t0, t1, k):
                src = bank[7][:, 192 * layer + 4 * t0:192 * layer + 4 * t1].rearrange("p (m h) -> p m h", h=2)
                V.tensor_reduce(mod[layer][:, t0:t1, :].rearrange("p t s -> p (t s)"), src, AX.X, ADD).then_inc(mod_step, 1)
                dve.wait_ge(mod_step, k)
                ab = par[:, PAR["ada_b"] + 48 * layer + t0:PAR["ada_b"] + 48 * layer + t1]
                V.tensor_tensor(mod[layer][:, t0:t1, :], mod[layer][:, t0:t1, :],
                                ab.unsqueeze(2).to_broadcast([128, t1 - t0, 2]), ADD).then_inc(mod_done, 1)

            def gains(which, layer, chunk, name, k):
                dve.wait_ge(mod_done, k)
                g = par[:, PAR[name] + 8 * layer:PAR[name] + 8 * layer + 8]
                V.scalar_tensor_tensor(gain[which][:, :, :], mod[layer][:, 8 * chunk:8 * chunk + 8, :], 1.0,
                                       g.unsqueeze(2).to_broadcast([128, 8, 2]), ADD, MUL).then_inc(mod_done, 1)
                dve.wait_ge(mod_done, k + 1)

            dve.wait_ge(sc_hi, 1)
            V.tensor_tensor(smov[:, :, :, 1], sc[:, :, :].rearrange("p s k -> p k s"), smov[:, :, :, 0].bitcast(f32), SUB).then_inc(sc_lo, 1)
            for n in range(RING):
                lo(n, n)
            for t in range(16):
                lo(A0 + t + RING, A0 + t + RING)
            dve.wait_ge(w_used, A0 + 16)
            mods(0, 0, 16, 1)
            gains(0, 0, 1, "norm_mix", 1)
            both = [(1, 0, CTX), (0, CTX, TOK)]
            dve.wait_ge(inputs_in, 48)
            norm(0, lambda k, c0, c1: X[:, k, c0:c1], 8, both, lambda k, m: gain[0][:, k, m:m + 1],
                 lambda k, c0, c1: Hmh[:, k, c0:c1], lambda k, c0, c1: Hml[:, k, c0:c1], lambda k, m: mod[0][:, k, m:m + 1])
            for t in range(7):
                lo(IN + t + RING, IN + t + RING)
            dve.wait_ge(proj_out, 7)
            V.tensor_tensor(rtmp[64:96, :], bank[0][96:128, CTX:TOK], tab[96:128, TAB["sin"]:TAB["sin"] + LAT], MUL).then_inc(kr_part, 1)
            V.tensor_tensor(kf[64:96, CTX:TOK], kf[64:96, CTX:TOK], tab[64:96, TAB["cos"]:TAB["cos"] + LAT], MUL).then_inc(kr_part, 1)
            dve.wait_ge(kr_part, 2)
            V.tensor_tensor(kf[64:96, CTX:TOK], kf[64:96, CTX:TOK], rtmp[64:96, :], ADD).then_inc(kr_done, 1)
            dve.wait_ge(kr_hi, 1)
            V.tensor_tensor(kl[64:96, :], kf[64:96, :], kh[64:96, :].bitcast(f32), SUB).then_inc(kr_lo, 1)
            whole = [(0, 0, TOK)]
            norm(1, lambda k, c0, c1: cq[:, k, c0:c1], KQ, whole, lambda k, m: par[:, PAR["q_norm"] + k:PAR["q_norm"] + k + 1],
                 lambda k, c0, c1: cnh[:, k, c0:c1], lambda k, c0, c1: cnl[:, k, c0:c1], None)
            norm(2, lambda k, c0, c1: cq[:, KQ + k, c0:c1], KKV, whole, lambda k, m: par[:, PAR["kv_norm"] + k:PAR["kv_norm"] + k + 1],
                 lambda k, c0, c1: cnh[:, KQ + k, c0:c1], lambda k, c0, c1: cnl[:, KQ + k, c0:c1], None)

            def project(i, n, s, u):
                dve.wait_ge(q_cp, i + 1)
                V.tensor_tensor(rtmp[64:96, :], bank[0][96:128, CTX:TOK], tab[96:128, TAB["sin"]:TAB["sin"] + LAT], MUL).then_inc(rope_part, 1)
                V.tensor_tensor(qf[64:96, CTX:TOK], qf[64:96, CTX:TOK], tab[64:96, TAB["cos"]:TAB["cos"] + LAT], MUL).then_inc(rope_part, 1)
                dve.wait_ge(rope_part, 2 * i + 2)
                V.tensor_tensor(qf[64:96, CTX:TOK], qf[64:96, CTX:TOK], rtmp[64:96, :], ADD).then_inc(q_rope, 1)
                dve.wait_ge(k_hi, i + 1)
                V.tensor_tensor(kl[0:64, :], bank[1][0:64, :], kh[0:64, :].bitcast(f32), SUB).then_inc(k_lo, 1)
                dve.wait_ge(v_hi, i + 1)
                V.tensor_tensor(vl[:, u, :, :], bank[2][:, 0:256].rearrange("p (t d) -> p t d", d=64),
                                vh[:, u, :, :].bitcast(f32), SUB).then_inc(v_lo, 1)
                dve.wait_ge(q_hi, i + 1)
                V.tensor_tensor(ql[0:QKD, :], qf[0:QKD, :], qh[0:QKD, :].bitcast(f32), SUB).then_inc(q_lo, 1)
                lo(n + 4, s + 4)
                lo(n + 5, s + 5)

            def maxes(i, p):
                dve.wait_ge(s_mm, 3 * i + p + 1)
                c = slice(p, p + 1) if p < 2 else slice(2, 4)
                if p < 2:
                    V.tensor_reduce(mx[:, c], bank[p][:, :], AX.X, ALU.max).then_inc(maxed, 1)
                else:
                    V.tensor_reduce(mx[:, c], bank[4][:, :].rearrange("p (a k) -> p a k", a=2), AX.X, ALU.max).then_inc(maxed, 1)
                dve.wait_ge(maxed, 3 * i + p + 1)
                V.tensor_scalar(nm[:, c], mx[:, c], -(float(QKD) ** -0.5), None, MUL).then_inc(nmax, 1)

            def inverse(i, p):
                dve.wait_ge(exp_done, 4 * i + (1, 2, 4)[p])
                if late(i, 1):
                    dve.wait_ge(p_norm, 3 * i - 2 + p)
                c = slice(p, p + 1) if p < 2 else slice(2, 4)
                V.reciprocal(rs_[:, c], ssum[:, c]).then_inc(rcp, 1)

            def pt_split(i, p, u):
                dve.wait_ge(pt_hi, 3 * i + p + 1)
                b = bank[5 + (3 * u + p) % 2]
                if p < 2:
                    k, q, src = slice(0, 4), slice(128 * p, 128 * p + 128), b[:, :].rearrange("p (k q) -> p k q", q=128)
                else:
                    k, q, src = slice(4, 6), slice(0, 256), b[:, :].rearrange("p (k q) -> p k q", q=256)
                V.tensor_tensor(PTl[:, k, q], src, PTh[:, k, q].bitcast(f32), SUB).then_inc(pt_lo, 1)

            def head(i, j, u):
                n, s = HL + 4 * i, HL + 4 * (i if isinstance(i, int) else u)
                more = not isinstance(i, int) or i < 15
                if more:
                    project(i + 1, n, s, 1 - u)
                for p in range(3):
                    pt_split(i, p, u)
                    if more:
                        maxes(i + 1, p)
                        if p:
                            inverse(i + 1, p - 1)
                if more:
                    inverse(i + 1, 2)
                dve.wait_ge(o_hi, i + 1)
                o = (slice(64 * u, 64 * u + 64), ds(j, 1), slice(None))
                V.tensor_tensor(Ol[o].rearrange("p o t -> p (o t)"), bank[3][0:64, :],
                                Oh[o].rearrange("p o t -> p (o t)").bitcast(f32), SUB).then_inc(o_lo, 1)
                if more:
                    n, s = n + 2, s + 2
                lo(n + 4, s + 4)
                lo(n + 5, s + 5)

            project(0, HP, HP, 0)
            for p in range(3):
                maxes(0, p)
                inverse(0, p)
            head(0, 0, 0)
            head(1, 0, 1)
            with dve.Fori(1, 7) as j:
                head(2 * j, j, 0)
                head(2 * j + 1, j, 1)
            head(14, 7, 0)
            head(15, 7, 1)
            dve.wait_ge(w_used, WO)
            mods(0, 16, 48, 2)
            gains(1, 0, 4, "norm_ffn", 3)

            def add(used, m, u, layer, chunk, groups):
                dve.wait_ge(w_used, used)
                for src, c0, c1 in groups:
                    x = X[:, ds(m, 1), c0:c1].rearrange("p o t -> p (o t)")
                    b0 = c0 - groups[0][1]
                    ins = V.scalar_tensor_tensor(x, bank[u][:, b0:b0 + c1 - c0],
                                                 mod[layer][:, ds(8 * chunk + m, 1), src], x, MUL, ADD)
                ins.then_inc(added, 1)

            for m in range(8):
                lo(WO + m + RING, WO + m + RING)
                add(WO + m + 1, m, m % 2, 0, 2, both)
            dve.wait_ge(added, 8)
            norm(3, lambda k, c0, c1: X[:, k, c0:c1], 8, both, lambda k, m: gain[1][:, k, m:m + 1],
                 lambda k, c0, c1: H0h[:, k, c0:c1], lambda k, c0, c1: H0l[:, k, c0:c1], lambda k, m: mod[0][:, 24 + k, m:m + 1])

            def hidden(j, g, u, nt, Uh, Ul, n, s, splits):
                lo(n + 4, s + 4)
                dve.wait_ge(w_used, n + 2)
                dve.wait_ge(silu_done, g + 1)
                if late(g, 2):
                    dve.wait_ge(hid_lo, g - 1)
                V.tensor_tensor(T[:, 2 + u, 0:nt], bank[3 + 2 * u][:, 0:nt], T[:, u, 0:nt], MUL).then_inc(hid_f, 1)
                lo(n + 5, s + 5)
                dve.wait_ge(hid_hi, g + 1)
                V.tensor_tensor(Ul[:, ds(j, 1), :].rearrange("p o t -> p (o t)"), T[:, 2 + u, 0:nt],
                                Uh[:, ds(j, 1), :].rearrange("p o t -> p (o t)").bitcast(f32), SUB).then_inc(hid_lo, 1)
                for r in range(6, splits):
                    lo(n + r, s + r)

            for j in range(2):
                hidden(j, j, j % 2, TOK, U0h, U0l, F0 + 4 * j, F0 + 4 * j, 8)
            with dve.Fori(1, KH // 2) as i:
                for u in range(2):
                    hidden(2 * i + u, 2 * i + u, u, TOK, U0h, U0l, F0 + 8 * i + 4 * u, F0 + 4 * u, 8)
            for t in range(4):
                lo(AR + t + RING, AR + t + RING)
            dve.wait_ge(w_used, G0)
            mods(1, 0, 48, 3)
            gains(2, 1, 1, "norm_mix", 5)
            gains(3, 1, 4, "norm_ffn", 6)
            for m in range(8):
                for r in range(3):
                    lo(G0 + 3 * m + r + RING, G0 + 3 * m + r + RING)
                add(G0 + 3 * m + 3, m, m % 2, 0, 5, both)
            dve.wait_ge(added, 16)

            norm(4, lambda k, c0, c1: X[:, k, c0:c1], 8, both, lambda k, m: gain[2][:, k, m:m + 1],
                 lambda k, c0, c1: H1h[:, k, c0:c1], lambda k, c0, c1: H1l[:, k, c0:c1], lambda k, m: mod[1][:, k, m:m + 1])

            def conv(t, n, s, u, kind):
                seg = slice(1, 2) if kind == "C" else slice(0, 2)
                acc = T[:, u, :].rearrange("p (s t) -> p s t", s=2)[:, seg, :]
                dve.wait_ge(conv_init, t + 1)
                for r in range(1, 5):
                    if r > 1:
                        dve.wait_ge(conv_tap, 4 * t + r - 1)
                    V.scalar_tensor_tensor(acc, up[:, u, seg, r:r + 256], par[:, ds(PAR["conv_w"] + 5 * t + r, 1)],
                                           acc, MUL, ADD).then_inc(conv_tap, 1)
                lo(n + 4, s + 4)
                if kind in "BC":
                    g, h, l = t % 4, (BTh if kind == "B" else CTh), (BTl if kind == "B" else CTl)
                    dve.wait_ge(ct_hi, t + 1)
                    V.tensor_tensor(l[:, g, :], T[:, 2 + u, 256:512], h[:, g, :].bitcast(f32), SUB).then_inc(ct_lo, 1)
                if kind == "B":
                    dve.wait_ge(conv_hi, t + 1)
                    V.tensor_tensor(Btl[:, :, t, :], bank[2 + u][:, :].rearrange("p (t n) -> p t n", n=128),
                                    Bth[:, :, t, :].bitcast(f32), SUB).then_inc(conv_ev, 1)

            def to_tokens(t, u):
                dve.wait_ge(conv_tr, t - 3)
                V.tensor_copy(xtok[:, :, ds(128 * (t - 8), 128)], bank[2 + u][:, :].rearrange("p (t n) -> p t n", n=128)).then_inc(conv_ev, 1)

            for t in range(8):
                conv(t, BC + t, BC + t, t % 2, "BC"[t // 4])
            lo(DT + RING, DT + RING)
            W = dtw
            dve.wait_ge(w_used, DT + 1)
            V.tensor_tensor(W[:, 0, :].rearrange("p (t h) -> p t h", t=4), bank[4][:, 0:256].rearrange("p (t h) -> p t h", t=4),
                            rows[:, 0:64].unsqueeze(1).to_broadcast([128, 4, 64]), ADD).then_inc(dt_dve, 1)
            dve.wait_ge(dt_dve, 1)
            V.scalar_tensor_tensor(W[:, 1, :], W[:, 0, :], -1.0, W[:, 0, :], MUL, ALU.max).then_inc(dt_dve, 1)
            dve.wait_ge(dt_act, 1)
            V.tensor_scalar(W[:, 3, :], W[:, 2, :], 1.0, None, ADD).then_inc(dt_dve, 1)
            dve.wait_ge(dt_dve, 3)
            V.tensor_scalar(W[:, 5, :], W[:, 3, :], -1.0, None, ADD).then_inc(dt_dve, 1)
            dve.wait_ge(dt_dve, 4)
            V.tensor_scalar(W[:, 1, :], W[:, 5, :], 0.0, None, ALU.is_equal).then_inc(dt_dve, 1)
            dve.wait_ge(dt_dve, 5)
            V.tensor_tensor(W[:, 5, :], W[:, 5, :], W[:, 1, :], ADD).then_inc(dt_dve, 1)
            dve.wait_ge(dt_act, 3)
            V.tensor_tensor(W[:, 4, :], W[:, 4, :], W[:, 1, :], ADD).then_inc(dt_dve, 1)
            dve.wait_ge(dt_dve, 7)
            V.reciprocal(W[:, 5, :], W[:, 5, :]).then_inc(dt_dve, 1)
            dve.wait_ge(dt_dve, 8)
            V.tensor_tensor(W[:, 4, :], W[:, 4, :], W[:, 5, :], MUL).then_inc(dt_dve, 1)
            dve.wait_ge(dt_dve, 9)
            V.tensor_tensor(W[:, 4, :], W[:, 4, :], W[:, 2, :], MUL).then_inc(dt_dve, 1)
            dve.wait_ge(dt_dve, 10)
            V.scalar_tensor_tensor(dt[:, :, :].rearrange("p t h -> p (t h)"), W[:, 0, :], 0.0, W[:, 4, :], ALU.max, ADD).then_inc(dt_dve, 1)
            dve.wait_ge(dt_dve, 11)
            V.scalar_tensor_tensor(dtA[:, :, :], dt[:, :, :], -1.0, rows[:, 64:128].unsqueeze(1).to_broadcast([128, 4, 64]), MUL, MUL).then_inc(dt_dve, 1)
            dve.wait_ge(dt_dve, 12)
            V.tensor_copy(maskr[:, 0, :], tabv("gt")).then_inc(masks_r, 1)
            V.tensor_copy(maskr[:, 1, :], tabv("lt")).then_inc(masks_r, 1)
            V.tensor_copy(dtAh[:, :, :].bitcast(f32r), dtA[:, 2:4, :]).then_inc(dta_hi, 1)
            dve.wait_ge(dta_hi, 1)
            V.tensor_tensor(dtAl[:, :, :].bitcast(f32r), dtA[:, 2:4, :], dtAh[:, :, :], SUB).then_inc(dta_hi, 1)

            conv(8, XS, XS, 0, "x")
            for u in range(1, 4):
                conv(8 + u, XS + u, XS + u, u % 2, "x")
                to_tokens(7 + u, 1 - u % 2)
            with dve.Fori(1, 4) as i:
                for u in range(4):
                    conv(8 + 4 * i + u, XS + 4 * i + u, XS + u, u % 2, "x")
                    to_tokens(7 + 4 * i + u, 1 - u % 2)
            to_tokens(23, 1)
            with dve.Fori(0, 4) as i:
                for u in range(4):
                    lo(ZS + 4 * i + u + 4, ZS + u + 4)
            dve.wait_ge(cum_exp, 1)
            V.tensor_tensor(w6[:, 0:4, :].rearrange("p s h -> p (s h)"), et[:, 0:128], dt[:, 0:2, :].rearrange("p t h -> p (t h)"), MUL).then_inc(w6_done, 1)
            V.tensor_tensor(w6[:, 4, :], et[:, 128:160], dt[:, 2, 0:32], MUL).then_inc(w6_done, 1)
            V.tensor_tensor(w6[:, 5, :], et[:, 160:192], dt[:, 3, 32:64], MUL).then_inc(w6_done, 1)

            steps = {"y": 0, "g": 0}

            def heads64(ap):
                return ap.rearrange("p (h d) -> p h d", d=64)

            for g in range(GROUPS):
                for s in range(6):
                    m = 6 * g + s
                    dve.wait_ge(xs_hi, m + 1)
                    V.tensor_tensor(xsl[:, s % 2, :], T[:, s % 2, :], xsh[:, s % 2, :].bitcast(f32), SUB).then_inc(xs_lo, 1)
                dve.wait_ge(xg_hi, g + 1)
                V.tensor_tensor(xgl[:, :, :], xtok[:, 2:4, GW * g:GW * g + GW], xgh[:, :, :].bitcast(f32), SUB).then_inc(xg_lo, 1)
                for d_ in range(2):
                    q = 2 * g + d_
                    dve.wait_ge(st_hi, 2 * q + 1)
                    V.tensor_tensor(hl[:, 0, :], bank[d_][:, :], hh[:, 0, :].bitcast(f32), SUB).then_inc(st_lo, 1)
                    dtot = et[:, 320 + 32 * d_ + GH * g:320 + 32 * d_ + GH * g + GH]
                    if q >= 1:
                        dve.wait_ge(st_lo, 2 * q)
                    V.tensor_tensor(heads64(T[:, 6, :]), heads64(bank[d_][:, :]), dtot.unsqueeze(2).to_broadcast([128, GH, 64]), MUL).then_inc(st_dec, 1)
                    dve.wait_ge(st_dec, q + 1)
                    V.tensor_tensor(T[:, 6, :], T[:, 6, :], bank[2 + d_][:, :], ADD).then_inc(st_sum, 1)
                    dve.wait_ge(st_hi, 2 * q + 2)
                    V.tensor_tensor(hl[:, 1, :], T[:, 6, :], hh[:, 1, :].bitcast(f32), SUB).then_inc(st_lo, 1)
                    for z in range(2):
                        c = z if d_ == 0 else 1 - z
                        dve.wait_ge(off_mm, 2 * q + z + 1)
                        ec = et[:, 192 + 64 * c + 32 * d_ + GH * g:192 + 64 * c + 32 * d_ + GH * g + GH].unsqueeze(2).to_broadcast([128, GH, 64])
                        src = bank[4 + c] if d_ == 0 else bank[2 * c]
                        if d_ == 0:
                            if g:
                                dve.wait_ge(yt_mm, 2 * g)
                            V.tensor_tensor(heads64(Y[:, c, :]), heads64(src[:, :]), ec, MUL).then_inc(y_step, 1)
                            steps["y"] += 1
                        else:
                            dve.wait_ge(st_lo, 2 * q + 2)
                            V.tensor_tensor(heads64(T[:, 6, :]), heads64(src[:, :]), ec, MUL).then_inc(y_step, 1)
                            steps["y"] += 1
                            dve.wait_ge(y_step, steps["y"])
                            V.tensor_tensor(Y[:, c, :], Y[:, c, :], T[:, 6, :], ADD).then_inc(y_step, 1)
                            steps["y"] += 1
                            dve.wait_ge(y_step, steps["y"])
                for c in range(2):
                    m = 2 * g + c
                    G = T[:, 2:4, :].rearrange("p a (h q) -> p (a h) q", q=128)
                    Gb = T[:, 4:6, :].rearrange("p a (h q) -> p (a h) q", q=128)
                    V.tensor_tensor(G, tabv("le").unsqueeze(1).to_broadcast([128, GH, 128]),
                                    dt[:, 2 + c, GH * g:GH * g + GH].unsqueeze(2).to_broadcast([128, GH, 128]), MUL).then_inc(g_step, 1)
                    dve.wait_ge(gb, m + 1)
                    dve.wait_ge(g_step, 2 * m + 1)
                    V.tensor_tensor(G, G, Gb, ADD).then_inc(wf, 1)
                    dve.wait_ge(wf, 3 * m + 1)
                    V.tensor_tensor(G, G, cb[:, c, g, :].unsqueeze(1).to_broadcast([128, GH, 128]), MUL).then_inc(wf, 1)
                    dve.wait_ge(wf, 3 * m + 2)
                    dve.wait_ge(dec_exp, 2 * m + 2)
                    V.tensor_tensor(E[:, :, :], E[:, :, :], G, MUL).then_inc(wf, 1)
                    dve.wait_ge(W_hi, m + 1)
                    V.tensor_tensor(Wl[:, :, :], E[:, :, :], Wh[:, :, :].bitcast(f32), SUB).then_inc(W_lo, 1)
                    dve.wait_ge(dx, m + 1)
                    V.tensor_tensor(Y[:, c, :], Y[:, c, :], T[:, 7, :], ADD).then_inc(g_step, 1)
                    dve.wait_ge(g_step, 2 * m + 2)
                    dve.wait_ge(dg_mm, m + 1)
                    V.tensor_tensor(Y[:, c, :], Y[:, c, :], bank[4 + c][:, :], ADD).then_inc(y_done, 1)
                    dve.wait_ge(yt_mm, m + 1)
                    z = zs[:, 4 * g:4 * g + 4, 128 * c:128 * c + 128]
                    V.tensor_tensor(z, bank[1][:, :].rearrange("p (f q) -> p f q", q=128), z, MUL).then_inc(yt_done, 1)
            lat = [(0, 0, LAT)]
            dve.wait_ge(yt_done, 8)
            norm(5, lambda k, c0, c1: zs[:, k, :], KI, lat, lambda k, m: par[:, PAR["ssd_norm"] + k:PAR["ssd_norm"] + k + 1],
                 lambda k, c0, c1: Hyh[:, k, :], lambda k, c0, c1: Hyl[:, k, :], None)
            xlat = [(0, CTX, TOK)]
            with dve.Fori(0, 4) as i:
                for u in range(2):
                    for r in range(2):
                        lo(SO + 4 * i + 2 * u + r + 4, SO + 2 * u + r + 4)
                    add(SO + 4 * i + 2 * u + 2, 2 * i + u, u, 1, 2, xlat)
            dve.wait_ge(added, 24)
            norm(6, lambda k, c0, c1: X[:, k, c0:c1], 8, xlat, lambda k, m: gain[3][:, k, m:m + 1],
                 lambda k, c0, c1: H2h[:, k, :], lambda k, c0, c1: H2l[:, k, :], lambda k, m: mod[1][:, 24 + k, m:m + 1])
            with dve.Fori(0, KH // 2) as i:
                for u in range(2):
                    hidden(2 * i + u, KH + 2 * i + u, u, LAT, U1h, U1l, F1 + 4 * i + 2 * u, F1 + 2 * u, 0)
            for m in range(8):
                for r in range(3):
                    lo(G1 + 3 * m + r + RING, G1 + 3 * m + r + RING)
                add(G1 + 3 * m + 3, m, m % 2, 1, 5, xlat)
            dve.wait_ge(added, 32)
            dve.wait_ge(root, 8)
            V.reciprocal(T[:, 5, 0:LAT], T[:, 4, 0:LAT]).then_inc(inv, 1)
            dve.wait_ge(inv, 8)
            for k in range(KD):
                V.scalar_tensor_tensor(yout[:, k, :], X[:, k, CTX:TOK], par[:, PAR["final"] + k:PAR["final"] + k + 1],
                                       T[:, 5, 0:LAT], MUL, MUL).then_inc(out_done, 1)

        @block.tensor
        def _(pe):
            mm = nc.tensor.matmul

            def three(o, lh, ll, rh, rl, first, final):
                mm(o, lh, rl, start=first, stop=False)
                mm(o, lh, rh, start=False, stop=False)
                return mm(o, ll, rh, start=False, stop=final)

            def tile(n, s, o, h, l, k0, nk, first, final, kwait=None):
                pe.wait_ge(w_lo, n + 1)
                for k in range(nk):
                    if kwait is not None:
                        pe.wait_ge(nlo, kwait + k0 + k + 1)
                    w = slice(128 * k, 128 * k + 128)
                    last = three(o, wh[s % RING][:, w], wl[s % RING][:, w], h(k0 + k), l(k0 + k),
                                 first and k == 0, final and k == nk - 1)
                return last

            def ada(n, s, layer, t):
                pe.wait_ge(w_lo, n + 1)
                o = bank[7][:, ds(192 * layer + 4 * t, 4)]
                for k in range(8):
                    r = smov[:, k, :, :].rearrange("p s h -> p (s h)")
                    w = slice(128 * k, 128 * k + 128)
                    mm(o, wh[s % RING][:, w], r, start=k == 0, stop=False)
                    last = mm(o, wl[s % RING][:, w], r, start=False, stop=k == 7)
                last.then_inc(w_used, 1)

            def norm(w, nk, n):
                if w >= 1:
                    pe.wait_ge(root, w)
                for k in range(nk):
                    pe.wait_ge(sq_ready, NB[w] + k + 1)
                    mm(bank[6][:, 0:n], ones[:, :], T[:, k % 2, 0:n], start=k == 0, stop=k == nk - 1).then_inc(sq_used, 1)

            pe.wait_ge(sc_lo, 1)
            for t in range(16):
                ada(A0 + t, A0 + t, 0, t)
            norm(0, 8, TOK)
            for t in range(7):
                if t >= 2:
                    pe.wait_ge(proj_out, t - 1)
                tile(IN + t, IN + t, bank[t % 2][:, :], lambda k: Hmh[:, k, :], lambda k: Hml[:, k, :], 0, 8,
                     True, True, NB[0] if t == 0 else None).then_inc(w_used, 1)
            norm(1, KQ, TOK)
            norm(2, KKV, TOK)

            def project(i, n, s):
                if late(i, 1):
                    pe.wait_ge(exp_done, 4 * i - 3)
                else:
                    pe.wait_ge(kr_done, 1)
                    pe.wait_ge(nlo, NB[3])
                tile(n, s, bank[0][:, :], lambda k: cnh[:, k, :], lambda k: cnl[:, k, :], 0, KQ, True, True).then_inc(w_used, 1)
                pe.wait_ge(w_lo, n + 2)
                if late(i, 1):
                    pe.wait_ge(exp_done, 4 * i - 2)
                s1 = (s + 1) % RING
                for k in range(KKV):
                    w = slice(128 * k, 128 * k + 64)
                    three(bank[1][0:64, :], wh[s1][:, w], wl[s1][:, w], cnh[:, KQ + k, :], cnl[:, KQ + k, :], k == 0, k == KKV - 1)
                if late(i, 1):
                    pe.wait_ge(v_lo, i)
                for t in range(4):
                    for k in range(KKV):
                        w, tk = slice(128 * k + 64, 128 * k + 128), slice(128 * t, 128 * t + 128)
                        last = three(bank[2][:, 64 * t:64 * t + 64], cnh[:, KQ + k, tk], cnl[:, KQ + k, tk],
                                     wh[s1][:, w], wl[s1][:, w], k == 0, k == KKV - 1)
                last.then_inc(w_used, 1)

            def scores(i, p):
                if p == 0:
                    pe.wait_ge(q_lo, i + 1)
                    pe.wait_ge(k_lo, i + 1)
                if p < 2:
                    q = slice(CTX + 128 * p, CTX + 128 * p + 128)
                    last = three(bank[p][:, :], qh[0:QKD, q], ql[0:QKD, q], kh[0:QKD, :], kl[0:QKD, :], True, True)
                else:
                    if late(i, 1):
                        pe.wait_ge(exp_done, 4 * i)
                    for t in range(2):
                        q = slice(128 * t, 128 * t + 128)
                        last = three(bank[4][:, 256 * t:256 * t + 256], qh[0:QKD, q], ql[0:QKD, q],
                                     kh[0:QKD, 0:CTX], kl[0:QKD, 0:CTX], True, True)
                last.then_inc(s_mm, 1)

            def transpose_probs(i, p, u):
                pe.wait_ge(p_norm, 3 * i + p + 1)
                if late(i, 1) or p == 2:
                    pe.wait_ge(pt_lo, 3 * i + p - 1)
                b = bank[5 + (3 * u + p) % 2]
                if p < 2:
                    for k in range(4):
                        last = nc.tensor.transpose(b[:, 128 * k:128 * k + 128], P[:, p, 128 * k:128 * k + 128], tabv("ident"))
                else:
                    for k in range(2):
                        for t in range(2):
                            last = nc.tensor.transpose(b[:, 256 * k + 128 * t:256 * k + 128 * t + 128],
                                                       P[:, 2, 256 * t + 128 * k:256 * t + 128 * k + 128], tabv("ident"))
                last.then_inc(pt_mm, 1)

            def values(i, u):
                pe.wait_ge(pt_lo, 3 * i + 3)
                pe.wait_ge(v_lo, i + 1)
                if late(i, 1):
                    pe.wait_ge(o_lo, i)
                for k in range(4):
                    three(bank[3][0:64, CTX:TOK], vh[:, u, k, :], vl[:, u, k, :], PTh[:, k, :], PTl[:, k, :], k == 0, k == 3)
                for k in range(2):
                    last = three(bank[3][0:64, 0:CTX], vh[:, u, k, :], vl[:, u, k, :], PTh[:, 4 + k, :], PTl[:, 4 + k, :], k == 0, k == 1)
                last.then_inc(o_mm, 1)

            def head(i, u):
                n, s = HL + 4 * i, HL + 4 * (i if isinstance(i, int) else u)
                more = not isinstance(i, int) or i < 15
                if more:
                    project(i + 1, n, s)
                for p in range(3):
                    transpose_probs(i, p, u)
                    if more:
                        scores(i + 1, p)
                values(i, u)
                if more:
                    n, s = n + 2, s + 2
                ada(n, s, 0, 16 + 2 * i)
                ada(n + 1, s + 1, 0, 17 + 2 * i)

            pe.wait_ge(mod_done, 2)
            project(0, HP, HP)
            pe.wait_ge(kr_lo, 1)
            for p in range(3):
                scores(0, p)
            head(0, 0)
            head(1, 1)
            with pe.Fori(1, 7) as j:
                head(2 * j, 0)
                head(2 * j + 1, 1)
            head(14, 0)
            head(15, 1)

            pe.wait_ge(o_lo, HEADS)
            for m in range(8):
                if m >= 2:
                    pe.wait_ge(added, m - 1)
                tile(WO + m, WO + m, bank[m % 2][:, :], lambda k: Oh[:, k, :], lambda k: Ol[:, k, :], 0, 8, True, True).then_inc(w_used, 1)
            norm(3, 8, TOK)

            def ffn(j, g, u, nt, h, l, n, s, kwait):
                if late(g, 2):
                    pe.wait_ge(silu_done, g - 1)
                tile(n, s, bank[2 + 2 * u][:, 0:nt], h, l, 0, 8, True, True, kwait).then_inc(w_used, 1)
                if late(g, 2):
                    pe.wait_ge(hid_f, g - 1)
                tile(n + 1, s + 1, bank[3 + 2 * u][:, 0:nt], h, l, 0, 8, True, True).then_inc(w_used, 1)

            pe.wait_ge(mod_done, 4)
            h0 = (lambda k: H0h[:, k, :]), (lambda k: H0l[:, k, :])
            for j in range(2):
                ffn(j, j, j % 2, TOK, *h0, F0 + 4 * j, F0 + 4 * j, NB[3] if j == 0 else None)
                ada(F0 + 4 * j + 2, F0 + 4 * j + 2, 1, 2 * j)
                ada(F0 + 4 * j + 3, F0 + 4 * j + 3, 1, 2 * j + 1)
            with pe.Fori(1, KH // 2) as i:
                for u in range(2):
                    n, s = F0 + 8 * i + 4 * u, F0 + 4 * u
                    ffn(2 * i + u, 2 * i + u, u, TOK, *h0, n, s, None)
                    ada(n + 2, s + 2, 1, 4 * i + 2 * u)
                    ada(n + 3, s + 3, 1, 4 * i + 2 * u + 1)
            for t in range(4):
                ada(AR + t, AR + t, 1, 44 + t)

            def w2(q0, base, nt, h, l):
                with pe.Fori(0, 2) as i:
                    for u in range(4):
                        pe.wait_ge(added, q0 + 4 * i + u - 1)
                        for r, (k0, nk) in enumerate(((0, 8), (8, 8), (16, KH - 16))):
                            tile(base + 12 * i + 3 * u + r, base + 3 * u + r, bank[u % 2][:, 0:nt], h, l, k0, nk,
                                 r == 0, r == 2).then_inc(w_used, 1)

            pe.wait_ge(hid_lo, KH)
            w2(8, G0, TOK, lambda k: U0h[:, k, :], lambda k: U0l[:, k, :])

            norm(4, 8, TOK)

            def conv_tile(t, n, s, u, kind, kwait):
                if late(t, 2):
                    pe.wait_ge(conv_up, t - 1)
                c = slice(CTX, TOK) if kind == "C" else slice(0, TOK)
                tile(n, s, bank[u][:, c], lambda k: H1h[:, k, c], lambda k: H1l[:, k, c], 0, 8, True, True, kwait).then_inc(w_used, 1)

            def to_tokens(t, u, r):
                pe.wait_ge(conv_y, t + 1)
                if late(r, 2):
                    pe.wait_ge(conv_ev, r - 1)
                for k in range(4):
                    last = nc.tensor.transpose(bank[2 + u][:, 128 * k:128 * k + 128], T[:, 2 + u, 128 * k:128 * k + 128], tabv("ident"))
                last.then_inc(conv_tr, 1)

            for t in range(8):
                conv_tile(t, BC + t, BC + t, t % 2, "BC"[t // 4], NB[4] if t == 0 else None)
                if 1 <= t <= 4:
                    to_tokens(t - 1, (t - 1) % 2, t - 1)
            pe.wait_ge(w_lo, DT + 1)
            for t in range(4):
                for k in range(8):
                    w, tk, sl = slice(64 * k, 64 * k + 64), slice(128 * t, 128 * t + 128), DT % RING
                    last = three(bank[4][:, 64 * t:64 * t + 64], H1h[:, k, tk], H1l[:, k, tk], wh[sl][:, w], wl[sl][:, w], k == 0, k == 7)
            last.then_inc(w_used, 1)
            conv_tile(8, XS, XS, 0, "x", None)
            for u in range(1, 4):
                conv_tile(8 + u, XS + u, XS + u, u % 2, "x", None)
                to_tokens(7 + u, 1 - u % 2, 3 + u)
            with pe.Fori(1, 4) as i:
                for u in range(4):
                    conv_tile(8 + 4 * i + u, XS + 4 * i + u, XS + u, u % 2, "x", None)
                    to_tokens(7 + 4 * i + u, 1 - u % 2, 3 + 4 * i + u)
            to_tokens(23, 1, 19)
            pe.wait_ge(dt_dve, 1)
            with pe.Fori(0, 4) as i:
                for u in range(4):
                    pe.wait_ge(conv_y, 23 + 4 * i + u)
                    tile(ZS + 4 * i + u, ZS + u, bank[4 + u % 2][:, 0:LAT], lambda k: H1h[:, k, CTX:TOK],
                         lambda k: H1l[:, k, CTX:TOK], 0, 8, True, True).then_inc(w_used, 1)
            pe.wait_ge(dt_dve, 12)
            F, B = slice(0, SH), slice(SH, 2 * SH)
            sums = (("gt", 0, F, 1), ("lt", 0, B, None), ("gt", 1, F, None), ("lt", 1, B, 0),
                    ("gt", 2, F, None), ("lt", 3, B, None), ("le", 2, F, None), ("ge", 2, B, None),
                    ("le", 3, F, None), ("ge", 3, B, None), (None, 2, F, None), (None, 3, B, None))
            for q, (name, tt, hs, whole) in enumerate(sums):
                o = bank[6][:, SH * q:SH * q + SH]
                last = mm(o, tabv(name) if name else ones[:, :], dtA[:, tt, hs], start=True, stop=whole is None)
                if whole is not None:
                    last = mm(o, ones[:, :], dtA[:, whole, hs], start=False, stop=True)
            last.then_inc(cum_mm, 1)
            pe.wait_ge(ct_lo, 8)
            pe.wait_ge(conv_ev, 20)
            for c in range(2):
                cs = slice(128 * c, 128 * c + 128)
                for g in range(GROUPS):
                    last = three(bank[2 + c][:, 128 * g:128 * g + 128], BTh[:, g, cs], BTl[:, g, cs], CTh[:, g, cs], CTl[:, g, cs], True, True)
                last.then_inc(cb_mm, 1)

            def decay(g, c):
                for d_ in range(2):
                    m = 4 * g + 2 * c + d_
                    pe.wait_ge(mk, m + 1)
                    if d_ == 0 and 2 * g + c >= 1:
                        pe.wait_ge(dec_exp, 2 * (2 * g + c))
                    if m == 0:
                        pe.wait_ge(cum_exp, 1)
                    for b in range(2):
                        for part in (mh, ml):
                            last = mm(bank[6 + b][:, :], maskr[:, d_, :], part[:, 4 * b:4 * b + 4, :].rearrange("p h q -> p (h q)"),
                                      start=d_ == 0 and part is mh, stop=d_ == 1 and part is ml)
                    last.then_inc(dec_mm, 1)

            pe.wait_ge(masks_r, 2)
            for g in range(GROUPS):
                if g:
                    pe.wait_ge(yt_done, 2 * g)
                else:
                    pe.wait_ge(cb_done, 2)
                for s, (tt, b) in enumerate(((0, 0), (1, 0), (0, 1), (1, 1), (2, 2), (3, 3))):
                    pe.wait_ge(xs_lo, 6 * g + s + 1)
                    three(bank[b][:, :], Bth[:, tt, g, :], Btl[:, tt, g, :], xsh[:, s % 2, :], xsl[:, s % 2, :],
                          s in (0, 2, 4, 5), s in (1, 3, 4, 5)).then_inc(st_mm, 1)
                decay(g, 0)
                for d_ in range(2):
                    for z in range(2):
                        c = z if d_ == 0 else 1 - z
                        pe.wait_ge(st_lo, 4 * g + 2 * d_ + z + 1)
                        cs = slice(128 * c, 128 * c + 128)
                        three(bank[4 + c if d_ == 0 else 2 * c][:, :], CTh[:, g, cs], CTl[:, g, cs], hh[:, z, :], hl[:, z, :],
                              True, True).then_inc(off_mm, 1)
                decay(g, 1)
                pe.wait_ge(xg_lo, g + 1)
                for c in range(2):
                    m = 2 * g + c
                    pe.wait_ge(W_lo, m + 1)
                    for h in range(GH):
                        xs = slice(64 * h, 64 * h + 64)
                        last = three(bank[4 + c][:, xs], Wh[:, h, :], Wl[:, h, :], xgh[:, c, xs], xgl[:, c, xs], True, True)
                    last.then_inc(dg_mm, 1)
                    pe.wait_ge(y_done, m + 1)
                    if m:
                        pe.wait_ge(yt_done, m)
                    for f in range(4):
                        last = nc.tensor.transpose(bank[1][:, 128 * f:128 * f + 128], Y[:, c, 128 * f:128 * f + 128], tabv("ident"))
                    last.then_inc(yt_mm, 1)
            norm(5, KI, LAT)
            pe.wait_ge(nlo, NB[6])
            with pe.Fori(0, 4) as i:
                for u in range(2):
                    pe.wait_ge(added, 15 + 2 * i + u)
                    for r in range(2):
                        tile(SO + 4 * i + 2 * u + r, SO + 2 * u + r, bank[u][:, 0:LAT], lambda k: Hyh[:, k, :], lambda k: Hyl[:, k, :],
                             8 * r, 8, r == 0, r == 1).then_inc(w_used, 1)
            norm(6, 8, LAT)
            pe.wait_ge(nlo, NB[7])
            with pe.Fori(0, KH // 2) as i:
                for u in range(2):
                    ffn(2 * i + u, KH + 2 * i + u, u, LAT, lambda k: H2h[:, k, :], lambda k: H2l[:, k, :], F1 + 4 * i + 2 * u, F1 + 2 * u, None)
            pe.wait_ge(hid_lo, 2 * KH)
            w2(24, G1, LAT, lambda k: U1h[:, k, :], lambda k: U1l[:, k, :])
            norm(7, 8, LAT)


def tiles(w, cols=128):
    k, m = w.shape
    return np.ascontiguousarray(w.reshape(k // 128, 128, m // cols, cols).transpose(2, 1, 0, 3).reshape(m // cols, 128, -1))


def columns(v):
    return v.reshape(-1, 128).T


def swap_halves():
    return np.concatenate([np.arange(8, 16), np.arange(0, 8), np.arange(24, 32), np.arange(16, 24)])


def shape_tables():
    i = np.arange(128)
    r, c = i[:, None], i[None, :]
    t = np.zeros((128, NTAB), np.float32)
    for name, m in (("ident", r == c), ("gt", r > c), ("lt", r < c), ("le", r <= c), ("ge", r >= c)):
        t[:, TAB[name]:TAB[name] + 128] = m
    tok = np.arange(LAT)
    inv = (10000.0 ** (-np.arange(8, dtype=np.float32) * 2.0 / 16)).astype(np.float32)
    for axis, pos in ((0, tok // GRID_W), (1, tok % GRID_W)):
        ang = (pos.astype(np.float32)[None, :] * inv[:, None]).astype(np.float32)
        for half, sign in ((0, -1.0), (1, 1.0)):
            at = 16 * axis + 8 * half
            t[64 + at:72 + at, TAB["cos"]:TAB["cos"] + LAT] = np.cos(ang)
            t[96 + at:104 + at, TAB["sin"]:TAB["sin"] + LAT] = sign * np.sin(ang)
    return t


def lay_out(i):
    o = {}
    o["xT"] = np.concatenate([i["ctx"][0], i["x"][0]], axis=0).T.reshape(KD, 128, TOK).transpose(1, 0, 2)
    cw, cbias = i["ssd_conv_w"][0], i["ssd_conv_b"][0]
    order = np.concatenate([np.arange(INNER, INNER + 1024), np.arange(INNER)])
    cwt = cw[:, order].reshape(5, 24, 128).transpose(2, 1, 0).reshape(128, 120)
    o["par"] = np.concatenate([
        columns(i["c"][0]), columns(i["c_ctx"]), columns(i["ada_b"].reshape(-1)), columns(i["norm_mix"].reshape(-1)),
        columns(i["norm_ffn"].reshape(-1)), columns(i["mla_q_norm"][0]), columns(i["mla_kv_norm"][0]), cwt,
        columns(cbias[order]), columns(i["ssd_norm"][0]), columns(i["final_norm"])], axis=1)
    r = np.concatenate([i["ssd_dt_bias"][0].reshape(-1), i["ssd_a_log"][0].reshape(-1), i["ssd_d"][0]])
    o["rows"] = np.broadcast_to(r, (128, 160))
    o["tab"] = shape_tables()
    o["ada_w"] = np.concatenate([tiles(w) for w in i["ada_w"]])
    w = i["mla_w_in"][0]
    o["w_in"] = tiles(np.concatenate([w[:, 0:768], w[:, 704:800], w[:, 768 + swap_halves()]], axis=1))
    q = i["mla_w_uq"][0].reshape(512, HEADS, QKD)
    o["w_uq"] = tiles(np.concatenate([q, q[:, :, 64 + swap_halves()]], axis=2).reshape(512, -1))
    o["w_ukv"] = tiles(i["mla_w_ukv"][0])
    o["w_o"] = tiles(i["mla_w_o"][0])
    for n in ("w1", "w3", "w2"):
        o[n] = np.concatenate([tiles(w) for w in i["ffn_" + n]])
    w = i["ssd_w_in"][0]
    o["w_z"] = tiles(w[:, 0:INNER])
    xbc = w[:, INNER:INNER + 3072]
    o["w_xbc"] = tiles(xbc[:, order])
    o["w_dt"] = tiles(w[:, INNER + 3072:], 64)[0]
    o["w_so"] = tiles(i["ssd_w_o"][0]).reshape(8, 128, 2, 1024).transpose(0, 2, 1, 3).reshape(16, 128, 1024)
    return {k: np.ascontiguousarray(v) for k, v in o.items()}


def kernel(**inputs):
    import concourse.bacc as bacc
    from concourse import mybir
    from concourse.bass_utils import run_bass_kernel_spmd

    nc = bacc.Bacc("TRN2", target_bir_lowering=False, num_devices=1, dynamic_dma_scratch_size=1024)
    arrays = lay_out({k: np.asarray(v) for k, v in inputs.items()})
    aps = {k: nc.dram_tensor("in_" + k, v.shape, mybir.dt.from_np(v.dtype), kind="ExternalInput").ap() for k, v in arrays.items()}
    out = nc.dram_tensor("out", (128, KD, LAT), mybir.dt.float32, kind="ExternalOutput").ap()
    program(nc, aps, out)
    r = run_bass_kernel_spmd(nc, [{"in_" + k: v for k, v in arrays.items()}], core_ids=[0])
    got = r.results[0]["out"]
    return np.ascontiguousarray(got.transpose(2, 1, 0).reshape(1, LAT, D))
```

```python
import numpy as np


D = 1024
CTX = 256
LAT = 256
TOK = CTX + LAT
KD = D // 128
HEADS = 16
ROPE = 32
QKD = 96
KQ = 512 // 128
KKV = 256 // 128
HID = 2816
KH = HID // 128
SH = 32
GH = 8
GROUPS = 4
GW = GH * 64
INNER = 2048
KI = INNER // 128
EPS = 1e-6
GRID_W = 64

PAR = {}
_at = 0
for _name, _n in (("c", 8), ("cctx", 8), ("ada_b", 96), ("norm_mix", 16), ("norm_ffn", 16), ("q_norm", 4),
                  ("kv_norm", 2), ("conv_w", 120), ("conv_b", 24), ("ssd_norm", 16), ("final", 8)):
    PAR[_name] = _at
    _at += _n
NPAR = _at
TAB = {"ident": 0, "gt": 128, "lt": 256, "le": 384, "ge": 512, "cos": 640, "sin": 896}
NTAB = 1152

A0 = 0
IN = A0 + 16
VB = IN + 7
HP = VB + 2
HL = HP + 2
WO = HL + 4 * 15 + 2
F0 = WO + 8
G0 = F0 + 4 * KH
BC = G0 + 3 * KD + 4
DT = BC + 8
XS = DT + 1
ZS = XS + 16
SO = ZS + 16
F1 = SO + 2 * KD
G1 = F1 + 2 * KH
NBLK = G1 + 3 * KD
RING = 4


def g0(m):
    return G0 + 3 * m + 2 * min(m, 2)


def block_cols():
    cols = [1024] * NBLK
    for i in range(-1, 15):
        n = HP if i < 0 else HL + 4 * i
        cols[n], cols[n + 1] = 512, 128
    cols[DT] = 512
    return cols


COLS = block_cols()
NORM_K = [8, 2, 4, 8, 8, 16, 8, 8]
NB = [sum(NORM_K[:w]) for w in range(len(NORM_K) + 1)]
NORM_BANK = [6, 7, 6, 6, 6, 6, 6, 6]


def late(t, k):
    return t >= k if isinstance(t, int) else True


def program(nc, a, out):
    import concourse.bass as bass
    from concourse import mybir
    from contextlib import ExitStack

    f32, f32r = mybir.dt.float32, mybir.dt.float32r
    ALU, ACT, AX = mybir.AluOpType, mybir.ActivationFunctionType, mybir.AxisListType
    MUL, ADD, SUB = ALU.mult, ALU.add, ALU.subtract
    ds = bass.ds

    with ExitStack() as fixed:
        def sb(name, shape, dt=f32, stack=fixed):
            return stack.enter_context(nc.sbuf_tensor(name, shape, dt))

        def sem(name):
            return fixed.enter_context(nc.semaphore(name))

        X = sb("residual", [128, KD, TOK])
        raw = [sb(f"raw{i}", [128, 1024]) for i in range(RING)]
        wh = [sb(f"w_hi{i}", [128, 1024], f32r) for i in range(RING)]
        wl = [sb(f"w_lo{i}", [128, 1024], f32r) for i in range(RING)]
        T = sb("scratch", [128, 8, 512])
        par = sb("par", [128, NPAR])
        rows = sb("rows", [128, 160])
        tab = sb("tab", [128, NTAB])
        ones = sb("ones", [128, 128])
        eps = sb("eps", [128, 1])
        sc = sb("silu_c", [128, 2, 8])
        smov = sb("silu_c_parts", [128, 8, 2, 2], f32r)
        mrow = sb("mod_rows", [4, 256])
        mod = [sb(f"mod{i}", [128, 48, 2]) for i in range(2)]
        gain = [sb(f"gain{i}", [128, 8, 2]) for i in range(4)]
        bank = [fixed.enter_context(nc.psum_tensor(f"bank{i}", [128, 512], f32)) for i in range(8)]

        def tabv(name, n=128):
            return tab[:, TAB[name]:TAB[name] + n]

        with ExitStack() as ph:
            Hmh, Hml = (sb(f"mla_h_{p}", [128, KD, TOK], f32r, ph) for p in ("hi", "lo"))
            Oh, Ol = Hmh, Hml
            cq = sb("cq", [128, KQ + KKV, TOK], f32, ph)
            kf = sb("k_rope", [128, TOK], f32, ph)
            cnh, cnl = (sb(f"c_normed_{p}", [128, KQ + KKV, TOK], f32r, ph) for p in ("hi", "lo"))
            qf = sb("q_f32", [128, TOK], f32, ph)
            qh, ql = (sb(f"q_{p}", [128, TOK], f32r, ph) for p in ("hi", "lo"))
            kh, kl = (sb(f"k_{p}", [128, TOK], f32r, ph) for p in ("hi", "lo"))
            vh, vl = (sb(f"v_{p}", [128, 4, 64 * HEADS], f32r, ph) for p in ("hi", "lo"))
            vsh, vsl = (sb(f"v_head_{p}", [128, 2, 4, 64], f32r, ph) for p in ("hi", "lo"))
            P, rtmp = T[:, 5:8, :], T[:, 4, 0:LAT]
            PTh, PTl = (sb(f"probs_t_{p}", [128, 6, 256], f32r, ph) for p in ("hi", "lo"))
            mx, nm, ssum, rs_ = (sb(f"softmax_{p}", [128, 4], f32, ph) for p in ("max", "negmax", "sum", "inv"))
        with ExitStack() as ph:
            H0h, H0l = (sb(f"ffn0_h_{p}", [128, KD, TOK], f32r, ph) for p in ("hi", "lo"))
            U0h, U0l = (sb(f"ffn0_hidden_{p}", [128, KH, TOK], f32r, ph) for p in ("hi", "lo"))
        with ExitStack() as ph:
            xtok = sb("x_tok", [128, 4, INNER], f32, ph)
            Bth, Btl = (sb(f"B_tok_{p}", [128, 4, GROUPS, 128], f32r, ph) for p in ("hi", "lo"))
            CTh, CTl = (sb(f"C_T_{p}", [128, GROUPS, LAT], f32r, ph) for p in ("hi", "lo"))
            zs = sb("z_gate", [128, KI, LAT], f32, ph)
            dt = sb("dt", [128, 4, 64], f32, ph)
            dtA = sb("dtA", [128, 4, 64], f32, ph)
            dtAh, dtAl = (sb(f"dtA_{p}", [128, 2, 64], f32, ph) for p in ("hi", "lo"))
            w6 = sb("state_w", [128, 6, SH], f32, ph)
            et = sb("exp_sums", [128, 384], f32, ph)
            maskr = sb("masks_r", [128, 2, 128], f32r, ph)
            with ExitStack() as ph2:
                H1h, H1l = (sb(f"ssd_h_{p}", [128, KD, TOK], f32r, ph2) for p in ("hi", "lo"))
                up = sb("conv_in", [128, 2, 2, 260], f32, ph2)
                dtw = sb("dt_work", [128, 6, 256], f32, ph2)
                dtT = sb("dt_T", [64, TOK], f32, ph2)
                BTh, BTl = (sb(f"B_T_{p}", [128, GROUPS, LAT], f32r, ph2) for p in ("hi", "lo"))
            with ExitStack() as ph2:
                xsh, xsl = (sb(f"xs_{p}", [128, 2, GW], f32r, ph2) for p in ("hi", "lo"))
                hh, hl = (sb(f"state_{p}", [128, 2, GW], f32r, ph2) for p in ("hi", "lo"))
                mh, ml = (sb(f"dtA_mask_{p}", [128, GH, 128], f32r, ph2) for p in ("hi", "lo"))
                E = sb("decay", [128, GH, 128], f32, ph2)
                xgh, xgl = (sb(f"x_group_{p}", [128, 2, GW], f32r, ph2) for p in ("hi", "lo"))
                Y = sb("y_tok", [128, 2, GW], f32, ph2)
                Wh, Wl = (sb(f"W_{p}", [128, GH, 128], f32r, ph2) for p in ("hi", "lo"))
                cb = sb("CB", [128, 2, GROUPS, 128], f32, ph2)
            with ExitStack() as ph2:
                Hyh, Hyl = (sb(f"y_{p}", [128, KI, LAT], f32r, ph2) for p in ("hi", "lo"))
        with ExitStack() as ph:
            H2h, H2l = (sb(f"ffn1_h_{p}", [128, KD, LAT], f32r, ph) for p in ("hi", "lo"))
            U1h, U1l = (sb(f"ffn1_hidden_{p}", [128, KH, LAT], f32r, ph) for p in ("hi", "lo"))
            yout = sb("y_out", [128, KD, LAT], f32, ph)

        raw_loaded = [sem(f"raw_loaded{i}") for i in range(RING)]
        w_hi, w_lo, w_used = sem("w_hi"), sem("w_lo"), sem("w_used")
        par_in, x_in, inputs_in = sem("par_in"), sem("x_in"), sem("inputs_in")
        ones_set, silu_c, sc_hi, sc_lo = sem("ones_set"), sem("silu_c_done"), sem("sc_hi"), sem("sc_lo")
        row_cp, row_tr, mod_ev, mod_done = sem("row_copied"), sem("row_turned"), sem("mod_out"), sem("mod_done")
        sq_ready, sq_used, root, inv = sem("sq_ready"), sem("sq_used"), sem("rms_root"), sem("rms_inv")
        nv, nhi, nlo = sem("normed"), sem("normed_hi"), sem("normed_lo")
        proj_out = sem("proj_out")
        kr_part, kr_done, kr_hi, kr_lo = sem("kr_part"), sem("kr_done"), sem("kr_hi"), sem("kr_lo")
        q_cp, rope_part, q_rope, q_hi, q_lo = sem("q_copied"), sem("rope_part"), sem("q_roped"), sem("q_hi_"), sem("q_lo_")
        k_hi, k_lo, v_hi, v_lo, v_mm, v_cp = sem("k_hi_"), sem("k_lo_"), sem("v_hi_"), sem("v_lo_"), sem("v_mm"), sem("v_cp")
        dt_cp, dt_tr = sem("dt_copied"), sem("dt_turned")
        s_mm, maxed, nmax, exp_done, rcp, p_norm = (sem(x) for x in ("scores_mm", "maxed", "negmax", "exp_done", "sum_inv", "p_norm"))
        pt_mm, pt_hi, pt_lo, o_mm, o_hi, o_lo = (sem(x) for x in ("pt_mm", "pt_hi", "pt_lo", "o_mm", "o_hi_", "o_lo_"))
        added = sem("added")
        silu_done, hid_f, hid_hi, hid_lo = (sem(x) for x in ("silu_done", "hid_f", "hid_hi", "hid_lo"))
        up_zero, conv_up, conv_init, conv_tap, conv_y, conv_tr, conv_ev, conv_hi, ct_hi, ct_lo = (sem(x) for x in (
            "up_zero", "conv_up", "conv_init", "conv_tap", "conv_y", "conv_tr", "conv_ev", "conv_hi", "ct_hi", "ct_lo"))
        dt_dve, dt_act, cum_mm, cum_exp = (sem(x) for x in ("dt_dve", "dt_act", "cum_mm", "cum_exp"))
        masks_r, dta_hi, w6_done = sem("masks_r_done"), sem("dta_parts"), sem("state_w_done")
        cb_mm, cb_done = sem("cb_mm"), sem("cb_done")
        xs_f, xs_hi, xs_lo, st_mm = (sem(x) for x in ("xs_f", "xs_hi_", "xs_lo_", "states_mm"))
        st_hi, st_dec, st_sum, st_lo, off_mm = (sem(x) for x in ("st_hi", "st_dec", "st_sum", "st_lo", "off_mm"))
        mk, dec_mm, dec_exp, gb, g_step, wf, W_hi, W_lo = (sem(x) for x in ("masked", "dec_mm", "dec_exp", "gb", "g_step", "wf", "W_hi_", "W_lo_"))
        xg_hi, xg_lo, dg_mm, dx, y_step, y_done, yt_mm, yt_done = (sem(x) for x in (
            "xg_hi_", "xg_lo_", "diag_mm", "dx", "y_step", "y_done", "yt_mm", "yt_done"))
        out_done, stored = sem("out_done"), sem("stored")

        block = fixed.enter_context(nc.Block())

        @block.sync
        def _(sp):
            def load(n, s, dst_cols, src):
                if late(n, RING):
                    sp.wait_ge(w_lo, n - RING + 1)
                sp.dma_start(raw[s % RING][:, 0:dst_cols], src).then_inc(raw_loaded[s % RING], 16)

            def one(name, t):
                return a[name][ds(t, 1), :, :].rearrange("o p n -> (o p) n")

            def ada(n, s, q):
                load(n, s, 1024, one("ada_w", 2 * q))
                load(n + 1, s + 1, 1024, one("ada_w", 2 * q + 1))

            sp.dma_start(par[:, :], a["par"]).then_inc(par_in, 16)
            ada(A0, A0, 0)
            sp.dma_start(tab[:, :], a["tab"]).then_inc(inputs_in, 16)
            sp.dma_start(rows[:, :], a["rows"]).then_inc(inputs_in, 16)
            for q in range(1, 3):
                ada(A0 + 2 * q, A0 + 2 * q, q)
            sp.dma_start(X[:, :, :], a["xT"]).then_inc(x_in, 16)
            for q in range(3, 8):
                ada(A0 + 2 * q, A0 + 2 * q, q)
            for t in range(7):
                load(IN + t, IN + t, 1024, one("w_in", t))
            for t in range(2):
                load(VB + t, VB + t, 1024, one("w_uv", t))
            load(HP, HP, 512, one("w_uq", 0))
            load(HP + 1, HP + 1, 128, one("w_uk", 0))
            with sp.Fori(0, 15) as i:
                n = HL + 4 * i
                load(n, HL, 512, one("w_uq", i + 1))
                load(n + 1, HL + 1, 128, one("w_uk", i + 1))
                ada(n + 2, HL + 2, 8 + i)
            ada(WO - 2, WO - 2, 23)
            for t in range(8):
                load(WO + t, WO + t, 1024, one("w_o", t))
            with sp.Fori(0, KH) as j:
                load(F0 + 4 * j, F0, 1024, one("w1", j))
                load(F0 + 4 * j + 1, F0 + 1, 1024, one("w3", j))
                ada(F0 + 4 * j + 2, F0 + 2, 24 + j)

            K3 = ((0, 8), (8, 16), (16, KH))
            for m in range(8):
                for r, (k0, k1) in enumerate(K3):
                    load(g0(m) + r, g0(m) + r, 128 * (k1 - k0), one("w2", m)[:, 128 * k0:128 * k1])
                if m < 2:
                    ada(g0(m) + 3, g0(m) + 3, 46 + m)
            for t in range(8):
                load(BC + t, BC + t, 1024, one("w_xbc", t))
            load(DT, DT, 512, a["w_dt"])
            with sp.Fori(0, 4) as i:
                for u in range(4):
                    load(XS + 4 * i + u, XS + u, 1024, one("w_xbc", 8 + 4 * i + u))
            with sp.Fori(0, 4) as i:
                for u in range(4):
                    load(ZS + 4 * i + u, ZS + u, 1024, one("w_z", 4 * i + u))
            with sp.Fori(0, 4) as i:
                for u in range(4):
                    load(SO + 4 * i + u, SO + u, 1024, one("w_so", 4 * i + u))
            with sp.Fori(0, KH // 2) as i:
                for u in range(2):
                    load(F1 + 4 * i + 2 * u, F1 + 2 * u, 1024, one("w1", KH + 2 * i + u))
                    load(F1 + 4 * i + 2 * u + 1, F1 + 2 * u + 1, 1024, one("w3", KH + 2 * i + u))
            with sp.Fori(0, 2) as i:
                for u in range(4):
                    for r, (k0, k1) in enumerate(K3):
                        load(G1 + 12 * i + 3 * u + r, G1 + 3 * u + r, 128 * (k1 - k0), one("w2", 8 + 4 * i + u)[:, 128 * k0:128 * k1])
            for k in range(KD):
                sp.wait_ge(out_done, k + 1)
                sp.dma_start(out[:, k, :], yout[:, k, :]).then_inc(stored, 16)
            sp.wait_ge(stored, 16 * KD)

        @block.gpsimd
        def _(pool):
            nc.gpsimd.memset(ones[:, :], 1.0).then_inc(ones_set, 1)
            nc.gpsimd.memset(eps[:, :], EPS).then_inc(ones_set, 1)

            def scale_probs(i, u):
                pool.wait_ge(rcp, 3 * i + 1)
                if late(i, 2):
                    pool.wait_ge(o_mm, i - 1)
                nc.gpsimd.tensor_tensor(P[:, 0, :], P[:, 0, :], rs_[:, 0:1].to_broadcast([128, 512]), MUL).then_inc(p_norm, 1)
                nc.gpsimd.tensor_copy(vsh[:, u, :, :], vh[:, :, ds(64 * i, 64)])
                nc.gpsimd.tensor_copy(vsl[:, u, :, :], vl[:, :, ds(64 * i, 64)]).then_inc(v_cp, 1)
                pool.wait_ge(rcp, 3 * i + 2)
                nc.gpsimd.tensor_tensor(P[:, 1, :], P[:, 1, :], rs_[:, 1:2].to_broadcast([128, 512]), MUL).then_inc(p_norm, 1)
                pool.wait_ge(rcp, 3 * i + 3)
                nc.gpsimd.tensor_tensor(P[:, 2, :].rearrange("p (a k) -> p a k", a=2), P[:, 2, :].rearrange("p (a k) -> p a k", a=2),
                                        rs_[:, 2:4].unsqueeze(2).to_broadcast([128, 2, 256]), MUL).then_inc(p_norm, 1)

            pool.wait_ge(v_lo, 8)
            for i in range(2):
                scale_probs(i, i)
            with pool.Fori(1, HEADS // 2) as i:
                for u in range(2):
                    scale_probs(2 * i + u, u)

            pool.wait_ge(added, 16)
            pool.wait_ge(w_used, BC)
            for u in range(2):
                nc.gpsimd.memset(up[:, u, :, 0:2], 0.0).then_inc(up_zero, 1)
                nc.gpsimd.memset(up[:, u, :, 258:260], 0.0).then_inc(up_zero, 1)

            for g in range(GROUPS):
                hs = slice(GH * g, GH * g + GH)
                if g == 0:
                    pool.wait_ge(w_used, SO)
                    pool.wait_ge(w6_done, 3)
                    pool.wait_ge(conv_ev, 20)
                for s, (tt, row) in enumerate(((0, 0), (1, 2), (0, 1), (1, 3), (2, 4), (3, 5))):
                    m = 6 * g + s
                    if m >= 2:
                        pool.wait_ge(xs_lo, m - 1)
                    nc.gpsimd.tensor_tensor(
                        T[:, s % 2, :].rearrange("p (h d) -> p h d", d=64),
                        xtok[:, tt, GW * g:GW * g + GW].rearrange("p (h d) -> p h d", d=64),
                        w6[:, row, hs].unsqueeze(2).to_broadcast([128, GH, 64]), MUL).then_inc(xs_f, 1)
                if g == 0:
                    pool.wait_ge(dta_hi, 2)
                for c in range(2):
                    for d_, name in ((0, "le"), (1, "ge")):
                        m = 4 * g + 2 * c + d_
                        if m >= 1:
                            pool.wait_ge(dec_mm, m)
                        for dst, src in ((mh, dtAh), (ml, dtAl)):
                            last = nc.gpsimd.tensor_tensor(
                                dst[:, :, :], tabv(name).unsqueeze(1).to_broadcast([128, GH, 128]),
                                src[:, c, 32 * d_ + GH * g:32 * d_ + GH * g + GH].unsqueeze(2).to_broadcast([128, GH, 128]), MUL)
                        last.then_inc(mk, 1)
                    if 2 * g + c >= 1:
                        pool.wait_ge(wf, 3 * (2 * g + c))
                    nc.gpsimd.tensor_tensor(
                        T[:, 4:6, :].rearrange("p a (h q) -> p (a h) q", q=128),
                        tabv("ge").unsqueeze(1).to_broadcast([128, GH, 128]),
                        dt[:, 2 + c, 32 + GH * g:32 + GH * g + GH].unsqueeze(2).to_broadcast([128, GH, 128]), MUL).then_inc(gb, 1)
                    if 2 * g + c >= 1:
                        pool.wait_ge(y_done, 2 * g + c)
                    nc.gpsimd.tensor_tensor(
                        T[:, 7, :].rearrange("p (h d) -> p h d", d=64),
                        xtok[:, 2 + c, GW * g:GW * g + GW].rearrange("p (h d) -> p h d", d=64),
                        rows[:, 128 + GH * g:128 + GH * g + GH].unsqueeze(2).to_broadcast([128, GH, 64]), MUL).then_inc(dx, 1)

        @block.scalar
        def _(act):
            A = nc.scalar.activation

            def hi(n, s):
                if isinstance(n, int) and n >= NBLK:
                    return
                act.wait_ge(raw_loaded[s % RING], 4 * (n - s % RING) + 16)
                if late(n, RING):
                    act.wait_ge(w_used, n - RING + 1)
                c = COLS[s]
                A(wh[s % RING][:, 0:c], raw[s % RING][:, 0:c], ACT.Copy).then_inc(w_hi, 1)

            def square(w, k, src):
                m = NB[w] + k
                if m >= 2:
                    act.wait_ge(sq_used, m - 1)
                A(T[:, m % 2, 0:src.shape[-1]], src, ACT.Square).then_inc(sq_ready, 1)

            def squares(w, m, q0, c0):
                act.wait_ge(added, q0 + m + 1)
                square(w, m, X[:, m, c0:TOK])

            def rms(w, n, dim):
                act.wait_ge(sq_used, NB[w + 1])
                if w >= 1:
                    act.wait_ge(inv, w)
                A(T[:, 4, 0:n], bank[NORM_BANK[w]][:, 0:n], ACT.Sqrt, bias=eps[:, 0:1], scale=1.0 / dim).then_inc(root, 1)

            def his(w, groups, hdst, shift):
                t0 = groups[0][1]
                for k in range(NORM_K[w]):
                    act.wait_ge(nv, NB[w] + k + 1)
                    for g, (m, c0, c1) in enumerate(groups):
                        v = T[:, 2 + k % 2, c0 - t0:c1 - t0]
                        if shift is None:
                            ins = A(hdst(k, c0, c1), v, ACT.Copy)
                        else:
                            ins = A(hdst(k, c0, c1), v, ACT.Identity, bias=shift(k, m))
                    ins.then_inc(nhi, 1)

            act.wait_ge(par_in, 16)
            A(sc[:, :, :], par[:, 0:16].rearrange("p (s k) -> p s k", s=2), ACT.Silu).then_inc(silu_c, 1)
            act.wait_ge(silu_c, 1)
            A(smov[:, :, :, 0], sc[:, :, :].rearrange("p s k -> p k s"), ACT.Copy).then_inc(sc_hi, 1)
            for n in range(RING):
                hi(n, n)
            for t in range(8):
                hi(A0 + t + RING, A0 + t + RING)
            act.wait_ge(x_in, 16)
            for t in range(8, 16):
                hi(A0 + t + RING, A0 + t + RING)
                square(0, t - 8, X[:, t - 8, :])
            act.wait_ge(inputs_in, 32)
            act.wait_ge(ones_set, 2)
            both = [(1, 0, CTX), (0, CTX, TOK)]
            rms(0, TOK, D)
            his(0, both, lambda k, c0, c1: Hmh[:, k, c0:c1], lambda k, m: mod[0][:, k, m:m + 1])

            whole = [(0, 0, TOK)]
            for t in range(7):
                act.wait_ge(w_used, IN + t + 1)
                if t == 2:
                    A(kf[64:96, :], bank[0][64:96, :], ACT.Copy).then_inc(proj_out, 1)
                else:
                    c = t if t < 2 else t - 1
                    square(1 if t < 2 else 2, c if t < 2 else c - 2, bank[t % 2][:, :])
                    A(cq[:, c, :], bank[t % 2][:, :], ACT.Copy).then_inc(proj_out, 1)
                hi(IN + t + RING, IN + t + RING)
                if t == 2:
                    act.wait_ge(kr_done, 1)
                    A(kh[64:96, :], kf[64:96, :], ACT.Copy).then_inc(kr_hi, 1)
                if t == 3:
                    rms(1, TOK, 128 * KKV)
                    his(1, whole, lambda k, c0, c1: cnh[:, k, c0:c1], None)
            for g in range(8):
                if g == 2:
                    rms(2, TOK, 128 * KQ)
                if g < 7:
                    act.wait_ge(v_mm, g + 1)
                else:
                    act.wait_ge(w_used, VB + 2)
                A(vh[:, g // 2, 512 * (g % 2):512 * (g % 2) + 512], bank[2 + g % 4][:, :], ACT.Copy).then_inc(v_hi, 1)
            his(2, whole, lambda k, c0, c1: cnh[:, KKV + k, c0:c1], None)
            hi(VB + 4, VB + 4)
            hi(VB + 5, VB + 5)

            def project(i, n, s, u):
                act.wait_ge(w_used, n + 1)
                if late(i, 1):
                    act.wait_ge(q_lo, i)
                    act.wait_ge(s_mm, 3 * i)
                A(qf[0:QKD, :], bank[0][0:QKD, :], ACT.Copy).then_inc(q_cp, 1)
                act.wait_ge(w_used, n + 2)
                A(kh[0:64, :], bank[1][0:64, :], ACT.Copy).then_inc(k_hi, 1)
                act.wait_ge(q_rope, i + 1)
                A(qh[0:QKD, :], qf[0:QKD, :], ACT.Copy).then_inc(q_hi, 1)
                hi(n + 4, s + 4)
                hi(n + 5, s + 5)

            def exps(i, p):
                act.wait_ge(nmax, 3 * i + p + 1)
                if late(i, 1):
                    act.wait_ge(pt_mm, 3 * i - 2 + p)
                    act.wait_ge(rcp, 3 * i - 2 + p)
                scale = float(QKD) ** -0.5
                if p < 2:
                    A(P[:, p, :], bank[p][:, :], ACT.Exp, bias=nm[:, p:p + 1], scale=scale,
                      accum_out=ssum[:, p:p + 1]).then_inc(exp_done, 1)
                else:
                    for t in range(2):
                        A(P[:, 2, 256 * t:256 * t + 256], bank[4][:, 256 * t:256 * t + 256], ACT.Exp,
                          bias=nm[:, 2 + t:3 + t], scale=scale, accum_out=ssum[:, 2 + t:3 + t]).then_inc(exp_done, 1)

            def pt_split(i, p, u):
                act.wait_ge(pt_mm, 3 * i + p + 1)
                if late(i, 1):
                    act.wait_ge(o_mm, i)
                b = bank[5 + (3 * u + p) % 2]
                if p < 2:
                    dst, src = PTh[:, 0:4, 128 * p:128 * p + 128], b[:, :].rearrange("p (k q) -> p k q", q=128)
                else:
                    dst, src = PTh[:, 4:6, :], b[:, :].rearrange("p (k q) -> p k q", q=256)
                A(dst, src, ACT.Copy).then_inc(pt_hi, 1)

            def head(i, j, u):
                n, s = HL + 4 * i, HL + 4 * (i if isinstance(i, int) else u)
                more = not isinstance(i, int) or i < 15
                if more:
                    project(i + 1, n, s, 1 - u)
                for p in range(3):
                    pt_split(i, p, u)
                    if more:
                        exps(i + 1, p)
                act.wait_ge(o_mm, i + 1)
                A(Oh[64 * u:64 * u + 64, ds(j, 1), :].rearrange("p o t -> p (o t)"), bank[3][0:64, :], ACT.Copy).then_inc(o_hi, 1)
                if more:
                    n, s = n + 2, s + 2
                hi(n + 4, s + 4)
                hi(n + 5, s + 5)

            project(0, HP, HP, 0)
            for p in range(3):
                exps(0, p)
            head(0, 0, 0)
            head(1, 0, 1)
            with act.Fori(1, 7) as j:
                head(2 * j, j, 0)
                head(2 * j + 1, j, 1)
            head(14, 7, 0)
            head(15, 7, 1)
            for m in range(8):
                hi(WO + m + RING, WO + m + RING)
                squares(3, m, 0, 0)
            rms(3, TOK, D)
            his(3, both, lambda k, c0, c1: H0h[:, k, c0:c1], lambda k, m: mod[0][:, 24 + k, m:m + 1])

            def hidden(j, g, u, nt, U, n, s, splits):
                act.wait_ge(w_used, n + 1)
                if late(g, 2):
                    act.wait_ge(hid_f, g - 1)
                A(T[:, u, 0:nt], bank[2 + 2 * u][:, 0:nt], ACT.Silu).then_inc(silu_done, 1)
                hi(n + 4, s + 4)
                hi(n + 5, s + 5)
                act.wait_ge(hid_f, g + 1)
                A(U[:, ds(j, 1), :].rearrange("p o t -> p (o t)"), T[:, 2 + u, 0:nt], ACT.Copy).then_inc(hid_hi, 1)
                for r in range(6, splits):
                    hi(n + r, s + r)

            for j in range(2):
                hidden(j, j, j % 2, TOK, U0h, F0 + 4 * j, F0 + 4 * j, 8)
            with act.Fori(1, KH // 2) as i:
                for u in range(2):
                    hidden(2 * i + u, 2 * i + u, u, TOK, U0h, F0 + 8 * i + 4 * u, F0 + 4 * u, 8)
            for m in range(8):
                for n in range(g0(m), g0(m + 1)):
                    hi(n + RING, n + RING)
                squares(4, m, 8, 0)
            rms(4, TOK, D)

            act.wait_ge(mod_done, 6)
            his(4, both, lambda k, c0, c1: H1h[:, k, c0:c1], lambda k, m: mod[1][:, k, m:m + 1])
            act.wait_ge(up_zero, 4)

            def conv(t, n, s, u, kind):
                seg = slice(1, 2) if kind == "C" else slice(0, 2)
                act.wait_ge(w_used, n + 1)
                if late(t, 2):
                    act.wait_ge(conv_tap, 4 * t - 4)
                if kind == "C":
                    A(up[:, u, 1, 2:258], bank[u][:, 256:512], ACT.Copy).then_inc(conv_up, 1)
                else:
                    A(up[:, u, :, 2:258], bank[u][:, :].rearrange("p (s t) -> p s t", s=2), ACT.Copy).then_inc(conv_up, 1)
                act.wait_ge(conv_up, t + 1)
                acc = T[:, u, :].rearrange("p (s t) -> p s t", s=2)[:, seg, :]
                A(acc, up[:, u, seg, 0:256], ACT.Identity, bias=par[:, ds(PAR["conv_b"] + t, 1)],
                  scale=par[:, ds(PAR["conv_w"] + 5 * t, 1)]).then_inc(conv_init, 1)
                hi(n + 4, s + 4)
                act.wait_ge(conv_tap, 4 * t + 4)
                if kind == "x" and late(t, 10):
                    act.wait_ge(conv_tr, t - 5)
                if kind == "B" and t >= 2:
                    act.wait_ge(conv_tr, t - 1)
                    act.wait_ge(ct_lo, t - 1)
                if kind == "C":
                    act.wait_ge(ct_lo, t - 1)
                    act.wait_ge(conv_tr, min(4, t - 1))
                if kind == "x" and isinstance(t, int) and t < 10:
                    act.wait_ge(ct_lo, t - 1)
                y = T[:, 2 + u, :].rearrange("p (s t) -> p s t", s=2)[:, seg, :]
                A(y, acc, ACT.Silu).then_inc(conv_y, 1)
                if kind in "BC":
                    g, dst = t % 4, BTh if kind == "B" else CTh
                    act.wait_ge(conv_y, t + 1)
                    A(dst[:, g, :], T[:, 2 + u, 256:512], ACT.Copy).then_inc(ct_hi, 1)

            for t in range(8):
                conv(t, BC + t, BC + t, t % 2, "BC"[t // 4])
                if 1 <= t <= 4:
                    act.wait_ge(conv_tr, t)
                    A(Bth[:, :, t - 1, :], bank[3 - t % 2][:, :].rearrange("p (t n) -> p t n", n=128), ACT.Copy).then_inc(conv_hi, 1)
            act.wait_ge(w_used, DT + 1)
            A(dtT[:, :], bank[4][0:64, :], ACT.Copy).then_inc(dt_cp, 1)
            hi(DT + RING, DT + RING)
            W = dtw
            act.wait_ge(dt_dve, 2)
            A(W[:, 2, :], W[:, 1, :], ACT.Exp, scale=-1.0).then_inc(dt_act, 1)
            A(rows[:, 64:128], rows[:, 64:128], ACT.Exp).then_inc(dt_act, 1)
            act.wait_ge(dt_dve, 3)
            A(W[:, 4, :], W[:, 3, :], ACT.Ln).then_inc(dt_act, 1)
            act.wait_ge(masks_r, 2)

            for u in range(4):
                conv(8 + u, XS + u, XS + u, u % 2, "x")
            with act.Fori(1, 4) as i:
                for u in range(4):
                    conv(8 + 4 * i + u, XS + 4 * i + u, XS + u, u % 2, "x")
            with act.Fori(0, 4) as i:
                for u in range(4):
                    act.wait_ge(w_used, ZS + 4 * i + u + 1)
                    A(zs[:, ds(4 * i + u, 1), :].rearrange("p o t -> p (o t)"), bank[4 + u % 2][:, 0:LAT], ACT.Silu).then_inc(conv_y, 1)
                    hi(ZS + 4 * i + u + 4, ZS + u + 4)
            act.wait_ge(cum_mm, 1)
            A(et[:, :], bank[6][:, 0:384], ACT.Exp).then_inc(cum_exp, 1)

            act.wait_ge(cb_mm, 2)
            for c in range(2):
                A(cb[:, c, :, :], bank[2 + c][:, :].rearrange("p (g q) -> p g q", q=128), ACT.Copy).then_inc(cb_done, 1)
            for g in range(GROUPS):
                for s in range(6):
                    m = 6 * g + s
                    act.wait_ge(xs_f, m + 1)
                    if m >= 2:
                        act.wait_ge(st_mm, m - 1)
                    A(xsh[:, s % 2, :], T[:, s % 2, :], ACT.Copy).then_inc(xs_hi, 1)
                if g == 0:
                    act.wait_ge(conv_ev, 20)
                else:
                    act.wait_ge(dg_mm, 2 * g)
                A(xgh[:, :, :], xtok[:, 2:4, GW * g:GW * g + GW], ACT.Copy).then_inc(xg_hi, 1)
                for d_ in range(2):
                    m = 4 * g + 2 * d_
                    act.wait_ge(st_mm, 6 * g + 6)
                    if m >= 2:
                        act.wait_ge(off_mm, m)
                    A(hh[:, 0, :], bank[d_][:, :], ACT.Copy).then_inc(st_hi, 1)
                    act.wait_ge(st_sum, 2 * g + d_ + 1)
                    A(hh[:, 1, :], T[:, 6, :], ACT.Copy).then_inc(st_hi, 1)
                for c in range(2):
                    m = 2 * g + c
                    act.wait_ge(dec_mm, 2 * m + 2)
                    if m >= 1:
                        act.wait_ge(W_lo, m)
                    for b in range(2):
                        A(E[:, 4 * b:4 * b + 4, :], bank[6 + b][:, :].rearrange("p (h q) -> p h q", q=128), ACT.Exp).then_inc(dec_exp, 1)
                    act.wait_ge(wf, 3 * m + 3)
                    if m >= 1:
                        act.wait_ge(dg_mm, m)
                    A(Wh[:, :, :], E[:, :, :], ACT.Copy).then_inc(W_hi, 1)
            act.wait_ge(yt_done, 8)
            lat = [(0, 0, LAT)]
            for k in range(KI):
                square(5, k, zs[:, k, :])
            rms(5, LAT, INNER)
            his(5, lat, lambda k, c0, c1: Hyh[:, k, :], None)
            xlat = [(0, CTX, TOK)]
            for m in range(8):
                for r in range(2):
                    hi(SO + 2 * m + r + RING, SO + 2 * m + r + RING)
                squares(6, m, 16, CTX)
            rms(6, LAT, D)
            his(6, xlat, lambda k, c0, c1: H2h[:, k, :], lambda k, m: mod[1][:, 24 + k, m:m + 1])
            with act.Fori(0, KH // 2) as i:
                for u in range(2):
                    hidden(2 * i + u, KH + 2 * i + u, u, LAT, U1h, F1 + 4 * i + 2 * u, F1 + 2 * u, 0)
            for m in range(8):
                for r in range(3):
                    hi(G1 + 3 * m + r + RING, G1 + 3 * m + r + RING)
                squares(7, m, 24, CTX)
            rms(7, LAT, D)

        @block.vector
        def _(dve):
            V = nc.vector

            def lo(n, s):
                if isinstance(n, int) and n >= NBLK:
                    return
                dve.wait_ge(w_hi, n + 1)
                c = COLS[s]
                V.tensor_tensor(wl[s % RING][:, 0:c], raw[s % RING][:, 0:c], wh[s % RING][:, 0:c].bitcast(f32), SUB).then_inc(w_lo, 1)

            def norm(w, src, nk, groups, gn, hdst, ldst, shift):
                b = NB[w]
                t0, t1 = groups[0][1], groups[-1][2]
                dve.wait_ge(root, w + 1)
                V.reciprocal(T[:, 5, 0:t1 - t0], T[:, 4, 0:t1 - t0]).then_inc(inv, 1)
                dve.wait_ge(inv, w + 1)

                def value(k):
                    if k >= 2:
                        dve.wait_ge(nhi, b + k - 1)
                        dve.wait_ge(nlo, b + k - 1)
                    for m, c0, c1 in groups:
                        ins = V.scalar_tensor_tensor(T[:, 2 + k % 2, c0 - t0:c1 - t0], src(k, c0, c1), gn(k, m),
                                                     T[:, 5, c0 - t0:c1 - t0], MUL, MUL)
                    ins.then_inc(nv, 1)

                def low(k):
                    dve.wait_ge(nhi, b + k + 1)
                    for m, c0, c1 in groups:
                        v, h = T[:, 2 + k % 2, c0 - t0:c1 - t0], hdst(k, c0, c1).bitcast(f32)
                        if shift is None:
                            ins = V.tensor_tensor(ldst(k, c0, c1), v, h, SUB)
                        else:
                            ins = V.scalar_tensor_tensor(ldst(k, c0, c1), v, shift(k, m), h, ADD, SUB)
                    ins.then_inc(nlo, 1)

                value(0)
                for k in range(1, nk):
                    value(k)
                    low(k - 1)
                low(nk - 1)

            def ada_rows(q, used, acc):
                dve.wait_ge(w_used, used)
                if late(q, 1):
                    dve.wait_ge(row_tr, q)
                V.tensor_copy(mrow[:, :], acc[0:4, 0:256]).then_inc(row_cp, 1)

            def ada_out(q, layer, it):
                dve.wait_ge(row_tr, q + 1)
                V.tensor_reduce(mod[layer][:, ds(2 * it, 2), :].rearrange("p t s -> p (t s)"),
                                bank[7][:, 256:264].rearrange("p (m h) -> p m h", h=2), AX.X, ADD).then_inc(mod_ev, 1)

            def bias(layer, t0, t1, items):
                dve.wait_ge(mod_ev, items)
                ab = par[:, PAR["ada_b"] + 48 * layer + t0:PAR["ada_b"] + 48 * layer + t1]
                V.tensor_tensor(mod[layer][:, t0:t1, :], mod[layer][:, t0:t1, :],
                                ab.unsqueeze(2).to_broadcast([128, t1 - t0, 2]), ADD).then_inc(mod_done, 1)

            def gains(which, layer, chunk, name, k):
                dve.wait_ge(mod_done, k)
                g = par[:, PAR[name] + 8 * layer:PAR[name] + 8 * layer + 8]
                V.scalar_tensor_tensor(gain[which][:, :, :], mod[layer][:, 8 * chunk:8 * chunk + 8, :], 1.0,
                                       g.unsqueeze(2).to_broadcast([128, 8, 2]), ADD, MUL).then_inc(mod_done, 1)
                dve.wait_ge(mod_done, k + 1)

            dve.wait_ge(sc_hi, 1)
            V.tensor_tensor(smov[:, :, :, 1], sc[:, :, :].rearrange("p s k -> p k s"), smov[:, :, :, 0].bitcast(f32), SUB).then_inc(sc_lo, 1)
            for n in range(RING):
                lo(n, n)
            for q in range(8):
                for r in range(2):
                    lo(A0 + 2 * q + r + RING, A0 + 2 * q + r + RING)
                ada_rows(q, A0 + 2 * q + 2, bank[4 + q % 2])
                if q:
                    ada_out(q - 1, 0, q - 1)
            ada_out(7, 0, 7)
            bias(0, 0, 16, 8)
            gains(0, 0, 1, "norm_mix", 1)
            both = [(1, 0, CTX), (0, CTX, TOK)]
            dve.wait_ge(x_in, 16)
            norm(0, lambda k, c0, c1: X[:, k, c0:c1], 8, both, lambda k, m: gain[0][:, k, m:m + 1],
                 lambda k, c0, c1: Hmh[:, k, c0:c1], lambda k, c0, c1: Hml[:, k, c0:c1], lambda k, m: mod[0][:, k, m:m + 1])
            for t in range(7):
                lo(IN + t + RING, IN + t + RING)
                if t == 2:
                    dve.wait_ge(inputs_in, 32)
                    dve.wait_ge(proj_out, 3)
                    V.tensor_tensor(rtmp[64:96, :], bank[0][96:128, CTX:TOK], tab[96:128, TAB["sin"]:TAB["sin"] + LAT], MUL).then_inc(kr_part, 1)
                    V.tensor_tensor(kf[64:96, CTX:TOK], kf[64:96, CTX:TOK], tab[64:96, TAB["cos"]:TAB["cos"] + LAT], MUL).then_inc(kr_part, 1)
                    dve.wait_ge(kr_part, 2)
                    V.tensor_tensor(kf[64:96, CTX:TOK], kf[64:96, CTX:TOK], rtmp[64:96, :], ADD).then_inc(kr_done, 1)
                    dve.wait_ge(kr_hi, 1)
                    V.tensor_tensor(kl[64:96, :], kf[64:96, :], kh[64:96, :].bitcast(f32), SUB).then_inc(kr_lo, 1)
                if t == 3:
                    whole = [(0, 0, TOK)]
                    norm(1, lambda k, c0, c1: cq[:, k, c0:c1], KKV, whole, lambda k, m: par[:, PAR["kv_norm"] + k:PAR["kv_norm"] + k + 1],
                         lambda k, c0, c1: cnh[:, k, c0:c1], lambda k, c0, c1: cnl[:, k, c0:c1], None)
            for g in range(8):
                dve.wait_ge(v_hi, g + 1)
                c = (slice(None), g // 2, slice(512 * (g % 2), 512 * (g % 2) + 512))
                V.tensor_tensor(vl[c], bank[2 + g % 4][:, :], vh[c].bitcast(f32), SUB).then_inc(v_lo, 1)
            norm(2, lambda k, c0, c1: cq[:, KKV + k, c0:c1], KQ, whole, lambda k, m: par[:, PAR["q_norm"] + k:PAR["q_norm"] + k + 1],
                 lambda k, c0, c1: cnh[:, KKV + k, c0:c1], lambda k, c0, c1: cnl[:, KKV + k, c0:c1], None)
            lo(VB + 4, VB + 4)
            lo(VB + 5, VB + 5)

            def project(i, n, s, u):
                dve.wait_ge(q_cp, i + 1)
                V.tensor_tensor(rtmp[64:96, :], bank[0][96:128, CTX:TOK], tab[96:128, TAB["sin"]:TAB["sin"] + LAT], MUL).then_inc(rope_part, 1)
                V.tensor_tensor(qf[64:96, CTX:TOK], qf[64:96, CTX:TOK], tab[64:96, TAB["cos"]:TAB["cos"] + LAT], MUL).then_inc(rope_part, 1)
                dve.wait_ge(rope_part, 2 * i + 2)
                V.tensor_tensor(qf[64:96, CTX:TOK], qf[64:96, CTX:TOK], rtmp[64:96, :], ADD).then_inc(q_rope, 1)
                dve.wait_ge(k_hi, i + 1)
                V.tensor_tensor(kl[0:64, :], bank[1][0:64, :], kh[0:64, :].bitcast(f32), SUB).then_inc(k_lo, 1)
                dve.wait_ge(q_hi, i + 1)
                V.tensor_tensor(ql[0:QKD, :], qf[0:QKD, :], qh[0:QKD, :].bitcast(f32), SUB).then_inc(q_lo, 1)
                lo(n + 4, s + 4)
                lo(n + 5, s + 5)

            def maxes(i, p):
                dve.wait_ge(s_mm, 3 * i + p + 1)
                c = slice(p, p + 1) if p < 2 else slice(2, 4)
                if p < 2:
                    V.tensor_reduce(mx[:, c], bank[p][:, :], AX.X, ALU.max).then_inc(maxed, 1)
                else:
                    V.tensor_reduce(mx[:, c], bank[4][:, :].rearrange("p (a k) -> p a k", a=2), AX.X, ALU.max).then_inc(maxed, 1)
                dve.wait_ge(maxed, 3 * i + p + 1)
                V.tensor_scalar(nm[:, c], mx[:, c], -(float(QKD) ** -0.5), None, MUL).then_inc(nmax, 1)

            def inverse(i, p):
                dve.wait_ge(exp_done, 4 * i + (1, 2, 4)[p])
                if late(i, 1):
                    dve.wait_ge(p_norm, 3 * i - 2 + p)
                c = slice(p, p + 1) if p < 2 else slice(2, 4)
                V.reciprocal(rs_[:, c], ssum[:, c]).then_inc(rcp, 1)

            def pt_split(i, p, u):
                dve.wait_ge(pt_hi, 3 * i + p + 1)
                b = bank[5 + (3 * u + p) % 2]
                if p < 2:
                    k, q, src = slice(0, 4), slice(128 * p, 128 * p + 128), b[:, :].rearrange("p (k q) -> p k q", q=128)
                else:
                    k, q, src = slice(4, 6), slice(0, 256), b[:, :].rearrange("p (k q) -> p k q", q=256)
                V.tensor_tensor(PTl[:, k, q], src, PTh[:, k, q].bitcast(f32), SUB).then_inc(pt_lo, 1)

            def head(i, j, u):
                n, s = HL + 4 * i, HL + 4 * (i if isinstance(i, int) else u)
                more = not isinstance(i, int) or i < 15
                if late(i, 1):
                    ada_rows(7 + i, n, bank[7])
                if more:
                    project(i + 1, n, s, 1 - u)
                for p in range(3):
                    pt_split(i, p, u)
                    if p == 0 and late(i, 1):
                        ada_out(7 + i, 0, 7 + i)
                    if more:
                        maxes(i + 1, p)
                        if p:
                            inverse(i + 1, p - 1)
                if more:
                    inverse(i + 1, 2)
                dve.wait_ge(o_hi, i + 1)
                o = (slice(64 * u, 64 * u + 64), ds(j, 1), slice(None))
                V.tensor_tensor(Ol[o].rearrange("p o t -> p (o t)"), bank[3][0:64, :],
                                Oh[o].rearrange("p o t -> p (o t)").bitcast(f32), SUB).then_inc(o_lo, 1)
                if more:
                    n, s = n + 2, s + 2
                lo(n + 4, s + 4)
                lo(n + 5, s + 5)

            project(0, HP, HP, 0)
            for p in range(3):
                maxes(0, p)
                inverse(0, p)
            head(0, 0, 0)
            head(1, 0, 1)
            with dve.Fori(1, 7) as j:
                head(2 * j, j, 0)
                head(2 * j + 1, j, 1)
            head(14, 7, 0)
            head(15, 7, 1)
            ada_rows(23, WO, bank[7])
            ada_out(23, 0, 23)
            bias(0, 16, 48, 24)
            gains(1, 0, 4, "norm_ffn", 3)

            def add(used, m, u, layer, chunk, groups):
                dve.wait_ge(w_used, used)
                for src, c0, c1 in groups:
                    x = X[:, ds(m, 1), c0:c1].rearrange("p o t -> p (o t)")
                    b0 = c0 - groups[0][1]
                    ins = V.scalar_tensor_tensor(x, bank[u][:, b0:b0 + c1 - c0],
                                                 mod[layer][:, ds(8 * chunk + m, 1), src], x, MUL, ADD)
                ins.then_inc(added, 1)

            for m in range(8):
                lo(WO + m + RING, WO + m + RING)
                add(WO + m + 1, m, m % 2, 0, 2, both)
            dve.wait_ge(added, 8)
            norm(3, lambda k, c0, c1: X[:, k, c0:c1], 8, both, lambda k, m: gain[1][:, k, m:m + 1],
                 lambda k, c0, c1: H0h[:, k, c0:c1], lambda k, c0, c1: H0l[:, k, c0:c1], lambda k, m: mod[0][:, 24 + k, m:m + 1])

            def hidden(j, g, u, nt, Uh, Ul, n, s, splits):
                if splits and late(j, 1):
                    ada_rows(23 + j, n, bank[7])
                lo(n + 4, s + 4)
                if splits and late(j, 1):
                    ada_out(23 + j, 1, j - 1)
                dve.wait_ge(w_used, n + 2)
                dve.wait_ge(silu_done, g + 1)
                if late(g, 2):
                    dve.wait_ge(hid_lo, g - 1)
                V.tensor_tensor(T[:, 2 + u, 0:nt], bank[3 + 2 * u][:, 0:nt], T[:, u, 0:nt], MUL).then_inc(hid_f, 1)
                lo(n + 5, s + 5)
                dve.wait_ge(hid_hi, g + 1)
                V.tensor_tensor(Ul[:, ds(j, 1), :].rearrange("p o t -> p (o t)"), T[:, 2 + u, 0:nt],
                                Uh[:, ds(j, 1), :].rearrange("p o t -> p (o t)").bitcast(f32), SUB).then_inc(hid_lo, 1)
                for r in range(6, splits):
                    lo(n + r, s + r)

            for j in range(2):
                hidden(j, j, j % 2, TOK, U0h, U0l, F0 + 4 * j, F0 + 4 * j, 8)
            with dve.Fori(1, KH // 2) as i:
                for u in range(2):
                    hidden(2 * i + u, 2 * i + u, u, TOK, U0h, U0l, F0 + 8 * i + 4 * u, F0 + 4 * u, 8)
            for m in range(8):
                q = 45 + m
                if q < 48:
                    ada_rows(q, g0(m), bank[7])
                for n in range(g0(m), g0(m + 1)):
                    lo(n + RING, n + RING)
                    if n == g0(m) + 1 and q < 48:
                        ada_out(q, 1, q - 24)
                    if n == g0(m) + 2:
                        add(g0(m) + 3, m, m % 2, 0, 5, both)
                if q == 47:
                    bias(1, 0, 48, 48)
                    gains(2, 1, 1, "norm_mix", 5)
                    gains(3, 1, 4, "norm_ffn", 6)
            dve.wait_ge(added, 16)

            norm(4, lambda k, c0, c1: X[:, k, c0:c1], 8, both, lambda k, m: gain[2][:, k, m:m + 1],
                 lambda k, c0, c1: H1h[:, k, c0:c1], lambda k, c0, c1: H1l[:, k, c0:c1], lambda k, m: mod[1][:, k, m:m + 1])

            def conv(t, n, s, u, kind):
                seg = slice(1, 2) if kind == "C" else slice(0, 2)
                acc = T[:, u, :].rearrange("p (s t) -> p s t", s=2)[:, seg, :]
                dve.wait_ge(conv_init, t + 1)
                for r in range(1, 5):
                    if r > 1:
                        dve.wait_ge(conv_tap, 4 * t + r - 1)
                    V.scalar_tensor_tensor(acc, up[:, u, seg, r:r + 256], par[:, ds(PAR["conv_w"] + 5 * t + r, 1)],
                                           acc, MUL, ADD).then_inc(conv_tap, 1)
                lo(n + 4, s + 4)
                if kind in "BC":
                    g, h, l = t % 4, (BTh if kind == "B" else CTh), (BTl if kind == "B" else CTl)
                    dve.wait_ge(ct_hi, t + 1)
                    V.tensor_tensor(l[:, g, :], T[:, 2 + u, 256:512], h[:, g, :].bitcast(f32), SUB).then_inc(ct_lo, 1)

            def to_tokens(t, u):
                dve.wait_ge(conv_tr, t - 3)
                V.tensor_copy(xtok[:, :, ds(128 * (t - 8), 128)], bank[2 + u][:, :].rearrange("p (t n) -> p t n", n=128)).then_inc(conv_ev, 1)

            for t in range(8):
                conv(t, BC + t, BC + t, t % 2, "BC"[t // 4])
                if 1 <= t <= 4:
                    dve.wait_ge(conv_hi, t)
                    V.tensor_tensor(Btl[:, :, t - 1, :], bank[3 - t % 2][:, :].rearrange("p (t n) -> p t n", n=128),
                                    Bth[:, :, t - 1, :].bitcast(f32), SUB).then_inc(conv_ev, 1)
            lo(DT + RING, DT + RING)
            W = dtw
            dve.wait_ge(dt_tr, 1)
            V.tensor_tensor(W[:, 0, :].rearrange("p (t h) -> p t h", t=4), bank[5][:, 0:256].rearrange("p (t h) -> p t h", t=4),
                            rows[:, 0:64].unsqueeze(1).to_broadcast([128, 4, 64]), ADD).then_inc(dt_dve, 1)
            dve.wait_ge(dt_dve, 1)
            V.scalar_tensor_tensor(W[:, 1, :], W[:, 0, :], -1.0, W[:, 0, :], MUL, ALU.max).then_inc(dt_dve, 1)
            dve.wait_ge(dt_act, 1)
            V.tensor_scalar(W[:, 3, :], W[:, 2, :], 1.0, None, ADD).then_inc(dt_dve, 1)
            dve.wait_ge(dt_dve, 3)
            V.tensor_scalar(W[:, 5, :], W[:, 3, :], -1.0, None, ADD).then_inc(dt_dve, 1)
            dve.wait_ge(dt_dve, 4)
            V.tensor_scalar(W[:, 1, :], W[:, 5, :], 0.0, None, ALU.is_equal).then_inc(dt_dve, 1)
            dve.wait_ge(dt_dve, 5)
            V.tensor_tensor(W[:, 5, :], W[:, 5, :], W[:, 1, :], ADD).then_inc(dt_dve, 1)
            dve.wait_ge(dt_act, 3)
            V.tensor_tensor(W[:, 4, :], W[:, 4, :], W[:, 1, :], ADD).then_inc(dt_dve, 1)
            dve.wait_ge(dt_dve, 7)
            V.reciprocal(W[:, 5, :], W[:, 5, :]).then_inc(dt_dve, 1)
            dve.wait_ge(dt_dve, 8)
            V.tensor_tensor(W[:, 4, :], W[:, 4, :], W[:, 5, :], MUL).then_inc(dt_dve, 1)
            dve.wait_ge(dt_dve, 9)
            V.tensor_tensor(W[:, 4, :], W[:, 4, :], W[:, 2, :], MUL).then_inc(dt_dve, 1)
            dve.wait_ge(dt_dve, 10)
            V.scalar_tensor_tensor(dt[:, :, :].rearrange("p t h -> p (t h)"), W[:, 0, :], 0.0, W[:, 4, :], ALU.max, ADD).then_inc(dt_dve, 1)
            dve.wait_ge(dt_dve, 11)
            V.scalar_tensor_tensor(dtA[:, :, :], dt[:, :, :], -1.0, rows[:, 64:128].unsqueeze(1).to_broadcast([128, 4, 64]), MUL, MUL).then_inc(dt_dve, 1)
            dve.wait_ge(dt_dve, 12)
            V.tensor_copy(maskr[:, 0, :], tabv("gt")).then_inc(masks_r, 1)
            V.tensor_copy(maskr[:, 1, :], tabv("lt")).then_inc(masks_r, 1)
            V.tensor_copy(dtAh[:, :, :].bitcast(f32r), dtA[:, 2:4, :]).then_inc(dta_hi, 1)
            dve.wait_ge(dta_hi, 1)
            V.tensor_tensor(dtAl[:, :, :].bitcast(f32r), dtA[:, 2:4, :], dtAh[:, :, :], SUB).then_inc(dta_hi, 1)

            conv(8, XS, XS, 0, "x")
            for u in range(1, 4):
                conv(8 + u, XS + u, XS + u, u % 2, "x")
                to_tokens(7 + u, 1 - u % 2)
            with dve.Fori(1, 4) as i:
                for u in range(4):
                    conv(8 + 4 * i + u, XS + 4 * i + u, XS + u, u % 2, "x")
                    to_tokens(7 + 4 * i + u, 1 - u % 2)
            to_tokens(23, 1)
            with dve.Fori(0, 4) as i:
                for u in range(4):
                    lo(ZS + 4 * i + u + 4, ZS + u + 4)
            dve.wait_ge(cum_exp, 1)
            V.tensor_tensor(w6[:, 0:4, :].rearrange("p s h -> p (s h)"), et[:, 0:128], dt[:, 0:2, :].rearrange("p t h -> p (t h)"), MUL).then_inc(w6_done, 1)
            V.tensor_tensor(w6[:, 4, :], et[:, 128:160], dt[:, 2, 0:32], MUL).then_inc(w6_done, 1)
            V.tensor_tensor(w6[:, 5, :], et[:, 160:192], dt[:, 3, 32:64], MUL).then_inc(w6_done, 1)

            steps = {"y": 0, "g": 0}

            def heads64(ap):
                return ap.rearrange("p (h d) -> p h d", d=64)

            for g in range(GROUPS):
                for s in range(6):
                    m = 6 * g + s
                    dve.wait_ge(xs_hi, m + 1)
                    V.tensor_tensor(xsl[:, s % 2, :], T[:, s % 2, :], xsh[:, s % 2, :].bitcast(f32), SUB).then_inc(xs_lo, 1)
                dve.wait_ge(xg_hi, g + 1)
                V.tensor_tensor(xgl[:, :, :], xtok[:, 2:4, GW * g:GW * g + GW], xgh[:, :, :].bitcast(f32), SUB).then_inc(xg_lo, 1)
                for d_ in range(2):
                    q = 2 * g + d_
                    dve.wait_ge(st_hi, 2 * q + 1)
                    V.tensor_tensor(hl[:, 0, :], bank[d_][:, :], hh[:, 0, :].bitcast(f32), SUB).then_inc(st_lo, 1)
                    dtot = et[:, 320 + 32 * d_ + GH * g:320 + 32 * d_ + GH * g + GH]
                    if q >= 1:
                        dve.wait_ge(st_lo, 2 * q)
                    V.tensor_tensor(heads64(T[:, 6, :]), heads64(bank[d_][:, :]), dtot.unsqueeze(2).to_broadcast([128, GH, 64]), MUL).then_inc(st_dec, 1)
                    dve.wait_ge(st_dec, q + 1)
                    V.tensor_tensor(T[:, 6, :], T[:, 6, :], bank[2 + d_][:, :], ADD).then_inc(st_sum, 1)
                    dve.wait_ge(st_hi, 2 * q + 2)
                    V.tensor_tensor(hl[:, 1, :], T[:, 6, :], hh[:, 1, :].bitcast(f32), SUB).then_inc(st_lo, 1)
                    for z in range(2):
                        c = z if d_ == 0 else 1 - z
                        dve.wait_ge(off_mm, 2 * q + z + 1)
                        ec = et[:, 192 + 64 * c + 32 * d_ + GH * g:192 + 64 * c + 32 * d_ + GH * g + GH].unsqueeze(2).to_broadcast([128, GH, 64])
                        src = bank[4 + c] if d_ == 0 else bank[2 * c]
                        if d_ == 0:
                            if g:
                                dve.wait_ge(yt_mm, 2 * g)
                            V.tensor_tensor(heads64(Y[:, c, :]), heads64(src[:, :]), ec, MUL).then_inc(y_step, 1)
                            steps["y"] += 1
                        else:
                            dve.wait_ge(st_lo, 2 * q + 2)
                            V.tensor_tensor(heads64(T[:, 6, :]), heads64(src[:, :]), ec, MUL).then_inc(y_step, 1)
                            steps["y"] += 1
                            dve.wait_ge(y_step, steps["y"])
                            V.tensor_tensor(Y[:, c, :], Y[:, c, :], T[:, 6, :], ADD).then_inc(y_step, 1)
                            steps["y"] += 1
                            dve.wait_ge(y_step, steps["y"])
                for c in range(2):
                    m = 2 * g + c
                    G = T[:, 2:4, :].rearrange("p a (h q) -> p (a h) q", q=128)
                    Gb = T[:, 4:6, :].rearrange("p a (h q) -> p (a h) q", q=128)
                    V.tensor_tensor(G, tabv("le").unsqueeze(1).to_broadcast([128, GH, 128]),
                                    dt[:, 2 + c, GH * g:GH * g + GH].unsqueeze(2).to_broadcast([128, GH, 128]), MUL).then_inc(g_step, 1)
                    dve.wait_ge(gb, m + 1)
                    dve.wait_ge(g_step, 2 * m + 1)
                    V.tensor_tensor(G, G, Gb, ADD).then_inc(wf, 1)
                    dve.wait_ge(wf, 3 * m + 1)
                    V.tensor_tensor(G, G, cb[:, c, g, :].unsqueeze(1).to_broadcast([128, GH, 128]), MUL).then_inc(wf, 1)
                    dve.wait_ge(wf, 3 * m + 2)
                    dve.wait_ge(dec_exp, 2 * m + 2)
                    V.tensor_tensor(E[:, :, :], E[:, :, :], G, MUL).then_inc(wf, 1)
                    dve.wait_ge(W_hi, m + 1)
                    V.tensor_tensor(Wl[:, :, :], E[:, :, :], Wh[:, :, :].bitcast(f32), SUB).then_inc(W_lo, 1)
                    dve.wait_ge(dx, m + 1)
                    V.tensor_tensor(Y[:, c, :], Y[:, c, :], T[:, 7, :], ADD).then_inc(g_step, 1)
                    dve.wait_ge(g_step, 2 * m + 2)
                    dve.wait_ge(dg_mm, m + 1)
                    V.tensor_tensor(Y[:, c, :], Y[:, c, :], bank[4 + c][:, :], ADD).then_inc(y_done, 1)
                    dve.wait_ge(yt_mm, m + 1)
                    z = zs[:, 4 * g:4 * g + 4, 128 * c:128 * c + 128]
                    V.tensor_tensor(z, bank[1][:, :].rearrange("p (f q) -> p f q", q=128), z, MUL).then_inc(yt_done, 1)
            lat = [(0, 0, LAT)]
            dve.wait_ge(yt_done, 8)
            norm(5, lambda k, c0, c1: zs[:, k, :], KI, lat, lambda k, m: par[:, PAR["ssd_norm"] + k:PAR["ssd_norm"] + k + 1],
                 lambda k, c0, c1: Hyh[:, k, :], lambda k, c0, c1: Hyl[:, k, :], None)
            xlat = [(0, CTX, TOK)]
            with dve.Fori(0, 4) as i:
                for u in range(2):
                    for r in range(2):
                        lo(SO + 4 * i + 2 * u + r + 4, SO + 2 * u + r + 4)
                    add(SO + 4 * i + 2 * u + 2, 2 * i + u, u, 1, 2, xlat)
            dve.wait_ge(added, 24)
            norm(6, lambda k, c0, c1: X[:, k, c0:c1], 8, xlat, lambda k, m: gain[3][:, k, m:m + 1],
                 lambda k, c0, c1: H2h[:, k, :], lambda k, c0, c1: H2l[:, k, :], lambda k, m: mod[1][:, 24 + k, m:m + 1])
            with dve.Fori(0, KH // 2) as i:
                for u in range(2):
                    hidden(2 * i + u, KH + 2 * i + u, u, LAT, U1h, U1l, F1 + 4 * i + 2 * u, F1 + 2 * u, 0)
            for m in range(8):
                for r in range(3):
                    lo(G1 + 3 * m + r + RING, G1 + 3 * m + r + RING)
                add(G1 + 3 * m + 3, m, m % 2, 1, 5, xlat)
            dve.wait_ge(added, 32)
            dve.wait_ge(root, 8)
            V.reciprocal(T[:, 5, 0:LAT], T[:, 4, 0:LAT]).then_inc(inv, 1)
            dve.wait_ge(inv, 8)
            for k in range(KD):
                V.scalar_tensor_tensor(yout[:, k, :], X[:, k, CTX:TOK], par[:, PAR["final"] + k:PAR["final"] + k + 1],
                                       T[:, 5, 0:LAT], MUL, MUL).then_inc(out_done, 1)

        @block.tensor
        def _(pe):
            mm = nc.tensor.matmul

            def three(o, lh, ll, rh, rl, first, final):
                mm(o, lh, rl, start=first, stop=False)
                mm(o, lh, rh, start=False, stop=False)
                return mm(o, ll, rh, start=False, stop=final)

            def tile(n, s, o, h, l, k0, nk, first, final, kwait=None, mid=None):
                pe.wait_ge(w_lo, n + 1)
                for k in range(nk):
                    if kwait is not None:
                        pe.wait_ge(nlo, kwait + k0 + k + 1)
                    w = slice(128 * k, 128 * k + 128)
                    last = three(o, wh[s % RING][:, w], wl[s % RING][:, w], h(k0 + k), l(k0 + k),
                                 first and k == 0, final and k == nk - 1)
                    if k == 3 and mid is not None:
                        mid()
                return last

            def ada(n, s, q, acc):
                if late(q, 8):
                    pe.wait_ge(mod_ev, q)
                elif q >= 2:
                    pe.wait_ge(row_cp, q - 1)
                for r in range(2):
                    pe.wait_ge(w_lo, n + r + 1)
                    for k in range(4):
                        lhs = smov[:, 4 * r + k, :, :].rearrange("p s h -> p (s h)")
                        w, sl = slice(256 * k, 256 * k + 256), (s + r) % RING
                        mm(acc[0:4, 0:256], lhs, wh[sl][:, w], start=r + k == 0, stop=False)
                        last = mm(acc[0:4, 0:256], lhs, wl[sl][:, w], start=False, stop=r == 1 and k == 3)
                    last.then_inc(w_used, 1)

            def turn_ready(q):
                pe.wait_ge(row_cp, q + 1)
                if late(q, 1):
                    pe.wait_ge(mod_ev, q)

            def turn(q):
                for t in range(2):
                    last = nc.tensor.transpose(bank[7][:, 256 + 4 * t:260 + 4 * t], mrow[:, 128 * t:128 * t + 128], tab[0:4, 0:4])
                last.then_inc(row_tr, 1)

            def norm(w, k, n):
                if k == 0 and w >= 1:
                    pe.wait_ge(root, w)
                m = NB[w] + k
                pe.wait_ge(sq_ready, m + 1)
                mm(bank[NORM_BANK[w]][:, 0:n], ones[:, :], T[:, m % 2, 0:n], start=k == 0, stop=k == NORM_K[w] - 1).then_inc(sq_used, 1)

            pe.wait_ge(sc_lo, 1)
            for q in range(8):
                ada(A0 + 2 * q, A0 + 2 * q, q, bank[4 + q % 2])
                if q == 1:
                    pe.wait_ge(inputs_in, 32)
                    pe.wait_ge(ones_set, 2)
                if q >= 1:
                    turn_ready(q - 1)
                    turn(q - 1)
                if q >= 4:
                    norm(0, 2 * q - 8, TOK)
                    norm(0, 2 * q - 7, TOK)
            turn_ready(7)
            turn(7)
            for t in range(7):
                if t >= 2:
                    pe.wait_ge(proj_out, t - 1)
                if t == 2:
                    pe.wait_ge(mod_ev, 8)
                if t == 4:
                    pe.wait_ge(kr_part, 1)
                tile(IN + t, IN + t, bank[t % 2][:, :], lambda k: Hmh[:, k, :], lambda k: Hml[:, k, :], 0, 8,
                     True, True, NB[0] if t == 0 else None).then_inc(w_used, 1)
                if t in (1, 2):
                    norm(1, t - 1, TOK)
                if t >= 4:
                    norm(2, t - 4, TOK)
            pe.wait_ge(w_lo, VB + 2)
            pe.wait_ge(nlo, NB[2])
            for g in range(8):
                if g >= 4:
                    pe.wait_ge(v_lo, g - 3)
                tk, c = slice(128 * (g // 2), 128 * (g // 2) + 128), slice(512 * (g % 2), 512 * (g % 2) + 512)
                for k in range(KKV):
                    sl = (VB + k) % RING
                    last = three(bank[2 + g % 4][:, :], cnh[:, k, tk], cnl[:, k, tk], wh[sl][:, c], wl[sl][:, c], k == 0, k == KKV - 1)
                    if g == 7:
                        last.then_inc(w_used, 1)
                if g < 7:
                    last.then_inc(v_mm, 1)
                if g == 0:
                    norm(2, 3, TOK)

            def project(i, n, s):
                if late(i, 1):
                    pe.wait_ge(exp_done, 4 * i - 3)
                else:
                    pe.wait_ge(nlo, NB[3])
                tile(n, s, bank[0][:, :], lambda k: cnh[:, KKV + k, :], lambda k: cnl[:, KKV + k, :], 0, KQ, True, True).then_inc(w_used, 1)
                pe.wait_ge(w_lo, n + 2)
                if late(i, 1):
                    pe.wait_ge(exp_done, 4 * i - 2)
                s1 = (s + 1) % RING
                for k in range(KKV):
                    w = slice(64 * k, 64 * k + 64)
                    last = three(bank[1][0:64, :], wh[s1][:, w], wl[s1][:, w], cnh[:, k, :], cnl[:, k, :], k == 0, k == KKV - 1)
                last.then_inc(w_used, 1)

            def scores(i, p):
                if p == 0:
                    pe.wait_ge(q_lo, i + 1)
                    pe.wait_ge(k_lo, i + 1)
                if p < 2:
                    q = slice(CTX + 128 * p, CTX + 128 * p + 128)
                    last = three(bank[p][:, :], qh[0:QKD, q], ql[0:QKD, q], kh[0:QKD, :], kl[0:QKD, :], True, True)
                else:
                    if late(i, 1):
                        pe.wait_ge(exp_done, 4 * i)
                    for t in range(2):
                        q = slice(128 * t, 128 * t + 128)
                        last = three(bank[4][:, 256 * t:256 * t + 256], qh[0:QKD, q], ql[0:QKD, q],
                                     kh[0:QKD, 0:CTX], kl[0:QKD, 0:CTX], True, True)
                last.then_inc(s_mm, 1)

            def transpose_probs(i, p, u):
                pe.wait_ge(p_norm, 3 * i + p + 1)
                if late(i, 1) or p == 2:
                    pe.wait_ge(pt_lo, 3 * i + p - 1)
                b = bank[5 + (3 * u + p) % 2]
                if p < 2:
                    for k in range(4):
                        last = nc.tensor.transpose(b[:, 128 * k:128 * k + 128], P[:, p, 128 * k:128 * k + 128], tabv("ident"))
                else:
                    for k in range(2):
                        for t in range(2):
                            last = nc.tensor.transpose(b[:, 256 * k + 128 * t:256 * k + 128 * t + 128],
                                                       P[:, 2, 256 * t + 128 * k:256 * t + 128 * k + 128], tabv("ident"))
                last.then_inc(pt_mm, 1)

            def values(i, u):
                pe.wait_ge(pt_lo, 3 * i + 3)
                pe.wait_ge(v_cp, i + 1)
                if late(i, 1):
                    pe.wait_ge(o_lo, i)
                for k in range(4):
                    three(bank[3][0:64, CTX:TOK], vsh[:, u, k, :], vsl[:, u, k, :], PTh[:, k, :], PTl[:, k, :], k == 0, k == 3)
                for k in range(2):
                    last = three(bank[3][0:64, 0:CTX], vsh[:, u, k, :], vsl[:, u, k, :], PTh[:, 4 + k, :], PTl[:, 4 + k, :], k == 0, k == 1)
                last.then_inc(o_mm, 1)

            def head(i, u):
                n, s = HL + 4 * i, HL + 4 * (i if isinstance(i, int) else u)
                more = not isinstance(i, int) or i < 15
                if more:
                    project(i + 1, n, s)
                if late(i, 1):
                    turn_ready(7 + i)
                for p in range(3):
                    transpose_probs(i, p, u)
                    if p == 0 and late(i, 1):
                        turn(7 + i)
                    if more:
                        scores(i + 1, p)
                values(i, u)
                if more:
                    n, s = n + 2, s + 2
                ada(n, s, 8 + i, bank[7])

            project(0, HP, HP)
            pe.wait_ge(kr_lo, 1)
            for p in range(3):
                scores(0, p)
            head(0, 0)
            head(1, 1)
            with pe.Fori(1, 7) as j:
                head(2 * j, 0)
                head(2 * j + 1, 1)
            head(14, 0)
            head(15, 1)

            turn_ready(23)
            turn(23)
            pe.wait_ge(o_lo, HEADS)
            for m in range(8):
                if m >= 2:
                    pe.wait_ge(added, m - 1)
                tile(WO + m, WO + m, bank[m % 2][:, :], lambda k: Oh[:, k, :], lambda k: Ol[:, k, :], 0, 8, True, True).then_inc(w_used, 1)
                if m:
                    norm(3, m - 1, TOK)
            norm(3, 7, TOK)

            def ffn(j, g, u, nt, h, l, n, s, kwait):
                if late(g, 2):
                    pe.wait_ge(silu_done, g - 1)
                tile(n, s, bank[2 + 2 * u][:, 0:nt], h, l, 0, 8, True, True, kwait).then_inc(w_used, 1)
                if nt == TOK and late(j, 1):
                    turn_ready(23 + j)
                if late(g, 2):
                    pe.wait_ge(hid_f, g - 1)
                mid = (lambda: turn(23 + j)) if nt == TOK and late(j, 1) else None
                tile(n + 1, s + 1, bank[3 + 2 * u][:, 0:nt], h, l, 0, 8, True, True, None, mid).then_inc(w_used, 1)

            h0 = (lambda k: H0h[:, k, :]), (lambda k: H0l[:, k, :])
            for j in range(2):
                ffn(j, j, j % 2, TOK, *h0, F0 + 4 * j, F0 + 4 * j, NB[3] if j == 0 else None)
                ada(F0 + 4 * j + 2, F0 + 4 * j + 2, 24 + j, bank[7])
            with pe.Fori(1, KH // 2) as i:
                for u in range(2):
                    n, s = F0 + 8 * i + 4 * u, F0 + 4 * u
                    ffn(2 * i + u, 2 * i + u, u, TOK, *h0, n, s, None)
                    ada(n + 2, s + 2, 24 + 2 * i + u, bank[7])

            def w2(q0, m, n, nt, h, l, w):
                pe.wait_ge(added, q0 + m - 1)
                for r, (k0, nk) in enumerate(((0, 8), (8, 8), (16, KH - 16))):
                    tile(n + r, n + r, bank[m % 2][:, 0:nt], h, l, k0, nk, r == 0, r == 2).then_inc(w_used, 1)
                    if r == 0 and m:
                        norm(w, m - 1, nt)
                    if r == 1 and nt == TOK and m < 3:
                        turn_ready(45 + m)
                        turn(45 + m)

            pe.wait_ge(hid_lo, KH)
            for m in range(8):
                w2(8, m, g0(m), TOK, lambda k: U0h[:, k, :], lambda k: U0l[:, k, :], 4)
                if m < 2:
                    ada(g0(m) + 3, g0(m) + 3, 46 + m, bank[7])
            norm(4, 7, TOK)

            def conv_tile(t, n, s, u, kind, kwait):
                if late(t, 2):
                    pe.wait_ge(conv_up, t - 1)
                c = slice(CTX, TOK) if kind == "C" else slice(0, TOK)
                tile(n, s, bank[u][:, c], lambda k: H1h[:, k, c], lambda k: H1l[:, k, c], 0, 8, True, True, kwait).then_inc(w_used, 1)

            def to_tokens(t, u, r):
                pe.wait_ge(conv_y, t + 1)
                if late(r, 2):
                    pe.wait_ge(conv_ev, r - 1)
                for k in range(4):
                    last = nc.tensor.transpose(bank[2 + u][:, 128 * k:128 * k + 128], T[:, 2 + u, 128 * k:128 * k + 128], tabv("ident"))
                last.then_inc(conv_tr, 1)

            for t in range(8):
                conv_tile(t, BC + t, BC + t, t % 2, "BC"[t // 4], NB[4] if t == 0 else None)
                if 1 <= t <= 4:
                    to_tokens(t - 1, (t - 1) % 2, t - 1)
            pe.wait_ge(w_lo, DT + 1)
            for k in range(8):
                w, sl = slice(64 * k, 64 * k + 64), DT % RING
                last = three(bank[4][0:64, :], wh[sl][:, w], wl[sl][:, w], H1h[:, k, :], H1l[:, k, :], k == 0, k == 7)
            last.then_inc(w_used, 1)
            conv_tile(8, XS, XS, 0, "x", None)
            pe.wait_ge(dt_cp, 1)
            for t in range(4):
                last = nc.tensor.transpose(bank[5][:, 64 * t:64 * t + 64], dtT[:, 128 * t:128 * t + 128], tab[0:64, 0:64])
            last.then_inc(dt_tr, 1)
            for u in range(1, 4):
                conv_tile(8 + u, XS + u, XS + u, u % 2, "x", None)
                to_tokens(7 + u, 1 - u % 2, 3 + u)
            with pe.Fori(1, 4) as i:
                for u in range(4):
                    conv_tile(8 + 4 * i + u, XS + 4 * i + u, XS + u, u % 2, "x", None)
                    to_tokens(7 + 4 * i + u, 1 - u % 2, 3 + 4 * i + u)
            to_tokens(23, 1, 19)
            pe.wait_ge(dt_dve, 1)
            with pe.Fori(0, 4) as i:
                for u in range(4):
                    pe.wait_ge(conv_y, 23 + 4 * i + u)
                    tile(ZS + 4 * i + u, ZS + u, bank[4 + u % 2][:, 0:LAT], lambda k: H1h[:, k, CTX:TOK],
                         lambda k: H1l[:, k, CTX:TOK], 0, 8, True, True).then_inc(w_used, 1)
            pe.wait_ge(dt_dve, 12)
            F, B = slice(0, SH), slice(SH, 2 * SH)
            sums = (("gt", 0, F, 1), ("lt", 0, B, None), ("gt", 1, F, None), ("lt", 1, B, 0),
                    ("gt", 2, F, None), ("lt", 3, B, None), ("le", 2, F, None), ("ge", 2, B, None),
                    ("le", 3, F, None), ("ge", 3, B, None), (None, 2, F, None), (None, 3, B, None))
            for q, (name, tt, hs, whole) in enumerate(sums):
                o = bank[6][:, SH * q:SH * q + SH]
                last = mm(o, tabv(name) if name else ones[:, :], dtA[:, tt, hs], start=True, stop=whole is None)
                if whole is not None:
                    last = mm(o, ones[:, :], dtA[:, whole, hs], start=False, stop=True)
            last.then_inc(cum_mm, 1)
            pe.wait_ge(ct_lo, 8)
            pe.wait_ge(conv_ev, 20)
            for c in range(2):
                cs = slice(128 * c, 128 * c + 128)
                for g in range(GROUPS):
                    last = three(bank[2 + c][:, 128 * g:128 * g + 128], BTh[:, g, cs], BTl[:, g, cs], CTh[:, g, cs], CTl[:, g, cs], True, True)
                last.then_inc(cb_mm, 1)

            def decay(g, c):
                for d_ in range(2):
                    m = 4 * g + 2 * c + d_
                    pe.wait_ge(mk, m + 1)
                    if d_ == 0 and 2 * g + c >= 1:
                        pe.wait_ge(dec_exp, 2 * (2 * g + c))
                    if m == 0:
                        pe.wait_ge(cum_exp, 1)
                    for b in range(2):
                        for part in (mh, ml):
                            last = mm(bank[6 + b][:, :], maskr[:, d_, :], part[:, 4 * b:4 * b + 4, :].rearrange("p h q -> p (h q)"),
                                      start=d_ == 0 and part is mh, stop=d_ == 1 and part is ml)
                    last.then_inc(dec_mm, 1)

            pe.wait_ge(masks_r, 2)
            for g in range(GROUPS):
                if g:
                    pe.wait_ge(yt_done, 2 * g)
                else:
                    pe.wait_ge(cb_done, 2)
                for s, (tt, b) in enumerate(((0, 0), (1, 0), (0, 1), (1, 1), (2, 2), (3, 3))):
                    pe.wait_ge(xs_lo, 6 * g + s + 1)
                    three(bank[b][:, :], Bth[:, tt, g, :], Btl[:, tt, g, :], xsh[:, s % 2, :], xsl[:, s % 2, :],
                          s in (0, 2, 4, 5), s in (1, 3, 4, 5)).then_inc(st_mm, 1)
                decay(g, 0)
                for d_ in range(2):
                    for z in range(2):
                        c = z if d_ == 0 else 1 - z
                        pe.wait_ge(st_lo, 4 * g + 2 * d_ + z + 1)
                        cs = slice(128 * c, 128 * c + 128)
                        three(bank[4 + c if d_ == 0 else 2 * c][:, :], CTh[:, g, cs], CTl[:, g, cs], hh[:, z, :], hl[:, z, :],
                              True, True).then_inc(off_mm, 1)
                decay(g, 1)
                pe.wait_ge(xg_lo, g + 1)
                for c in range(2):
                    m = 2 * g + c
                    pe.wait_ge(W_lo, m + 1)
                    for h in range(GH):
                        xs = slice(64 * h, 64 * h + 64)
                        last = three(bank[4 + c][:, xs], Wh[:, h, :], Wl[:, h, :], xgh[:, c, xs], xgl[:, c, xs], True, True)
                    last.then_inc(dg_mm, 1)
                    pe.wait_ge(y_done, m + 1)
                    if m:
                        pe.wait_ge(yt_done, m)
                    for f in range(4):
                        last = nc.tensor.transpose(bank[1][:, 128 * f:128 * f + 128], Y[:, c, 128 * f:128 * f + 128], tabv("ident"))
                    last.then_inc(yt_mm, 1)
            for k in range(KI):
                norm(5, k, LAT)
            pe.wait_ge(nlo, NB[6])
            for m in range(8):
                pe.wait_ge(added, 15 + m)
                for r in range(2):
                    tile(SO + 2 * m + r, SO + 2 * m + r, bank[m % 2][:, 0:LAT], lambda k: Hyh[:, k, :], lambda k: Hyl[:, k, :],
                         8 * r, 8, r == 0, r == 1).then_inc(w_used, 1)
                if m:
                    norm(6, m - 1, LAT)
            norm(6, 7, LAT)
            pe.wait_ge(nlo, NB[7])
            with pe.Fori(0, KH // 2) as i:
                for u in range(2):
                    ffn(2 * i + u, KH + 2 * i + u, u, LAT, lambda k: H2h[:, k, :], lambda k: H2l[:, k, :], F1 + 4 * i + 2 * u, F1 + 2 * u, None)
            pe.wait_ge(hid_lo, 2 * KH)
            for m in range(8):
                w2(24, m, G1 + 3 * m, LAT, lambda k: U1h[:, k, :], lambda k: U1l[:, k, :], 7)
            norm(7, 7, LAT)


def tiles(w, cols=128):
    k, m = w.shape
    return np.ascontiguousarray(w.reshape(k // 128, 128, m // cols, cols).transpose(2, 1, 0, 3).reshape(m // cols, 128, -1))


def columns(v):
    return v.reshape(-1, 128).T


def swap_halves():
    return np.concatenate([np.arange(8, 16), np.arange(0, 8), np.arange(24, 32), np.arange(16, 24)])


def shape_tables():
    i = np.arange(128)
    r, c = i[:, None], i[None, :]
    t = np.zeros((128, NTAB), np.float32)
    for name, m in (("ident", r == c), ("gt", r > c), ("lt", r < c), ("le", r <= c), ("ge", r >= c)):
        t[:, TAB[name]:TAB[name] + 128] = m
    tok = np.arange(LAT)
    inv = (10000.0 ** (-np.arange(8, dtype=np.float32) * 2.0 / 16)).astype(np.float32)
    for axis, pos in ((0, tok // GRID_W), (1, tok % GRID_W)):
        ang = (pos.astype(np.float32)[None, :] * inv[:, None]).astype(np.float32)
        for half, sign in ((0, -1.0), (1, 1.0)):
            at = 16 * axis + 8 * half
            t[64 + at:72 + at, TAB["cos"]:TAB["cos"] + LAT] = np.cos(ang)
            t[96 + at:104 + at, TAB["sin"]:TAB["sin"] + LAT] = sign * np.sin(ang)
    return t


def lay_out(i):
    o = {}
    o["xT"] = np.concatenate([i["ctx"][0], i["x"][0]], axis=0).T.reshape(KD, 128, TOK).transpose(1, 0, 2)
    cw, cbias = i["ssd_conv_w"][0], i["ssd_conv_b"][0]
    order = np.concatenate([np.arange(INNER, INNER + 1024), np.arange(INNER)])
    cwt = cw[:, order].reshape(5, 24, 128).transpose(2, 1, 0).reshape(128, 120)
    o["par"] = np.concatenate([
        columns(i["c"][0]), columns(i["c_ctx"]), columns(i["ada_b"].reshape(-1)), columns(i["norm_mix"].reshape(-1)),
        columns(i["norm_ffn"].reshape(-1)), columns(i["mla_q_norm"][0]), columns(i["mla_kv_norm"][0]), cwt,
        columns(cbias[order]), columns(i["ssd_norm"][0]), columns(i["final_norm"])], axis=1)
    r = np.concatenate([i["ssd_dt_bias"][0].reshape(-1), i["ssd_a_log"][0].reshape(-1), i["ssd_d"][0]])
    o["rows"] = np.broadcast_to(r, (128, 160))
    o["tab"] = shape_tables()
    o["ada_w"] = np.concatenate([tiles(w, 256) for w in i["ada_w"]]).reshape(48, 128, 2, 1024).transpose(0, 2, 1, 3).reshape(96, 128, 1024)
    w = i["mla_w_in"][0]
    o["w_in"] = tiles(np.concatenate([w[:, 512:768], w[:, 704:800], w[:, 768 + swap_halves()], w[:, 0:512]], axis=1))
    q = i["mla_w_uq"][0].reshape(512, HEADS, QKD)
    o["w_uq"] = tiles(np.concatenate([q, q[:, :, 64 + swap_halves()]], axis=2).reshape(512, -1))
    kv = i["mla_w_ukv"][0].reshape(256, HEADS, 2, 64)
    o["w_uk"] = tiles(kv[:, :, 0].reshape(256, -1), 64)
    o["w_uv"] = kv[:, :, 1].reshape(2, 128, 1024)
    o["w_o"] = tiles(i["mla_w_o"][0])
    for n in ("w1", "w3", "w2"):
        o[n] = np.concatenate([tiles(w) for w in i["ffn_" + n]])
    w = i["ssd_w_in"][0]
    o["w_z"] = tiles(w[:, 0:INNER])
    xbc = w[:, INNER:INNER + 3072]
    o["w_xbc"] = tiles(xbc[:, order])
    o["w_dt"] = tiles(w[:, INNER + 3072:], 64)[0]
    o["w_so"] = tiles(i["ssd_w_o"][0]).reshape(8, 128, 2, 1024).transpose(0, 2, 1, 3).reshape(16, 128, 1024)
    return {k: np.ascontiguousarray(v) for k, v in o.items()}


def kernel(**inputs):
    import concourse.bacc as bacc
    from concourse import mybir
    from concourse.bass_utils import run_bass_kernel_spmd

    nc = bacc.Bacc("TRN2", target_bir_lowering=False, num_devices=1, dynamic_dma_scratch_size=1024)
    arrays = lay_out({k: np.asarray(v) for k, v in inputs.items()})
    aps = {k: nc.dram_tensor("in_" + k, v.shape, mybir.dt.from_np(v.dtype), kind="ExternalInput").ap() for k, v in arrays.items()}
    out = nc.dram_tensor("out", (128, KD, LAT), mybir.dt.float32, kind="ExternalOutput").ap()
    program(nc, aps, out)
    r = run_bass_kernel_spmd(nc, [{"in_" + k: v for k, v in arrays.items()}], core_ids=[0])
    got = r.results[0]["out"]
    return np.ascontiguousarray(got.transpose(2, 1, 0).reshape(1, LAT, D))
```

```python
import numpy as np


D = 1024
CTX = 256
LAT = 256
TOK = CTX + LAT
KD = D // 128
HEADS = 16
ROPE = 32
QKD = 96
KQ = 512 // 128
KKV = 256 // 128
HID = 2816
KH = HID // 128
SH = 32
GH = 8
GROUPS = 4
GW = GH * 64
INNER = 2048
KI = INNER // 128
EPS = 1e-6
GRID_W = 64

PAR = {}
_at = 0
for _name, _n in (("c", 8), ("cctx", 8), ("ada_b", 96), ("norm_mix", 16), ("norm_ffn", 16), ("q_norm", 4),
                  ("kv_norm", 2), ("conv_w", 120), ("conv_b", 24), ("ssd_norm", 16), ("final", 8)):
    PAR[_name] = _at
    _at += _n
NPAR = _at
TAB = {"ident": 0, "gt": 128, "lt": 256, "le": 384, "ge": 512, "cos": 640, "sin": 896}
NTAB = 1152

A0 = 0
IN = A0 + 16
VB = IN + 7
HP = VB + 2
HL = HP + 2
WO = HL + 4 * 15 + 2
F0 = WO + 8
G0 = F0 + 4 * KH
BC = G0 + 3 * KD + 4
DT = BC + 8
XS = DT + 1
ZS = XS + 16
SO = ZS + 16
F1 = SO + 2 * KD
G1 = F1 + 2 * KH
NBLK = G1 + 3 * KD
RING = 4
CB_BANK = (7, 0)
PT_BANK = (5, 6, 2)


def g0(m):
    return G0 + 3 * m + 2 * min(m, 2)


def block_cols():
    cols = [1024] * NBLK
    for i in range(-1, 15):
        n = HP if i < 0 else HL + 4 * i
        cols[n], cols[n + 1] = 512, 128
    cols[DT] = 512
    return cols


COLS = block_cols()
NORM_K = [8, 2, 4, 8, 8, 16, 8, 8]
NB = [sum(NORM_K[:w]) for w in range(len(NORM_K) + 1)]
USED = [len([v for v in range(w) if v not in (0, 5)]) for w in range(len(NORM_K) + 1)]
SQ = [sum(k for v, k in enumerate(NORM_K[:w]) if v not in (0, 5)) for w in range(len(NORM_K) + 1)]
SHARED = (0, 3, 4, 5, 6)
ODD = [sum(NORM_K[v] // 2 for v in range(w) if v in SHARED) for w in range(len(NORM_K) + 1)]
NORM_BANK = [6, 7, 6, 6, 6, 6, 6, 6]


STATE_TILES = (((0, 0), (1, 2), (2, 4)), ((0, 1), (1, 3), (3, 5)))


def late(t, k):
    return t >= k if isinstance(t, int) else True


def program(nc, a, out):
    import concourse.bass as bass
    from concourse import mybir
    from contextlib import ExitStack

    f32, f32r = mybir.dt.float32, mybir.dt.float32r
    ALU, ACT, AX = mybir.AluOpType, mybir.ActivationFunctionType, mybir.AxisListType
    MUL, ADD, SUB = ALU.mult, ALU.add, ALU.subtract
    ds = bass.ds

    with ExitStack() as fixed:
        def sb(name, shape, dt=f32, stack=fixed):
            return stack.enter_context(nc.sbuf_tensor(name, shape, dt))

        def sem(name):
            return fixed.enter_context(nc.semaphore(name))

        X = sb("residual", [128, KD, TOK])
        raw = [sb(f"raw{i}", [128, 1024]) for i in range(RING)]
        wh = [sb(f"w_hi{i}", [128, 1024], f32r) for i in range(RING)]
        wl = [sb(f"w_lo{i}", [128, 1024], f32r) for i in range(RING)]
        T = sb("scratch", [128, 8, 512])
        par = sb("par", [128, NPAR])
        rows = sb("rows", [128, 160])
        tab = sb("tab", [128, NTAB])
        ones = sb("ones", [128, 128])
        eps = sb("eps", [128, 1])
        sc = sb("silu_c", [128, 2, 8])
        smov = sb("silu_c_parts", [128, 8, 2, 2], f32r)
        mrow = sb("mod_rows", [128, 256])
        mod = [sb(f"mod{i}", [128, 48, 2]) for i in range(2)]
        gain = [sb(f"gain{i}", [128, 8, 2]) for i in range(4)]
        bank = [fixed.enter_context(nc.psum_tensor(f"bank{i}", [128, 512], f32)) for i in range(8)]

        def tabv(name, n=128):
            return tab[:, TAB[name]:TAB[name] + n]

        with ExitStack() as ph:
            Hmh, Hml = (sb(f"mla_h_{p}", [128, KD, TOK], f32r, ph) for p in ("hi", "lo"))
            Oh, Ol = Hmh, Hml
            cq = sb("cq", [128, KQ + KKV, TOK], f32, ph)
            kf = sb("k_rope", [128, TOK], f32, ph)
            cnh, cnl = (sb(f"c_normed_{p}", [128, KQ + KKV, TOK], f32r, ph) for p in ("hi", "lo"))
            qf = sb("q_f32", [128, TOK], f32, ph)
            qh, ql = (sb(f"q_{p}", [128, TOK], f32r, ph) for p in ("hi", "lo"))
            kh, kl = (sb(f"k_{p}", [128, TOK], f32r, ph) for p in ("hi", "lo"))
            vh, vl = (sb(f"v_{p}", [128, 4, 64 * HEADS], f32r, ph) for p in ("hi", "lo"))
            vsh, vsl = (sb(f"v_head_{p}", [128, 2, 4, 64], f32r, ph) for p in ("hi", "lo"))
            P, rtmp = T[:, 5:8, :], T[:, 4, 0:LAT]
            PTh, PTl = (sb(f"probs_t_{p}", [128, 6, 256], f32r, ph) for p in ("hi", "lo"))
            mx, nm, ssum, rs_ = (sb(f"softmax_{p}", [128, 4], f32, ph) for p in ("max", "negmax", "sum", "inv"))
        with ExitStack() as ph:
            H0h, H0l = (sb(f"ffn0_h_{p}", [128, KD, TOK], f32r, ph) for p in ("hi", "lo"))
            U0h, U0l = (sb(f"ffn0_hidden_{p}", [128, KH, TOK], f32r, ph) for p in ("hi", "lo"))
        with ExitStack() as ph:
            xtok = sb("x_tok", [128, 4, INNER], f32, ph)
            Bth, Btl = (sb(f"B_tok_{p}", [128, 4, GROUPS, 128], f32r, ph) for p in ("hi", "lo"))
            CTh, CTl = (sb(f"C_T_{p}", [128, GROUPS, LAT], f32r, ph) for p in ("hi", "lo"))
            zs = sb("z_gate", [128, KI, LAT], f32, ph)
            dt = sb("dt", [128, 4, 64], f32, ph)
            dtA = sb("dtA", [128, 4, 64], f32, ph)
            dtAh, dtAl = (mrow[:, at:at + 128].rearrange("p (c h) -> p c h", c=2) for at in (0, 128))
            w6 = sb("state_w", [128, 6, SH], f32, ph)
            et = sb("exp_sums", [128, 384], f32, ph)
            maskr = sb("masks_r", [128, 2, 128], f32r, ph)
            cbf, cbb = X[:, :, 0:128], X[:, :, 128:256]
            with ExitStack() as ph2:
                H1h, H1l = (sb(f"ssd_h_{p}", [128, KD, TOK], f32r, ph2) for p in ("hi", "lo"))
                up = sb("conv_in", [128, 2, 2, 260], f32, ph2)
                dtw = sb("dt_work", [128, 6, 256], f32, ph2)
                dtT = sb("dt_T", [64, TOK], f32, ph2)
                BTh, BTl = (sb(f"B_T_{p}", [128, GROUPS, LAT], f32r, ph2) for p in ("hi", "lo"))
            with ExitStack() as ph2:
                xsh, xsl = (sb(f"xs_{p}", [128, 3, GW], f32r, ph2) for p in ("hi", "lo"))
                def squared(g):
                    return xtok[:, 2:4, GW * g:GW * g + GW]

                xsf = (T[:, 0, :], T[:, 1, :], tab[:, TAB["cos"]:NTAB])
                hh, hl = (sb(f"state_{p}", [128, 2, GW], f32r, ph2) for p in ("hi", "lo"))
                mh, ml = (sb(f"dtA_mask_{p}", [128, GH, 128], f32r, ph2) for p in ("hi", "lo"))
                E = sb("decay", [128, GH, 128], f32, ph2)
                xgh, xgl = (sb(f"x_group_{p}", [128, 2, GW], f32r, ph2) for p in ("hi", "lo"))
                Y = sb("y_tok", [128, 4, GW], f32, ph2)
                Wh, Wl = (sb(f"W_{p}", [128, GH, 128], f32r, ph2) for p in ("hi", "lo"))
            with ExitStack() as ph2:
                Hyh, Hyl = (sb(f"y_{p}", [128, KI, LAT], f32r, ph2) for p in ("hi", "lo"))
        with ExitStack() as ph:
            H2h, H2l = (sb(f"ffn1_h_{p}", [128, KD, LAT], f32r, ph) for p in ("hi", "lo"))
            U1h, U1l = (sb(f"ffn1_hidden_{p}", [128, KH, LAT], f32r, ph) for p in ("hi", "lo"))
            yout = sb("y_out", [128, KD, LAT], f32, ph)

        raw_loaded = [sem(f"raw_loaded{i}") for i in range(RING)]
        w_hi, w_lo, w_used = sem("w_hi"), sem("w_lo"), sem("w_used")
        par_in, x_in, inputs_in = sem("par_in"), sem("x_in"), sem("inputs_in")
        ones_set, silu_c, sc_hi, sc_lo = sem("ones_set"), sem("silu_c_done"), sem("sc_hi"), sem("sc_lo")
        row_cp, row_tr, mod_ev, mod_done = sem("row_copied"), sem("row_turned"), sem("mod_out"), sem("mod_done")
        sq_ready, sq_used, root, inv = sem("sq_ready"), sem("sq_used"), sem("rms_root"), sem("rms_inv")
        x_sq, x_acc, gate_sq, gate_acc, sum_done = (sem(x) for x in ("x_squared", "x_summed", "gate_squared", "gate_summed", "sum_done"))
        nx, nodd = sem("over_rms"), sem("normed_odd")
        nv, nhi, nlo = sem("normed"), sem("normed_hi"), sem("normed_lo")
        proj_out = sem("proj_out")
        kr_part, kr_done, kr_hi, kr_lo = sem("kr_part"), sem("kr_done"), sem("kr_hi"), sem("kr_lo")
        q_cp, rope_part, q_rope, q_hi, q_lo = sem("q_copied"), sem("rope_part"), sem("q_roped"), sem("q_hi_"), sem("q_lo_")
        k_hi, k_lo, v_hi, v_lo, v_mm, v_cp = sem("k_hi_"), sem("k_lo_"), sem("v_hi_"), sem("v_lo_"), sem("v_mm"), sem("v_cp")
        dt_cp, dt_tr = sem("dt_copied"), sem("dt_turned")
        s_mm, maxed, nmax, exp_done, rcp, p_norm = (sem(x) for x in ("scores_mm", "maxed", "negmax", "exp_done", "sum_inv", "p_norm"))
        pt_mm, pt_hi, pt_lo, o_mm, o_hi, o_lo = (sem(x) for x in ("pt_mm", "pt_hi", "pt_lo", "o_mm", "o_hi_", "o_lo_"))
        added = sem("added")
        silu_done, hid_f, hid_hi, hid_lo = (sem(x) for x in ("silu_done", "hid_f", "hid_hi", "hid_lo"))
        up_zero, conv_up, conv_init, conv_tap, conv_y, conv_tr, conv_ev, conv_hi, ct_hi, ct_lo = (sem(x) for x in (
            "up_zero", "conv_up", "conv_init", "conv_tap", "conv_y", "conv_tr", "conv_ev", "conv_hi", "ct_hi", "ct_lo"))
        dt_dve, dt_act, cum_mm, cum_exp = (sem(x) for x in ("dt_dve", "dt_act", "cum_mm", "cum_exp"))
        masks_r, dta_hi, w6_done = sem("masks_r_done"), sem("dta_parts"), sem("state_w_done")
        cb_mm, cb_done = sem("cb_mm"), sem("cb_done")
        xs_f, xs_hi, xs_lo, st_mm = (sem(x) for x in ("xs_f", "xs_hi_", "xs_lo_", "states_mm"))
        st_hi, st_dec, st_sum, st_lo, off_mm = (sem(x) for x in ("st_hi", "st_dec", "st_sum", "st_lo", "off_mm"))
        mk_hi, mk_lo, dec_mm, dec_exp, gb, gd, wf, W_hi, W_lo = (sem(x) for x in (
            "masked_hi", "masked_lo", "dec_mm", "dec_exp", "g_backward", "g_done", "w_f32", "W_hi_", "W_lo_"))
        off_rd, y_off = sem("off_read"), sem("y_off_done")
        xg_hi, xg_lo, dg_mm, dx, yx, y_done, yt_mm, yt_done = (sem(x) for x in (
            "xg_hi_", "xg_lo_", "diag_mm", "dx", "y_dx", "y_done", "yt_mm", "yt_done"))
        out_done, stored = sem("out_done"), sem("stored")

        block = fixed.enter_context(nc.Block())

        @block.sync
        def _(sp):
            def load(n, s, dst_cols, src):
                if late(n, RING):
                    sp.wait_ge(w_lo, n - RING + 1)
                sp.dma_start(raw[s % RING][:, 0:dst_cols], src).then_inc(raw_loaded[s % RING], 16)

            def one(name, t):
                return a[name][ds(t, 1), :, :].rearrange("o p n -> (o p) n")

            def ada(n, s, q):
                load(n, s, 1024, one("ada_w", 2 * q))
                load(n + 1, s + 1, 1024, one("ada_w", 2 * q + 1))

            sp.dma_start(par[:, :], a["par"]).then_inc(par_in, 16)
            ada(A0, A0, 0)
            sp.dma_start(tab[:, :], a["tab"]).then_inc(inputs_in, 16)
            sp.dma_start(rows[:, :], a["rows"]).then_inc(inputs_in, 16)
            for q in range(1, 3):
                ada(A0 + 2 * q, A0 + 2 * q, q)
            sp.dma_start(X[:, :, :], a["xT"]).then_inc(x_in, 16)
            for q in range(3, 8):
                ada(A0 + 2 * q, A0 + 2 * q, q)
            for t in range(7):
                load(IN + t, IN + t, 1024, one("w_in", t))
            for t in range(2):
                load(VB + t, VB + t, 1024, one("w_uv", t))
            load(HP, HP, 512, one("w_uq", 0))
            load(HP + 1, HP + 1, 128, one("w_uk", 0))
            with sp.Fori(0, 15) as i:
                n = HL + 4 * i
                load(n, HL, 512, one("w_uq", i + 1))
                load(n + 1, HL + 1, 128, one("w_uk", i + 1))
                ada(n + 2, HL + 2, 8 + i)
            ada(WO - 2, WO - 2, 23)
            for t in range(8):
                load(WO + t, WO + t, 1024, one("w_o", t))
            with sp.Fori(0, KH) as j:
                load(F0 + 4 * j, F0, 1024, one("w1", j))
                load(F0 + 4 * j + 1, F0 + 1, 1024, one("w3", j))
                ada(F0 + 4 * j + 2, F0 + 2, 24 + j)

            K3 = ((0, 8), (8, 16), (16, KH))
            for m in range(8):
                for r, (k0, k1) in enumerate(K3):
                    load(g0(m) + r, g0(m) + r, 128 * (k1 - k0), one("w2", m)[:, 128 * k0:128 * k1])
                if m < 2:
                    ada(g0(m) + 3, g0(m) + 3, 46 + m)
            for t in range(8):
                load(BC + t, BC + t, 1024, one("w_xbc", t))
            load(DT, DT, 512, a["w_dt"])
            with sp.Fori(0, 4) as i:
                for u in range(4):
                    load(XS + 4 * i + u, XS + u, 1024, one("w_xbc", 8 + 4 * i + u))
            with sp.Fori(0, 4) as i:
                for u in range(4):
                    load(ZS + 4 * i + u, ZS + u, 1024, one("w_z", 4 * i + u))
            with sp.Fori(0, 4) as i:
                for u in range(4):
                    load(SO + 4 * i + u, SO + u, 1024, one("w_so", 4 * i + u))
            with sp.Fori(0, KH // 2) as i:
                for u in range(2):
                    load(F1 + 4 * i + 2 * u, F1 + 2 * u, 1024, one("w1", KH + 2 * i + u))
                    load(F1 + 4 * i + 2 * u + 1, F1 + 2 * u + 1, 1024, one("w3", KH + 2 * i + u))
            with sp.Fori(0, 2) as i:
                for u in range(4):
                    for r, (k0, k1) in enumerate(K3):
                        load(G1 + 12 * i + 3 * u + r, G1 + 3 * u + r, 128 * (k1 - k0), one("w2", 8 + 4 * i + u)[:, 128 * k0:128 * k1])
            for k in range(KD):
                sp.wait_ge(out_done, k + 1)
                sp.dma_start(out[:, k, :], yout[:, k, :]).then_inc(stored, 16)
            sp.wait_ge(stored, 16 * KD)

        @block.gpsimd
        def _(pool):
            nc.gpsimd.memset(ones[:, :], 1.0).then_inc(ones_set, 1)
            nc.gpsimd.memset(eps[:, :], EPS).then_inc(ones_set, 1)

            pool.wait_ge(x_in, 16)
            nc.gpsimd.tensor_tensor(T[:, 6, :], X[:, 0, :], X[:, 0, :], MUL).then_inc(x_acc, 1)
            for k in range(1, KD):
                if k >= 3:
                    pool.wait_ge(x_acc, k - 1)
                nc.gpsimd.tensor_tensor(T[:, k % 2, :], X[:, k, :], X[:, k, :], MUL).then_inc(x_sq, 1)
                pool.wait_ge(x_sq, k)
                pool.wait_ge(x_acc, k)
                nc.gpsimd.tensor_tensor(T[:, 6, :], T[:, 6, :], T[:, k % 2, :], ADD).then_inc(x_acc, 1)

            def accumulate(w, n):
                b = SQ[w]
                pool.wait_ge(sum_done, w)
                for k in range(1, NORM_K[w] - 1):
                    pool.wait_ge(sq_ready, b + k + 1)
                    if k > 1:
                        pool.wait_ge(sq_used, b + k - USED[w])
                    before = T[:, b % 2, 0:n] if k == 1 else T[:, 6, 0:n]
                    nc.gpsimd.tensor_tensor(T[:, 6, 0:n], before, T[:, (b + k) % 2, 0:n], ADD).then_inc(sq_used, 2 if k == 1 else 1)

            def over_rms(w, src, c0, c1):
                pool.wait_ge(inv, w + 1)
                for k in range(1, NORM_K[w], 2):
                    if k >= 5:
                        pool.wait_ge(nlo, NB[w] + k - 3)
                    nc.gpsimd.tensor_tensor(T[:, 6 + k // 2 % 2, 0:c1 - c0], src(k), T[:, 5, 0:c1 - c0], MUL).then_inc(nx, 1)

            over_rms(0, lambda k: X[:, k, :], 0, TOK)
            accumulate(2, TOK)

            def scale_probs(i, u):
                pool.wait_ge(rcp, 3 * i + 1)
                if late(i, 2):
                    pool.wait_ge(o_mm, i - 1)
                nc.gpsimd.tensor_tensor(P[:, 0, :], P[:, 0, :], rs_[:, 0:1].to_broadcast([128, 512]), MUL).then_inc(p_norm, 1)
                nc.gpsimd.tensor_copy(vsh[:, u, :, :], vh[:, :, ds(64 * i, 64)])
                nc.gpsimd.tensor_copy(vsl[:, u, :, :], vl[:, :, ds(64 * i, 64)]).then_inc(v_cp, 1)
                pool.wait_ge(rcp, 3 * i + 2)
                nc.gpsimd.tensor_tensor(P[:, 1, :], P[:, 1, :], rs_[:, 1:2].to_broadcast([128, 512]), MUL).then_inc(p_norm, 1)
                pool.wait_ge(rcp, 3 * i + 3)
                nc.gpsimd.tensor_tensor(P[:, 2, :].rearrange("p (a k) -> p a k", a=2), P[:, 2, :].rearrange("p (a k) -> p a k", a=2),
                                        rs_[:, 2:4].unsqueeze(2).to_broadcast([128, 2, 256]), MUL).then_inc(p_norm, 1)

            def q_low(i):
                pool.wait_ge(q_hi, i + 1)
                nc.gpsimd.tensor_tensor(ql[0:QKD, :], qf[0:QKD, :], qh[0:QKD, :].bitcast(f32), SUB).then_inc(q_lo, 1)

            pool.wait_ge(v_lo, 8)
            q_low(0)
            for i in range(2):
                scale_probs(i, i)
                q_low(i + 1)
            with pool.Fori(1, HEADS // 2 - 1) as i:
                for u in range(2):
                    scale_probs(2 * i + u, u)
                    q_low(2 * i + u + 1)
            scale_probs(14, 0)
            q_low(15)
            scale_probs(15, 1)

            accumulate(3, TOK)
            over_rms(3, lambda k: X[:, k, :], 0, TOK)
            accumulate(4, TOK)
            over_rms(4, lambda k: X[:, k, :], 0, TOK)
            pool.wait_ge(added, 16)
            pool.wait_ge(w_used, BC)
            for u in range(2):
                nc.gpsimd.memset(up[:, u, :, 0:2], 0.0).then_inc(up_zero, 1)
                nc.gpsimd.memset(up[:, u, :, 258:260], 0.0).then_inc(up_zero, 1)

            def per_head(ap, w):
                return ap.unsqueeze(2).to_broadcast([128, GH, w])

            def weigh_x(e):
                g, d_ = divmod(e, 2)
                for s, (tt, row) in enumerate(STATE_TILES[d_]):
                    i = 3 * e + s
                    if e:
                        pool.wait_ge(xs_lo, i - 2)
                    nc.gpsimd.tensor_tensor(
                        xsf[s].rearrange("p (h d) -> p h d", d=64),
                        xtok[:, tt, GW * g:GW * g + GW].rearrange("p (h d) -> p h d", d=64),
                        per_head(w6[:, row, GH * g:GH * g + GH], 64), MUL).then_inc(xs_f, 1)

            def mask(m, d_):
                g, c = divmod(m, 2)
                if 2 * m + d_ >= 1:
                    pool.wait_ge(dec_mm, 2 * m + d_)
                nc.gpsimd.tensor_tensor(mh[:, :, :], tabv(("le", "ge")[d_]).unsqueeze(1).to_broadcast([128, GH, 128]),
                                        per_head(dtAh[:, c, 32 * d_ + GH * g:32 * d_ + GH * g + GH], 128), MUL).then_inc(mk_hi, 1)

            def backward(m):
                g, c = divmod(m, 2)
                if m >= 1:
                    pool.wait_ge(gd, m)
                nc.gpsimd.tensor_tensor(
                    T[:, 4:6, :].rearrange("p a (h q) -> p (a h) q", q=128),
                    cbb[:, 4 * c + g, :].unsqueeze(1).to_broadcast([128, GH, 128]),
                    per_head(dt[:, 2 + c, 32 + GH * g:32 + GH * g + GH], 128), MUL).then_inc(gb, 1)

            def skip(m):
                g, c = divmod(m, 2)
                if m >= 1:
                    pool.wait_ge(yx, m)
                nc.gpsimd.tensor_tensor(
                    T[:, 7, :].rearrange("p (h d) -> p h d", d=64),
                    xtok[:, 2 + c, GW * g:GW * g + GW].rearrange("p (h d) -> p h d", d=64),
                    per_head(rows[:, 128 + GH * g:128 + GH * g + GH], 64), MUL).then_inc(dx, 1)
                pool.wait_ge(dx, m + 1)
                pool.wait_ge(y_off, 2 * g + 2)
                y = Y[:, 2 * (g % 2) + c, :]
                nc.gpsimd.tensor_tensor(y, y, T[:, 7, :], ADD).then_inc(yx, 1)

            pool.wait_ge(w6_done, 3)
            pool.wait_ge(conv_ev, 20)
            pool.wait_ge(dta_hi, 2)
            pool.wait_ge(cb_done, 4)
            backward(0)
            weigh_x(0)
            pool.wait_ge(w_used, SO)
            mask(0, 0)
            mask(0, 1)
            weigh_x(1)
            mask(1, 0)
            backward(1)
            mask(1, 1)
            weigh_x(2)
            backward(2)
            mask(2, 0)
            for m in range(8):
                if m < 5:
                    weigh_x(m + 3)
                if m < 6:
                    mask(m + 2, 1)
                skip(m)
                if m < 5:
                    backward(m + 3)
                    mask(m + 3, 0)
                if m >= 6:
                    pool.wait_ge(gate_sq, m - 4)
                    if m == 7:
                        pool.wait_ge(gate_acc, 1)
                    nc.gpsimd.tensor_tensor(squared(0), squared(0), squared(m - 5), ADD).then_inc(gate_acc, 1)
            over_rms(5, lambda k: zs[:, k, :], 0, LAT)
            accumulate(6, LAT)
            over_rms(6, lambda k: X[:, k, CTX:TOK], CTX, TOK)
            accumulate(7, LAT)

        @block.scalar
        def _(act):
            A = nc.scalar.activation

            def hi(n, s):
                if isinstance(n, int) and n >= NBLK:
                    return
                act.wait_ge(raw_loaded[s % RING], 4 * (n - s % RING) + 16)
                if late(n, RING):
                    act.wait_ge(w_used, n - RING + 1)
                c = COLS[s]
                A(wh[s % RING][:, 0:c], raw[s % RING][:, 0:c], ACT.Copy).then_inc(w_hi, 1)

            def square(w, k, src):
                m = SQ[w] + k
                if k >= 2:
                    act.wait_ge(sq_used, m - 1 - USED[w])
                else:
                    act.wait_ge(sum_done, w)
                A(T[:, m % 2, 0:src.shape[-1]], src, ACT.Square).then_inc(sq_ready, 1)

            def squares(w, m, q0, c0):
                act.wait_ge(added, q0 + m + 1)
                square(w, m, X[:, m, c0:TOK])

            def rms(w, n, dim):
                act.wait_ge(sum_done, w + 1)
                if w >= 1:
                    act.wait_ge(inv, w)
                A(T[:, 4, 0:n], bank[NORM_BANK[w]][:, 0:n], ACT.Sqrt, bias=eps[:, 0:1], scale=1.0 / dim).then_inc(root, 1)

            def his(w, groups, hdst, shift, ks=None):
                t0 = groups[0][1]
                for k in ks or range(NORM_K[w]):
                    act.wait_ge(nv, NB[w] + k + 1)
                    for g, (m, c0, c1) in enumerate(groups):
                        v = T[:, 2 + k % 2, c0 - t0:c1 - t0]
                        if shift is None:
                            ins = A(hdst(k, c0, c1), v, ACT.Copy)
                        else:
                            ins = A(hdst(k, c0, c1), v, ACT.Identity, bias=shift(k, m))
                    ins.then_inc(nhi, 1)

            def his_shared(w, groups, hdst, gn, shift):
                t0, t1 = groups[0][1], groups[-1][2]
                for k in range(NORM_K[w]):
                    if k % 2 == 0:
                        act.wait_ge(nv, NB[w] + k + 2)
                        for m, c0, c1 in groups:
                            v = T[:, 2 + k // 2 % 2, c0 - t0:c1 - t0]
                            if shift is None:
                                ins = A(hdst(k, c0, c1), v, ACT.Copy)
                            else:
                                ins = A(hdst(k, c0, c1), v, ACT.Identity, bias=shift(k, m))
                    else:
                        act.wait_ge(nx, ODD[w] + k // 2 + 1)
                        for m, c0, c1 in groups:
                            v = T[:, 6 + k // 2 % 2, c0 - t0:c1 - t0]
                            if shift is None:
                                ins = A(v, v, ACT.Copy, scale=gn(k, m))
                            else:
                                ins = A(v, v, ACT.Identity, bias=shift(k, m), scale=gn(k, m))
                        ins.then_inc(nodd, 1)
                        act.wait_ge(nodd, ODD[w] + k // 2 + 1)
                        ins = A(hdst(k, t0, t1), T[:, 6 + k // 2 % 2, 0:t1 - t0], ACT.Copy)
                    ins.then_inc(nhi, 1)

            act.wait_ge(par_in, 16)
            A(sc[:, :, :], par[:, 0:16].rearrange("p (s k) -> p s k", s=2), ACT.Silu).then_inc(silu_c, 1)
            act.wait_ge(silu_c, 1)
            A(smov[:, :, :, 0], sc[:, :, :].rearrange("p s k -> p k s"), ACT.Copy).then_inc(sc_hi, 1)
            for n in range(RING):
                hi(n, n)
            for t in range(16):
                hi(A0 + t + RING, A0 + t + RING)
            act.wait_ge(inputs_in, 32)
            act.wait_ge(ones_set, 2)
            both = [(1, 0, CTX), (0, CTX, TOK)]
            rms(0, TOK, D)
            his_shared(0, both, lambda k, c0, c1: Hmh[:, k, c0:c1], lambda k, m: gain[0][:, k, m:m + 1], lambda k, m: mod[0][:, k, m:m + 1])

            whole = [(0, 0, TOK)]
            for t in range(7):
                act.wait_ge(w_used, IN + t + 1)
                if t == 2:
                    A(kf[64:96, :], bank[0][64:96, :], ACT.Copy).then_inc(proj_out, 1)
                else:
                    c = t if t < 2 else t - 1
                    square(1 if t < 2 else 2, c if t < 2 else c - 2, bank[t % 2][:, :])
                    A(cq[:, c, :], bank[t % 2][:, :], ACT.Copy).then_inc(proj_out, 1)
                hi(IN + t + RING, IN + t + RING)
                if t == 2:
                    act.wait_ge(kr_done, 1)
                    A(kh[64:96, :], kf[64:96, :], ACT.Copy).then_inc(kr_hi, 1)
                if t == 3:
                    rms(1, TOK, 128 * KKV)
                    his(1, whole, lambda k, c0, c1: cnh[:, k, c0:c1], None)
            for g in range(8):
                if g == 2:
                    rms(2, TOK, 128 * KQ)
                if g < 7:
                    act.wait_ge(v_mm, g + 1)
                else:
                    act.wait_ge(w_used, VB + 2)
                A(vh[:, g // 2, 512 * (g % 2):512 * (g % 2) + 512], bank[2 + g % 4][:, :], ACT.Copy).then_inc(v_hi, 1)
                if g >= 4:
                    his(2, whole, lambda k, c0, c1: cnh[:, KKV + k, c0:c1], None, [g - 4])
            hi(VB + 4, VB + 4)
            hi(VB + 5, VB + 5)

            def project(i, n, s, between):
                act.wait_ge(w_used, n + 1)
                if late(i, 1):
                    act.wait_ge(q_lo, i)
                    act.wait_ge(s_mm, 3 * i)
                A(qf[0:QKD, :], bank[0][0:QKD, :], ACT.Copy).then_inc(q_cp, 1)
                act.wait_ge(w_used, n + 2)
                A(kh[0:64, :], bank[1][0:64, :], ACT.Copy).then_inc(k_hi, 1)
                between()
                act.wait_ge(q_rope, i + 1)
                A(qh[0:QKD, :], qf[0:QKD, :], ACT.Copy).then_inc(q_hi, 1)
                hi(n + 4, s + 4)
                hi(n + 5, s + 5)

            def exps(i, p):
                act.wait_ge(nmax, 3 * i + p + 1)
                if late(i, 1):
                    act.wait_ge(pt_mm, 3 * i - 2 + p)
                    act.wait_ge(rcp, 3 * i - 2 + p)
                scale = float(QKD) ** -0.5
                if p < 2:
                    A(P[:, p, :], bank[p][:, :], ACT.Exp, bias=nm[:, p:p + 1], scale=scale,
                      accum_out=ssum[:, p:p + 1]).then_inc(exp_done, 1)
                else:
                    for t in range(2):
                        A(P[:, 2, 256 * t:256 * t + 256], bank[4][:, 256 * t:256 * t + 256], ACT.Exp,
                          bias=nm[:, 2 + t:3 + t], scale=scale, accum_out=ssum[:, 2 + t:3 + t]).then_inc(exp_done, 1)

            def pt_split(i, p):
                act.wait_ge(pt_mm, 3 * i + p + 1)
                if late(i, 1):
                    act.wait_ge(o_mm, i)
                b = bank[PT_BANK[p]]
                if p < 2:
                    dst, src = PTh[:, 0:4, 128 * p:128 * p + 128], b[:, :].rearrange("p (k q) -> p k q", q=128)
                else:
                    dst, src = PTh[:, 4:6, :], b[:, :].rearrange("p (k q) -> p k q", q=256)
                A(dst, src, ACT.Copy).then_inc(pt_hi, 1)

            def head(i, j, u):
                n, s = HL + 4 * i, HL + 4 * (i if isinstance(i, int) else u)
                more = not isinstance(i, int) or i < 15
                if more:
                    project(i + 1, n, s, lambda: pt_split(i, 0))
                    n, s = n + 2, s + 2
                else:
                    pt_split(i, 0)
                pt_split(i, 1)
                pt_split(i, 2)
                hi(n + 4, s + 4)
                hi(n + 5, s + 5)
                for p in range(3 if more else 0):
                    exps(i + 1, p)
                act.wait_ge(o_mm, i + 1)
                A(Oh[64 * u:64 * u + 64, ds(j, 1), :].rearrange("p o t -> p (o t)"), bank[3][0:64, :], ACT.Copy).then_inc(o_hi, 1)

            project(0, HP, HP, lambda: None)
            for p in range(3):
                exps(0, p)
            head(0, 0, 0)
            head(1, 0, 1)
            with act.Fori(1, 7) as j:
                head(2 * j, j, 0)
                head(2 * j + 1, j, 1)
            head(14, 7, 0)
            head(15, 7, 1)
            for m in range(8):
                hi(WO + m + RING, WO + m + RING)
                squares(3, m, 0, 0)
            rms(3, TOK, D)
            his_shared(3, both, lambda k, c0, c1: H0h[:, k, c0:c1], lambda k, m: gain[1][:, k, m:m + 1], lambda k, m: mod[0][:, 24 + k, m:m + 1])

            def hidden(j, g, u, nt, U, n, s, splits):
                act.wait_ge(w_used, n + 1)
                if late(g, 2):
                    act.wait_ge(hid_f, g - 1)
                A(T[:, u, 0:nt], bank[2 + 2 * u][:, 0:nt], ACT.Silu).then_inc(silu_done, 1)
                hi(n + 4, s + 4)
                hi(n + 5, s + 5)
                act.wait_ge(hid_f, g + 1)
                A(U[:, ds(j, 1), :].rearrange("p o t -> p (o t)"), T[:, 2 + u, 0:nt], ACT.Copy).then_inc(hid_hi, 1)
                for r in range(6, splits):
                    hi(n + r, s + r)

            for j in range(2):
                hidden(j, j, j % 2, TOK, U0h, F0 + 4 * j, F0 + 4 * j, 8)
            with act.Fori(1, KH // 2) as i:
                for u in range(2):
                    hidden(2 * i + u, 2 * i + u, u, TOK, U0h, F0 + 8 * i + 4 * u, F0 + 4 * u, 8)
            for m in range(8):
                for n in range(g0(m), g0(m + 1)):
                    hi(n + RING, n + RING)
                squares(4, m, 8, 0)
            rms(4, TOK, D)

            act.wait_ge(mod_done, 6)
            his_shared(4, both, lambda k, c0, c1: H1h[:, k, c0:c1], lambda k, m: gain[2][:, k, m:m + 1], lambda k, m: mod[1][:, k, m:m + 1])
            act.wait_ge(up_zero, 4)

            def conv(t, n, s, u, kind):
                seg = slice(1, 2) if kind == "C" else slice(0, 2)
                act.wait_ge(w_used, n + 1)
                if late(t, 2):
                    act.wait_ge(conv_tap, 4 * t - 4)
                if kind == "C":
                    A(up[:, u, 1, 2:258], bank[u][:, 256:512], ACT.Copy).then_inc(conv_up, 1)
                else:
                    A(up[:, u, :, 2:258], bank[u][:, :].rearrange("p (s t) -> p s t", s=2), ACT.Copy).then_inc(conv_up, 1)
                act.wait_ge(conv_up, t + 1)
                acc = T[:, u, :].rearrange("p (s t) -> p s t", s=2)[:, seg, :]
                A(acc, up[:, u, seg, 0:256], ACT.Identity, bias=par[:, ds(PAR["conv_b"] + t, 1)],
                  scale=par[:, ds(PAR["conv_w"] + 5 * t, 1)]).then_inc(conv_init, 1)
                hi(n + 4, s + 4)
                act.wait_ge(conv_tap, 4 * t + 4)
                if kind == "x" and late(t, 10):
                    act.wait_ge(conv_tr, t - 5)
                if kind == "B" and t >= 2:
                    act.wait_ge(conv_tr, t - 1)
                    act.wait_ge(ct_lo, t - 1)
                if kind == "C":
                    act.wait_ge(ct_lo, t - 1)
                    act.wait_ge(conv_tr, min(4, t - 1))
                if kind == "x" and isinstance(t, int) and t < 10:
                    act.wait_ge(ct_lo, t - 1)
                y = T[:, 2 + u, :].rearrange("p (s t) -> p s t", s=2)[:, seg, :]
                A(y, acc, ACT.Silu).then_inc(conv_y, 1)
                if kind in "BC":
                    g, dst = t % 4, BTh if kind == "B" else CTh
                    act.wait_ge(conv_y, t + 1)
                    A(dst[:, g, :], T[:, 2 + u, 256:512], ACT.Copy).then_inc(ct_hi, 1)

            for t in range(8):
                conv(t, BC + t, BC + t, t % 2, "BC"[t // 4])
                if 1 <= t <= 4:
                    act.wait_ge(conv_tr, t)
                    A(Bth[:, :, t - 1, :], bank[3 - t % 2][:, :].rearrange("p (t n) -> p t n", n=128), ACT.Copy).then_inc(conv_hi, 1)
            act.wait_ge(w_used, DT + 1)
            A(dtT[:, :], bank[4][0:64, :], ACT.Copy).then_inc(dt_cp, 1)
            hi(DT + RING, DT + RING)
            W = dtw
            conv(8, XS, XS, 0, "x")
            act.wait_ge(dt_dve, 2)
            A(W[:, 2, :], W[:, 1, :], ACT.Exp, scale=-1.0).then_inc(dt_act, 1)
            A(rows[:, 64:128], rows[:, 64:128], ACT.Exp).then_inc(dt_act, 1)
            conv(9, XS + 1, XS + 1, 1, "x")
            act.wait_ge(dt_dve, 3)
            A(W[:, 4, :], W[:, 3, :], ACT.Ln).then_inc(dt_act, 1)
            for u in range(2, 4):
                conv(8 + u, XS + u, XS + u, u % 2, "x")
            with act.Fori(1, 4) as i:
                for u in range(4):
                    conv(8 + 4 * i + u, XS + 4 * i + u, XS + u, u % 2, "x")
            act.wait_ge(masks_r, 2)
            act.wait_ge(cum_mm, 1)
            A(et[:, :], bank[6][:, 0:384], ACT.Exp).then_inc(cum_exp, 1)
            with act.Fori(0, 4) as i:
                for u in range(4):
                    act.wait_ge(w_used, ZS + 4 * i + u + 1)
                    A(zs[:, ds(4 * i + u, 1), :].rearrange("p o t -> p (o t)"), bank[4 + u % 2][:, 0:LAT], ACT.Silu).then_inc(conv_y, 1)
                    hi(ZS + 4 * i + u + 4, ZS + u + 4)

            def weighed_hi(e):
                for i in range(3 * e, 3 * e + 3):
                    act.wait_ge(xs_f, i + 1)
                    if e:
                        act.wait_ge(st_mm, i - 2)
                    A(xsh[:, i % 3, :], xsf[i % 3], ACT.Copy).then_inc(xs_hi, 1)

            def mask(m, d_):
                g, c = divmod(m, 2)
                if 2 * m + d_ >= 1:
                    act.wait_ge(dec_mm, 2 * m + d_)
                for h in range(GH):
                    at = 32 * d_ + GH * g + h
                    last = A(ml[:, h, :], tabv(("le", "ge")[d_]), ACT.Copy, scale=dtAl[:, c, at:at + 1])
                last.then_inc(mk_lo, 1)

            def state_hi(e):
                act.wait_ge(st_mm, 3 * e + 3)
                if e >= 1:
                    act.wait_ge(off_mm, 2 * e)
                A(hh[:, 0, :], bank[0][:, :], ACT.Copy).then_inc(st_hi, 1)

            def next_state_hi(e):
                act.wait_ge(st_sum, e + 1)
                A(hh[:, 1, :], T[:, 6, :], ACT.Copy).then_inc(st_hi, 1)

            def exps(m):
                act.wait_ge(dec_mm, 2 * m + 2)
                if m >= 1:
                    act.wait_ge(W_lo, m)
                for b in range(2):
                    A(E[:, 4 * b:4 * b + 4, :], bank[6 + b][:, :].rearrange("p (h q) -> p h q", q=128), ACT.Exp).then_inc(dec_exp, 1)

            def weights_hi(m):
                act.wait_ge(wf, m + 1)
                if m >= 1:
                    act.wait_ge(dg_mm, m)
                A(Wh[:, :, :], E[:, :, :], ACT.Copy).then_inc(W_hi, 1)

            def square_gated(g):
                act.wait_ge(yt_done, 2 * g + 2)
                act.wait_ge(yx, 2 * g + 2)
                act.wait_ge(xg_lo, g + 1)
                A(squared(g), zs[:, 4 * g:4 * g + 4, :].rearrange("p (a f) t -> p a (f t)", a=2), ACT.Square).then_inc(gate_sq, 1)

            def group_x(g):
                if g:
                    act.wait_ge(dg_mm, 2 * g)
                A(xgh[:, :, :], xtok[:, 2:4, GW * g:GW * g + GW], ACT.Copy).then_inc(xg_hi, 1)

            act.wait_ge(conv_ev, 20)
            mask(0, 0)
            weighed_hi(0)
            mask(0, 1)
            group_x(0)
            state_hi(0)
            next_state_hi(0)
            exps(0)
            weighed_hi(1)
            mask(1, 0)
            weights_hi(0)
            state_hi(1)
            next_state_hi(1)
            mask(1, 1)
            mask(2, 0)
            weighed_hi(2)
            exps(1)
            for m in range(8):
                if m < 6:
                    state_hi(m + 2)
                    mask(m + 2, 1)
                    next_state_hi(m + 2)
                if m < 5:
                    weighed_hi(m + 3)
                if m < 7:
                    weights_hi(m + 1)
                if m in (1, 3, 5):
                    group_x(m // 2 + 1)
                if m < 5:
                    mask(m + 3, 0)
                if m < 6:
                    exps(m + 2)
                if m in (2, 4, 6):
                    square_gated(m // 2 - 1)
            square_gated(3)
            lat = [(0, 0, LAT)]
            rms(5, LAT, INNER)
            his_shared(5, lat, lambda k, c0, c1: Hyh[:, k, :], lambda k, m: par[:, PAR["ssd_norm"] + k:PAR["ssd_norm"] + k + 1], None)
            xlat = [(0, CTX, TOK)]
            for m in range(8):
                for r in range(2):
                    hi(SO + 2 * m + r + RING, SO + 2 * m + r + RING)
                squares(6, m, 16, CTX)
            rms(6, LAT, D)
            his_shared(6, xlat, lambda k, c0, c1: H2h[:, k, :], lambda k, m: gain[3][:, k, m:m + 1], lambda k, m: mod[1][:, 24 + k, m:m + 1])
            with act.Fori(0, KH // 2) as i:
                for u in range(2):
                    hidden(2 * i + u, KH + 2 * i + u, u, LAT, U1h, F1 + 4 * i + 2 * u, F1 + 2 * u, 0)
            for m in range(8):
                for r in range(3):
                    hi(G1 + 3 * m + r + RING, G1 + 3 * m + r + RING)
                squares(7, m, 24, CTX)
            rms(7, LAT, D)

        @block.vector
        def _(dve):
            V = nc.vector

            def lo(n, s):
                if isinstance(n, int) and n >= NBLK:
                    return
                dve.wait_ge(w_hi, n + 1)
                c = COLS[s]
                V.tensor_tensor(wl[s % RING][:, 0:c], raw[s % RING][:, 0:c], wh[s % RING][:, 0:c].bitcast(f32), SUB).then_inc(w_lo, 1)

            def norm(w, src, nk, groups, gn, hdst, ldst, shift, between=lambda k: None):
                b = NB[w]
                t0, t1 = groups[0][1], groups[-1][2]
                dve.wait_ge(root, w + 1)
                V.reciprocal(T[:, 5, 0:t1 - t0], T[:, 4, 0:t1 - t0]).then_inc(inv, 1)
                dve.wait_ge(inv, w + 1)

                shared = w in SHARED
                slot = (lambda k: 2 + k // 2 % 2) if shared else (lambda k: 2 + k % 2)

                def value(k):
                    if k >= (4 if shared else 2):
                        dve.wait_ge(nlo, b + k - (3 if shared else 1))
                    for m, c0, c1 in groups:
                        ins = V.scalar_tensor_tensor(T[:, slot(k), c0 - t0:c1 - t0], src(k, c0, c1), gn(k, m),
                                                     T[:, 5, c0 - t0:c1 - t0], MUL, MUL)
                    ins.then_inc(nv, 2 if shared else 1)

                def low(k):
                    dve.wait_ge(nhi, b + k + 1)
                    if shared and k % 2:
                        V.tensor_tensor(ldst(k, t0, t1), T[:, 6 + k // 2 % 2, 0:t1 - t0], hdst(k, t0, t1).bitcast(f32), SUB).then_inc(nlo, 1)
                        return
                    for m, c0, c1 in groups:
                        v, h = T[:, slot(k), c0 - t0:c1 - t0], hdst(k, c0, c1).bitcast(f32)
                        if shift is None:
                            ins = V.tensor_tensor(ldst(k, c0, c1), v, h, SUB)
                        else:
                            ins = V.scalar_tensor_tensor(ldst(k, c0, c1), v, shift(k, m), h, ADD, SUB)
                    ins.then_inc(nlo, 1)

                if shared:
                    value(0)
                    for k in range(0, nk, 2):
                        if k + 2 < nk:
                            value(k + 2)
                        low(k)
                        low(k + 1)
                    return
                between(-1)
                value(0)
                for k in range(1, nk):
                    between(k - 1)
                    value(k)
                    low(k - 1)
                between(nk - 1)
                low(nk - 1)

            def ada_rows(q, used, acc):
                dve.wait_ge(w_used, used)
                if late(q, 1):
                    dve.wait_ge(row_tr, q)
                V.tensor_copy(mrow[0:4, :], acc[0:4, 0:256]).then_inc(row_cp, 1)

            def ada_out(q, layer, it):
                dve.wait_ge(row_tr, q + 1)
                V.tensor_reduce(mod[layer][:, ds(2 * it, 2), :].rearrange("p t s -> p (t s)"),
                                bank[7][:, 256:264].rearrange("p (m h) -> p m h", h=2), AX.X, ADD).then_inc(mod_ev, 1)

            def bias(layer, t0, t1, items):
                dve.wait_ge(mod_ev, items)
                ab = par[:, PAR["ada_b"] + 48 * layer + t0:PAR["ada_b"] + 48 * layer + t1]
                V.tensor_tensor(mod[layer][:, t0:t1, :], mod[layer][:, t0:t1, :],
                                ab.unsqueeze(2).to_broadcast([128, t1 - t0, 2]), ADD).then_inc(mod_done, 1)

            def gains(which, layer, chunk, name, k):
                dve.wait_ge(mod_done, k)
                g = par[:, PAR[name] + 8 * layer:PAR[name] + 8 * layer + 8]
                V.scalar_tensor_tensor(gain[which][:, :, :], mod[layer][:, 8 * chunk:8 * chunk + 8, :], 1.0,
                                       g.unsqueeze(2).to_broadcast([128, 8, 2]), ADD, MUL).then_inc(mod_done, 1)
                dve.wait_ge(mod_done, k + 1)

            dve.wait_ge(sc_hi, 1)
            V.tensor_tensor(smov[:, :, :, 1], sc[:, :, :].rearrange("p s k -> p k s"), smov[:, :, :, 0].bitcast(f32), SUB).then_inc(sc_lo, 1)
            for n in range(RING):
                lo(n, n)
            for q in range(8):
                for r in range(2):
                    lo(A0 + 2 * q + r + RING, A0 + 2 * q + r + RING)
                ada_rows(q, A0 + 2 * q + 2, bank[4 + q % 2])
                if q:
                    ada_out(q - 1, 0, q - 1)
            ada_out(7, 0, 7)
            bias(0, 0, 16, 8)
            gains(0, 0, 1, "norm_mix", 1)
            both = [(1, 0, CTX), (0, CTX, TOK)]
            dve.wait_ge(x_in, 16)
            norm(0, lambda k, c0, c1: X[:, k, c0:c1], 8, both, lambda k, m: gain[0][:, k, m:m + 1],
                 lambda k, c0, c1: Hmh[:, k, c0:c1], lambda k, c0, c1: Hml[:, k, c0:c1], lambda k, m: mod[0][:, k, m:m + 1])
            for t in range(7):
                lo(IN + t + RING, IN + t + RING)
                if t == 2:
                    dve.wait_ge(inputs_in, 32)
                    dve.wait_ge(proj_out, 3)
                    V.tensor_tensor(rtmp[64:96, :], bank[0][96:128, CTX:TOK], tab[96:128, TAB["sin"]:TAB["sin"] + LAT], MUL).then_inc(kr_part, 1)
                    V.tensor_tensor(kf[64:96, CTX:TOK], kf[64:96, CTX:TOK], tab[64:96, TAB["cos"]:TAB["cos"] + LAT], MUL).then_inc(kr_part, 1)
                    dve.wait_ge(kr_part, 2)
                    V.tensor_tensor(kf[64:96, CTX:TOK], kf[64:96, CTX:TOK], rtmp[64:96, :], ADD).then_inc(kr_done, 1)
                    dve.wait_ge(kr_hi, 1)
                    V.tensor_tensor(kl[64:96, :], kf[64:96, :], kh[64:96, :].bitcast(f32), SUB).then_inc(kr_lo, 1)
                if t == 3:
                    whole = [(0, 0, TOK)]
                    norm(1, lambda k, c0, c1: cq[:, k, c0:c1], KKV, whole, lambda k, m: par[:, PAR["kv_norm"] + k:PAR["kv_norm"] + k + 1],
                         lambda k, c0, c1: cnh[:, k, c0:c1], lambda k, c0, c1: cnl[:, k, c0:c1], None)
            def v_lo_part(g):
                dve.wait_ge(v_hi, g + 1)
                c = (slice(None), g // 2, slice(512 * (g % 2), 512 * (g % 2) + 512))
                V.tensor_tensor(vl[c], bank[2 + g % 4][:, :], vh[c].bitcast(f32), SUB).then_inc(v_lo, 1)

            def v_between(k):
                for g in ((2, 3) if k < 0 else (4 + k,)):
                    v_lo_part(g)

            v_lo_part(0)
            v_lo_part(1)
            norm(2, lambda k, c0, c1: cq[:, KKV + k, c0:c1], KQ, whole, lambda k, m: par[:, PAR["q_norm"] + k:PAR["q_norm"] + k + 1],
                 lambda k, c0, c1: cnh[:, KKV + k, c0:c1], lambda k, c0, c1: cnl[:, KKV + k, c0:c1], None, v_between)
            lo(VB + 4, VB + 4)
            lo(VB + 5, VB + 5)

            def project(i, n, s, between):
                dve.wait_ge(q_cp, i + 1)
                V.tensor_tensor(rtmp[64:96, :], bank[0][96:128, CTX:TOK], tab[96:128, TAB["sin"]:TAB["sin"] + LAT], MUL).then_inc(rope_part, 1)
                V.tensor_tensor(qf[64:96, CTX:TOK], qf[64:96, CTX:TOK], tab[64:96, TAB["cos"]:TAB["cos"] + LAT], MUL).then_inc(rope_part, 1)
                dve.wait_ge(rope_part, 2 * i + 2)
                V.tensor_tensor(qf[64:96, CTX:TOK], qf[64:96, CTX:TOK], rtmp[64:96, :], ADD).then_inc(q_rope, 1)
                dve.wait_ge(k_hi, i + 1)
                V.tensor_tensor(kl[0:64, :], bank[1][0:64, :], kh[0:64, :].bitcast(f32), SUB).then_inc(k_lo, 1)
                between()
                lo(n + 4, s + 4)
                lo(n + 5, s + 5)

            def maxes(i, p):
                dve.wait_ge(s_mm, 3 * i + p + 1)
                c = slice(p, p + 1) if p < 2 else slice(2, 4)
                if p < 2:
                    V.tensor_reduce(mx[:, c], bank[p][:, :], AX.X, ALU.max).then_inc(maxed, 1)
                else:
                    V.tensor_reduce(mx[:, c], bank[4][:, :].rearrange("p (a k) -> p a k", a=2), AX.X, ALU.max).then_inc(maxed, 1)
                dve.wait_ge(maxed, 3 * i + p + 1)
                V.tensor_scalar(nm[:, c], mx[:, c], -(float(QKD) ** -0.5), None, MUL).then_inc(nmax, 1)

            def inverse(i, p):
                dve.wait_ge(exp_done, 4 * i + (1, 2, 4)[p])
                if late(i, 1):
                    dve.wait_ge(p_norm, 3 * i - 2 + p)
                c = slice(p, p + 1) if p < 2 else slice(2, 4)
                V.reciprocal(rs_[:, c], ssum[:, c]).then_inc(rcp, 1)

            def pt_split(i, p):
                dve.wait_ge(pt_hi, 3 * i + p + 1)
                b = bank[PT_BANK[p]]
                if p < 2:
                    k, q, src = slice(0, 4), slice(128 * p, 128 * p + 128), b[:, :].rearrange("p (k q) -> p k q", q=128)
                else:
                    k, q, src = slice(4, 6), slice(0, 256), b[:, :].rearrange("p (k q) -> p k q", q=256)
                V.tensor_tensor(PTl[:, k, q], src, PTh[:, k, q].bitcast(f32), SUB).then_inc(pt_lo, 1)

            def head(i, j, u):
                n, s = HL + 4 * i, HL + 4 * (i if isinstance(i, int) else u)
                more = not isinstance(i, int) or i < 15
                if more:
                    project(i + 1, n, s, lambda: pt_split(i, 0))
                    n, s = n + 2, s + 2
                else:
                    pt_split(i, 0)
                pt_split(i, 1)
                pt_split(i, 2)
                ada_rows(8 + i, n + 2, bank[7])
                if more:
                    maxes(i + 1, 0)
                lo(n + 4, s + 4)
                if more:
                    maxes(i + 1, 1)
                    inverse(i + 1, 0)
                    maxes(i + 1, 2)
                    inverse(i + 1, 1)
                    inverse(i + 1, 2)
                lo(n + 5, s + 5)
                ada_out(8 + i, 0, 8 + i)
                dve.wait_ge(o_hi, i + 1)
                o = (slice(64 * u, 64 * u + 64), ds(j, 1), slice(None))
                V.tensor_tensor(Ol[o].rearrange("p o t -> p (o t)"), bank[3][0:64, :],
                                Oh[o].rearrange("p o t -> p (o t)").bitcast(f32), SUB).then_inc(o_lo, 1)

            project(0, HP, HP, lambda: None)
            for p in range(3):
                maxes(0, p)
                inverse(0, p)
            head(0, 0, 0)
            head(1, 0, 1)
            with dve.Fori(1, 7) as j:
                head(2 * j, j, 0)
                head(2 * j + 1, j, 1)
            head(14, 7, 0)
            head(15, 7, 1)
            bias(0, 16, 48, 24)
            gains(1, 0, 4, "norm_ffn", 3)

            def add(used, m, u, layer, chunk, groups):
                dve.wait_ge(w_used, used)
                for src, c0, c1 in groups:
                    x = X[:, ds(m, 1), c0:c1].rearrange("p o t -> p (o t)")
                    b0 = c0 - groups[0][1]
                    ins = V.scalar_tensor_tensor(x, bank[u][:, b0:b0 + c1 - c0],
                                                 mod[layer][:, ds(8 * chunk + m, 1), src], x, MUL, ADD)
                ins.then_inc(added, 1)

            for m in range(8):
                add(WO + m + 1, m, m % 2, 0, 2, both)
                lo(WO + m + RING, WO + m + RING)
            dve.wait_ge(added, 8)
            norm(3, lambda k, c0, c1: X[:, k, c0:c1], 8, both, lambda k, m: gain[1][:, k, m:m + 1],
                 lambda k, c0, c1: H0h[:, k, c0:c1], lambda k, c0, c1: H0l[:, k, c0:c1], lambda k, m: mod[0][:, 24 + k, m:m + 1])

            def hidden(j, g, u, nt, Uh, Ul, n, s, splits):
                if splits and late(j, 1):
                    ada_rows(23 + j, n, bank[7])
                lo(n + 4, s + 4)
                if splits and late(j, 1):
                    ada_out(23 + j, 1, j - 1)
                dve.wait_ge(w_used, n + 2)
                dve.wait_ge(silu_done, g + 1)
                if late(g, 2):
                    dve.wait_ge(hid_lo, g - 1)
                V.tensor_tensor(T[:, 2 + u, 0:nt], bank[3 + 2 * u][:, 0:nt], T[:, u, 0:nt], MUL).then_inc(hid_f, 1)
                lo(n + 5, s + 5)
                dve.wait_ge(hid_hi, g + 1)
                V.tensor_tensor(Ul[:, ds(j, 1), :].rearrange("p o t -> p (o t)"), T[:, 2 + u, 0:nt],
                                Uh[:, ds(j, 1), :].rearrange("p o t -> p (o t)").bitcast(f32), SUB).then_inc(hid_lo, 1)
                for r in range(6, splits):
                    lo(n + r, s + r)

            for j in range(2):
                hidden(j, j, j % 2, TOK, U0h, U0l, F0 + 4 * j, F0 + 4 * j, 8)
            with dve.Fori(1, KH // 2) as i:
                for u in range(2):
                    hidden(2 * i + u, 2 * i + u, u, TOK, U0h, U0l, F0 + 8 * i + 4 * u, F0 + 4 * u, 8)
            for m in range(8):
                q = 45 + m
                if q < 48:
                    ada_rows(q, g0(m), bank[7])
                for n in range(g0(m), g0(m + 1)):
                    if n == g0(m) + 2:
                        add(g0(m) + 3, m, m % 2, 0, 5, both)
                    lo(n + RING, n + RING)
                    if n == g0(m) + 1 and q < 48:
                        ada_out(q, 1, q - 24)
                if q == 47:
                    bias(1, 0, 48, 48)
                    gains(2, 1, 1, "norm_mix", 5)
                    gains(3, 1, 4, "norm_ffn", 6)
            dve.wait_ge(added, 16)

            norm(4, lambda k, c0, c1: X[:, k, c0:c1], 8, both, lambda k, m: gain[2][:, k, m:m + 1],
                 lambda k, c0, c1: H1h[:, k, c0:c1], lambda k, c0, c1: H1l[:, k, c0:c1], lambda k, m: mod[1][:, k, m:m + 1])

            def conv(t, n, s, u, kind):
                seg = slice(1, 2) if kind == "C" else slice(0, 2)
                acc = T[:, u, :].rearrange("p (s t) -> p s t", s=2)[:, seg, :]
                dve.wait_ge(conv_init, t + 1)
                for r in range(1, 5):
                    if r > 1:
                        dve.wait_ge(conv_tap, 4 * t + r - 1)
                    V.scalar_tensor_tensor(acc, up[:, u, seg, r:r + 256], par[:, ds(PAR["conv_w"] + 5 * t + r, 1)],
                                           acc, MUL, ADD).then_inc(conv_tap, 1)
                lo(n + 4, s + 4)
                if kind in "BC":
                    g, h, l = t % 4, (BTh if kind == "B" else CTh), (BTl if kind == "B" else CTl)
                    dve.wait_ge(ct_hi, t + 1)
                    V.tensor_tensor(l[:, g, :], T[:, 2 + u, 256:512], h[:, g, :].bitcast(f32), SUB).then_inc(ct_lo, 1)

            def to_tokens(t, u):
                dve.wait_ge(conv_tr, t - 3)
                V.tensor_copy(xtok[:, :, ds(128 * (t - 8), 128)], bank[2 + u][:, :].rearrange("p (t n) -> p t n", n=128)).then_inc(conv_ev, 1)

            for t in range(8):
                conv(t, BC + t, BC + t, t % 2, "BC"[t // 4])
                if 1 <= t <= 4:
                    dve.wait_ge(conv_hi, t)
                    V.tensor_tensor(Btl[:, :, t - 1, :], bank[3 - t % 2][:, :].rearrange("p (t n) -> p t n", n=128),
                                    Bth[:, :, t - 1, :].bitcast(f32), SUB).then_inc(conv_ev, 1)
            lo(DT + RING, DT + RING)
            W = dtw
            conv(8, XS, XS, 0, "x")
            dve.wait_ge(dt_tr, 1)
            V.tensor_tensor(W[:, 0, :].rearrange("p (t h) -> p t h", t=4), bank[5][:, 0:256].rearrange("p (t h) -> p t h", t=4),
                            rows[:, 0:64].unsqueeze(1).to_broadcast([128, 4, 64]), ADD).then_inc(dt_dve, 1)
            dve.wait_ge(dt_dve, 1)
            V.scalar_tensor_tensor(W[:, 1, :], W[:, 0, :], -1.0, W[:, 0, :], MUL, ALU.max).then_inc(dt_dve, 1)
            conv(9, XS + 1, XS + 1, 1, "x")
            dve.wait_ge(dt_act, 1)
            V.tensor_scalar(W[:, 3, :], W[:, 2, :], 1.0, None, ADD).then_inc(dt_dve, 1)
            dve.wait_ge(dt_dve, 3)
            V.tensor_scalar(W[:, 5, :], W[:, 3, :], -1.0, None, ADD).then_inc(dt_dve, 1)
            dve.wait_ge(dt_dve, 4)
            V.tensor_scalar(W[:, 1, :], W[:, 5, :], 0.0, None, ALU.is_equal).then_inc(dt_dve, 1)
            dve.wait_ge(dt_dve, 5)
            V.tensor_tensor(W[:, 5, :], W[:, 5, :], W[:, 1, :], ADD).then_inc(dt_dve, 1)
            conv(10, XS + 2, XS + 2, 0, "x")
            to_tokens(8, 0)
            dve.wait_ge(dt_act, 3)
            V.tensor_tensor(W[:, 4, :], W[:, 4, :], W[:, 1, :], ADD).then_inc(dt_dve, 1)
            dve.wait_ge(dt_dve, 7)
            V.reciprocal(W[:, 5, :], W[:, 5, :]).then_inc(dt_dve, 1)
            dve.wait_ge(dt_dve, 8)
            V.tensor_tensor(W[:, 4, :], W[:, 4, :], W[:, 5, :], MUL).then_inc(dt_dve, 1)
            dve.wait_ge(dt_dve, 9)
            V.tensor_tensor(W[:, 4, :], W[:, 4, :], W[:, 2, :], MUL).then_inc(dt_dve, 1)
            dve.wait_ge(dt_dve, 10)
            V.scalar_tensor_tensor(dt[:, :, :].rearrange("p t h -> p (t h)"), W[:, 0, :], 0.0, W[:, 4, :], ALU.max, ADD).then_inc(dt_dve, 1)
            dve.wait_ge(dt_dve, 11)
            V.scalar_tensor_tensor(dtA[:, :, :], dt[:, :, :], -1.0, rows[:, 64:128].unsqueeze(1).to_broadcast([128, 4, 64]), MUL, MUL).then_inc(dt_dve, 1)
            dve.wait_ge(dt_dve, 12)
            V.tensor_copy(maskr[:, 0, :], tabv("gt")).then_inc(masks_r, 1)
            V.tensor_copy(maskr[:, 1, :], tabv("lt")).then_inc(masks_r, 1)
            V.tensor_copy(dtAh[:, :, :].bitcast(f32r), dtA[:, 2:4, :]).then_inc(dta_hi, 1)
            dve.wait_ge(dta_hi, 1)
            V.tensor_tensor(dtAl[:, :, :].bitcast(f32r), dtA[:, 2:4, :], dtAh[:, :, :], SUB).then_inc(dta_hi, 1)

            conv(11, XS + 3, XS + 3, 1, "x")
            to_tokens(9, 1)
            with dve.Fori(1, 4) as i:
                for u in range(4):
                    conv(8 + 4 * i + u, XS + 4 * i + u, XS + u, u % 2, "x")
                    to_tokens(6 + 4 * i + u, u % 2)
            to_tokens(22, 0)
            to_tokens(23, 1)
            dve.wait_ge(cum_exp, 1)
            V.tensor_tensor(w6[:, 0:4, :].rearrange("p s h -> p (s h)"), et[:, 0:128], dt[:, 0:2, :].rearrange("p t h -> p (t h)"), MUL).then_inc(w6_done, 1)
            V.tensor_tensor(w6[:, 4, :], et[:, 128:160], dt[:, 2, 0:32], MUL).then_inc(w6_done, 1)
            V.tensor_tensor(w6[:, 5, :], et[:, 160:192], dt[:, 3, 32:64], MUL).then_inc(w6_done, 1)

            dve.wait_ge(cb_mm, 2)
            for c in range(2):
                for dst, name in ((cbf, "le"), (cbb, "ge")):
                    V.tensor_tensor(dst[:, 4 * c:4 * c + 4, :], bank[CB_BANK[c]][:, :].rearrange("p (g q) -> p g q", q=128),
                                    tabv(name).unsqueeze(1).to_broadcast([128, GROUPS, 128]), MUL).then_inc(cb_done, 1)
            dve.wait_ge(cb_done, 4)

            def heads64(ap):
                return ap.rearrange("p (h d) -> p h d", d=64)

            def per_head(ap):
                return ap.unsqueeze(2).to_broadcast([128, GH, 64])

            def weighed_lo(e):
                for i in range(3 * e, 3 * e + 3):
                    dve.wait_ge(xs_hi, i + 1)
                    V.tensor_tensor(xsl[:, i % 3, :], xsf[i % 3], xsh[:, i % 3, :].bitcast(f32), SUB).then_inc(xs_lo, 1)

            def states(e):
                g, d_ = divmod(e, 2)
                dve.wait_ge(st_hi, 2 * e + 1)
                V.tensor_tensor(hl[:, 0, :], bank[0][:, :], hh[:, 0, :].bitcast(f32), SUB).then_inc(st_lo, 1)
                dtot = et[:, 320 + 32 * d_ + GH * g:320 + 32 * d_ + GH * g + GH]
                if e:
                    dve.wait_ge(st_lo, 2 * e)
                if e >= 2:
                    dve.wait_ge(y_off, 2 * (e // 2))
                V.tensor_tensor(heads64(T[:, 6, :]), heads64(bank[0][:, :]), per_head(dtot), MUL).then_inc(st_dec, 1)
                dve.wait_ge(st_dec, e + 1)
                V.tensor_tensor(T[:, 6, :], T[:, 6, :], bank[1][:, :], ADD).then_inc(st_sum, 1)

            def next_state_lo(e):
                dve.wait_ge(st_hi, 2 * e + 2)
                V.tensor_tensor(hl[:, 1, :], T[:, 6, :], hh[:, 1, :].bitcast(f32), SUB).then_inc(st_lo, 1)

            def carried(e):
                g, d_ = divmod(e, 2)
                for z in range(2):
                    c = z if d_ == 0 else 1 - z
                    dve.wait_ge(off_mm, 2 * e + z + 1)
                    ec = per_head(et[:, 192 + 64 * c + 32 * d_ + GH * g:192 + 64 * c + 32 * d_ + GH * g + GH])
                    y, src = Y[:, 2 * (g % 2) + c, :], heads64(bank[2 + z][:, :])
                    if d_ == 0:
                        if g >= 2:
                            dve.wait_ge(yt_mm, 2 * g - 2)
                        V.tensor_tensor(heads64(y), src, ec, MUL).then_inc(off_rd, 1)
                    else:
                        dve.wait_ge(st_lo, 2 * e + 2)
                        if 2 * g + z >= 1:
                            dve.wait_ge(y_off, 2 * g + z)
                        V.tensor_tensor(heads64(T[:, 6, :]), src, ec, MUL).then_inc(off_rd, 1)
                        dve.wait_ge(off_rd, 2 * e + z + 1)
                        V.tensor_tensor(y, y, T[:, 6, :], ADD).then_inc(y_off, 1)

            def undecayed(m):
                g, c = divmod(m, 2)
                dve.wait_ge(gb, m + 1)
                if m >= 1:
                    dve.wait_ge(wf, m)
                for h in range(GH):
                    q = slice(128 * (h % 4), 128 * (h % 4) + 128)
                    last = V.scalar_tensor_tensor(T[:, 2 + h // 4, q], cbf[:, 4 * c + g, :], dt[:, 2 + c, GH * g + h:GH * g + h + 1],
                                                  T[:, 4 + h // 4, q], MUL, ADD)
                last.then_inc(gd, 1)

            def decayed(m):
                dve.wait_ge(gd, m + 1)
                dve.wait_ge(dec_exp, 2 * m + 2)
                V.tensor_tensor(E[:, :, :], E[:, :, :], T[:, 2:4, :].rearrange("p a (h q) -> p (a h) q", q=128), MUL).then_inc(wf, 1)

            def weights_lo(m):
                dve.wait_ge(W_hi, m + 1)
                V.tensor_tensor(Wl[:, :, :], E[:, :, :], Wh[:, :, :].bitcast(f32), SUB).then_inc(W_lo, 1)

            def group_x(g):
                dve.wait_ge(xg_hi, g + 1)
                V.tensor_tensor(xgl[:, :, :], xtok[:, 2:4, GW * g:GW * g + GW], xgh[:, :, :].bitcast(f32), SUB).then_inc(xg_lo, 1)

            def add_diagonal(m):
                g, c = divmod(m, 2)
                y = Y[:, 2 * (g % 2) + c, :]
                dve.wait_ge(yx, m + 1)
                dve.wait_ge(dg_mm, m + 1)
                V.tensor_tensor(y, y, bank[4][:, :], ADD).then_inc(y_done, 1)

            def gate(m):
                g, c = divmod(m, 2)
                dve.wait_ge(yt_mm, m + 1)
                z = zs[:, 4 * g:4 * g + 4, 128 * c:128 * c + 128]
                V.tensor_tensor(z, bank[5][:, :].rearrange("p (f q) -> p f q", q=128), z, MUL).then_inc(yt_done, 1)

            undecayed(0)
            with dve.Fori(0, 4) as i:
                for u in range(4):
                    lo(ZS + 4 * i + u + 4, ZS + u + 4)
            weighed_lo(0)
            group_x(0)
            states(0)
            next_state_lo(0)
            decayed(0)
            weighed_lo(1)
            carried(0)
            weights_lo(0)
            states(1)
            next_state_lo(1)
            undecayed(1)
            carried(1)
            weighed_lo(2)
            for m in range(8):
                if m < 7:
                    decayed(m + 1)
                if m < 6:
                    states(m + 2)
                    undecayed(m + 2)
                    next_state_lo(m + 2)
                add_diagonal(m)
                if m < 5:
                    weighed_lo(m + 3)
                if m < 7:
                    weights_lo(m + 1)
                if m in (1, 3, 5):
                    group_x(m // 2 + 1)
                gate(m)
                if m < 6:
                    carried(m + 2)
            lat = [(0, 0, LAT)]
            dve.wait_ge(yt_done, 8)
            norm(5, lambda k, c0, c1: zs[:, k, :], KI, lat, lambda k, m: par[:, PAR["ssd_norm"] + k:PAR["ssd_norm"] + k + 1],
                 lambda k, c0, c1: Hyh[:, k, :], lambda k, c0, c1: Hyl[:, k, :], None)
            xlat = [(0, CTX, TOK)]
            with dve.Fori(0, 4) as i:
                for u in range(2):
                    lo(SO + 4 * i + 2 * u + 4, SO + 2 * u + 4)
                    add(SO + 4 * i + 2 * u + 2, 2 * i + u, u, 1, 2, xlat)
                    lo(SO + 4 * i + 2 * u + 5, SO + 2 * u + 5)
            dve.wait_ge(added, 24)
            norm(6, lambda k, c0, c1: X[:, k, c0:c1], 8, xlat, lambda k, m: gain[3][:, k, m:m + 1],
                 lambda k, c0, c1: H2h[:, k, :], lambda k, c0, c1: H2l[:, k, :], lambda k, m: mod[1][:, 24 + k, m:m + 1])
            with dve.Fori(0, KH // 2) as i:
                for u in range(2):
                    hidden(2 * i + u, KH + 2 * i + u, u, LAT, U1h, U1l, F1 + 4 * i + 2 * u, F1 + 2 * u, 0)
            for m in range(8):
                lo(G1 + 3 * m + RING, G1 + 3 * m + RING)
                lo(G1 + 3 * m + 1 + RING, G1 + 3 * m + 1 + RING)
                add(G1 + 3 * m + 3, m, m % 2, 1, 5, xlat)
                lo(G1 + 3 * m + 2 + RING, G1 + 3 * m + 2 + RING)
            dve.wait_ge(added, 32)
            dve.wait_ge(root, 8)
            V.reciprocal(T[:, 5, 0:LAT], T[:, 4, 0:LAT]).then_inc(inv, 1)
            dve.wait_ge(inv, 8)
            for k in range(KD):
                V.scalar_tensor_tensor(yout[:, k, :], X[:, k, CTX:TOK], par[:, PAR["final"] + k:PAR["final"] + k + 1],
                                       T[:, 5, 0:LAT], MUL, MUL).then_inc(out_done, 1)

        @block.tensor
        def _(pe):
            mm = nc.tensor.matmul

            def three(o, lh, ll, rh, rl, first, final):
                mm(o, lh, rl, start=first, stop=False)
                mm(o, lh, rh, start=False, stop=False)
                return mm(o, ll, rh, start=False, stop=final)

            def tile(n, s, o, h, l, k0, nk, first, final, mid=None):
                pe.wait_ge(w_lo, n + 1)
                for k in range(nk):
                    w = slice(128 * k, 128 * k + 128)
                    last = three(o, wh[s % RING][:, w], wl[s % RING][:, w], h(k0 + k), l(k0 + k),
                                 first and k == 0, final and k == nk - 1)
                    if k == 3 and mid is not None:
                        mid()
                return last

            def pair(n, outs, h, l, nk, per, base):
                pe.wait_ge(w_lo, n + 2 * per)
                for k in range(nk):
                    pe.wait_ge(nlo, base + k + 1)
                    r, w = divmod(k, 8)
                    w = slice(128 * w, 128 * w + 128)
                    for i, o in enumerate(outs):
                        sl = (n + per * i + r) % RING
                        last = three(o, wh[sl][:, w], wl[sl][:, w], h(k), l(k), k == 0, k == nk - 1)
                        if k == nk - 1 and i == 0:
                            last.then_inc(w_used, per)
                last.then_inc(w_used, per)

            def ada(n, s, q, acc):
                if late(q, 8):
                    pe.wait_ge(mod_ev, q)
                elif q >= 2:
                    pe.wait_ge(row_cp, q - 1)
                for r in range(2):
                    pe.wait_ge(w_lo, n + r + 1)
                    for k in range(4):
                        lhs = smov[:, 4 * r + k, :, :].rearrange("p s h -> p (s h)")
                        w, sl = slice(256 * k, 256 * k + 256), (s + r) % RING
                        mm(acc[0:4, 0:256], lhs, wh[sl][:, w], start=r + k == 0, stop=False)
                        last = mm(acc[0:4, 0:256], lhs, wl[sl][:, w], start=False, stop=r == 1 and k == 3)
                    last.then_inc(w_used, 1)

            def turn_ready(q):
                pe.wait_ge(row_cp, q + 1)
                if late(q, 1):
                    pe.wait_ge(mod_ev, q)

            def turn(q):
                for t in range(2):
                    last = nc.tensor.transpose(bank[7][:, 256 + 4 * t:260 + 4 * t], mrow[0:4, 128 * t:128 * t + 128], tab[0:4, 0:4])
                last.then_inc(row_tr, 1)

            def norm_sum(w, n):
                b, K = SQ[w], NORM_K[w]
                pe.wait_ge(root, w)
                pe.wait_ge(sq_used, b + K - 1 - USED[w])
                mm(bank[NORM_BANK[w]][:, 0:n], ones[:, :], T[:, 6, 0:n], start=True, stop=False)
                pe.wait_ge(sq_ready, b + K)
                mm(bank[NORM_BANK[w]][:, 0:n], ones[:, :], T[:, (b + K - 1) % 2, 0:n], start=False, stop=True).then_inc(sum_done, 1)

            pe.wait_ge(sc_lo, 1)
            for q in range(8):
                if q == 7:
                    pe.wait_ge(x_acc, KD)
                    mm(bank[6][:, :], ones[:, :], T[:, 6, :], start=True, stop=True).then_inc(sum_done, 1)
                ada(A0 + 2 * q, A0 + 2 * q, q, bank[4 + q % 2])
                if q == 1:
                    pe.wait_ge(inputs_in, 32)
                    pe.wait_ge(ones_set, 2)
                if q >= 1:
                    turn_ready(q - 1)
                    turn(q - 1)
            turn_ready(7)
            turn(7)
            pair(IN, (bank[0][:, :], bank[1][:, :]), lambda k: Hmh[:, k, :], lambda k: Hml[:, k, :], KD, 1, NB[0])
            for t in range(1, 7):
                if t >= 2:
                    pe.wait_ge(proj_out, t - 1)
                if t == 2:
                    pe.wait_ge(mod_ev, 8)
                if t == 4:
                    pe.wait_ge(kr_part, 1)
                if t >= 2:
                    tile(IN + t, IN + t, bank[t % 2][:, :], lambda k: Hmh[:, k, :], lambda k: Hml[:, k, :], 0, 8,
                         True, True).then_inc(w_used, 1)
                if t in (1, 2):
                    if t == 1:
                        pe.wait_ge(root, 1)
                    pe.wait_ge(sq_ready, t)
                    last = mm(bank[7][:, :], ones[:, :], T[:, t - 1, :], start=t == 1, stop=t == 2)
                    last.then_inc(sum_done if t == 2 else sq_used, 1)
            pe.wait_ge(w_lo, VB + 2)
            pe.wait_ge(nlo, NB[2])
            for g in range(8):
                if g >= 4:
                    pe.wait_ge(v_lo, g - 3)
                tk, c = slice(128 * (g // 2), 128 * (g // 2) + 128), slice(512 * (g % 2), 512 * (g % 2) + 512)
                for k in range(KKV):
                    sl = (VB + k) % RING
                    last = three(bank[2 + g % 4][:, :], cnh[:, k, tk], cnl[:, k, tk], wh[sl][:, c], wl[sl][:, c], k == 0, k == KKV - 1)
                    if g == 7:
                        last.then_inc(w_used, 1)
                if g < 7:
                    last.then_inc(v_mm, 1)
                if g == 0:
                    norm_sum(2, TOK)

            def project(i, n, s):
                if late(i, 1):
                    pe.wait_ge(exp_done, 4 * i - 3)
                else:
                    pe.wait_ge(nlo, NB[3])
                tile(n, s, bank[0][:, :], lambda k: cnh[:, KKV + k, :], lambda k: cnl[:, KKV + k, :], 0, KQ, True, True).then_inc(w_used, 1)
                pe.wait_ge(w_lo, n + 2)
                if late(i, 1):
                    pe.wait_ge(exp_done, 4 * i - 2)
                s1 = (s + 1) % RING
                for k in range(KKV):
                    w = slice(64 * k, 64 * k + 64)
                    last = three(bank[1][0:64, :], wh[s1][:, w], wl[s1][:, w], cnh[:, k, :], cnl[:, k, :], k == 0, k == KKV - 1)
                last.then_inc(w_used, 1)

            def scores(i, p):
                if p == 0:
                    pe.wait_ge(q_lo, i + 1)
                    pe.wait_ge(k_lo, i + 1)
                if p < 2:
                    q = slice(CTX + 128 * p, CTX + 128 * p + 128)
                    last = three(bank[p][:, :], qh[0:QKD, q], ql[0:QKD, q], kh[0:QKD, :], kl[0:QKD, :], True, True)
                else:
                    if late(i, 1):
                        pe.wait_ge(exp_done, 4 * i)
                    for t in range(2):
                        q = slice(128 * t, 128 * t + 128)
                        last = three(bank[4][:, 256 * t:256 * t + 256], qh[0:QKD, q], ql[0:QKD, q],
                                     kh[0:QKD, 0:CTX], kl[0:QKD, 0:CTX], True, True)
                last.then_inc(s_mm, 1)

            def transpose_probs(i, p):
                pe.wait_ge(p_norm, 3 * i + p + 1)
                if late(i, 1):
                    pe.wait_ge(pt_lo, 3 * i - 2 + p)
                b = bank[PT_BANK[p]]
                if p < 2:
                    for k in range(4):
                        last = nc.tensor.transpose(b[:, 128 * k:128 * k + 128], P[:, p, 128 * k:128 * k + 128], tabv("ident"))
                else:
                    for k in range(2):
                        for t in range(2):
                            last = nc.tensor.transpose(b[:, 256 * k + 128 * t:256 * k + 128 * t + 128],
                                                       P[:, 2, 256 * t + 128 * k:256 * t + 128 * k + 128], tabv("ident"))
                last.then_inc(pt_mm, 1)

            def values(i, u):
                pe.wait_ge(pt_lo, 3 * i + 3)
                pe.wait_ge(v_cp, i + 1)
                if late(i, 1):
                    pe.wait_ge(o_lo, i)
                for k in range(4):
                    three(bank[3][0:64, CTX:TOK], vsh[:, u, k, :], vsl[:, u, k, :], PTh[:, k, :], PTl[:, k, :], k == 0, k == 3)
                for k in range(2):
                    last = three(bank[3][0:64, 0:CTX], vsh[:, u, k, :], vsl[:, u, k, :], PTh[:, 4 + k, :], PTl[:, 4 + k, :], k == 0, k == 1)
                last.then_inc(o_mm, 1)

            def head(i, u):
                n, s = HL + 4 * i, HL + 4 * (i if isinstance(i, int) else u)
                more = not isinstance(i, int) or i < 15
                if more:
                    project(i + 1, n, s)
                    n, s = n + 2, s + 2
                for p in range(3):
                    transpose_probs(i, p)
                ada(n, s, 8 + i, bank[7])
                if more:
                    scores(i + 1, 0)
                    scores(i + 1, 1)
                turn_ready(8 + i)
                if more:
                    scores(i + 1, 2)
                turn(8 + i)
                values(i, u)

            project(0, HP, HP)
            pe.wait_ge(kr_lo, 1)
            for p in range(3):
                scores(0, p)
            head(0, 0)
            head(1, 1)
            with pe.Fori(1, 7) as j:
                head(2 * j, 0)
                head(2 * j + 1, 1)
            head(14, 0)
            head(15, 1)

            pe.wait_ge(o_lo, HEADS)
            for m in range(8):
                if m >= 2:
                    pe.wait_ge(added, m - 1)
                tile(WO + m, WO + m, bank[m % 2][:, :], lambda k: Oh[:, k, :], lambda k: Ol[:, k, :], 0, 8, True, True).then_inc(w_used, 1)
            norm_sum(3, TOK)

            def ffn(j, g, u, nt, h, l, n, s, kwait):
                if kwait is not None:
                    for b, count in ((silu_done, g - 1), (hid_f, g - 1)):
                        if g >= 2:
                            pe.wait_ge(b, count)
                    pair(n, (bank[2 + 2 * u][:, 0:nt], bank[3 + 2 * u][:, 0:nt]), h, l, KD, 1, kwait)
                    return
                if late(g, 2):
                    pe.wait_ge(silu_done, g - 1)
                tile(n, s, bank[2 + 2 * u][:, 0:nt], h, l, 0, 8, True, True).then_inc(w_used, 1)
                if nt == TOK and late(j, 1):
                    turn_ready(23 + j)
                if late(g, 2):
                    pe.wait_ge(hid_f, g - 1)
                mid = (lambda: turn(23 + j)) if nt == TOK and late(j, 1) else None
                tile(n + 1, s + 1, bank[3 + 2 * u][:, 0:nt], h, l, 0, 8, True, True, mid).then_inc(w_used, 1)

            h0 = (lambda k: H0h[:, k, :]), (lambda k: H0l[:, k, :])
            for j in range(2):
                ffn(j, j, j % 2, TOK, *h0, F0 + 4 * j, F0 + 4 * j, NB[3] if j == 0 else None)
                ada(F0 + 4 * j + 2, F0 + 4 * j + 2, 24 + j, bank[7])
            with pe.Fori(1, KH // 2) as i:
                for u in range(2):
                    n, s = F0 + 8 * i + 4 * u, F0 + 4 * u
                    ffn(2 * i + u, 2 * i + u, u, TOK, *h0, n, s, None)
                    ada(n + 2, s + 2, 24 + 2 * i + u, bank[7])

            def w2(q0, m, n, nt, h, l):
                pe.wait_ge(added, q0 + m - 1)
                for r, (k0, nk) in enumerate(((0, 8), (8, 8), (16, KH - 16))):
                    tile(n + r, n + r, bank[m % 2][:, 0:nt], h, l, k0, nk, r == 0, r == 2).then_inc(w_used, 1)
                    if r == 1 and nt == TOK and m < 3:
                        turn_ready(45 + m)
                        turn(45 + m)

            pe.wait_ge(hid_lo, KH)
            for m in range(8):
                w2(8, m, g0(m), TOK, lambda k: U0h[:, k, :], lambda k: U0l[:, k, :])
                if m < 2:
                    ada(g0(m) + 3, g0(m) + 3, 46 + m, bank[7])
            norm_sum(4, TOK)

            def conv_tile(t, n, s, u, kind):
                if late(t, 2):
                    pe.wait_ge(conv_up, t - 1)
                c = slice(CTX, TOK) if kind == "C" else slice(0, TOK)
                tile(n, s, bank[u][:, c], lambda k: H1h[:, k, c], lambda k: H1l[:, k, c], 0, 8, True, True).then_inc(w_used, 1)

            def to_tokens(t, u, r):
                pe.wait_ge(conv_y, t + 1)
                if late(r, 2):
                    pe.wait_ge(conv_ev, r - 1)
                for k in range(4):
                    last = nc.tensor.transpose(bank[2 + u][:, 128 * k:128 * k + 128], T[:, 2 + u, 128 * k:128 * k + 128], tabv("ident"))
                last.then_inc(conv_tr, 1)

            pair(BC, (bank[0][:, :], bank[1][:, :]), lambda k: H1h[:, k, :], lambda k: H1l[:, k, :], KD, 1, NB[4])
            for t in range(1, 8):
                if t >= 2:
                    conv_tile(t, BC + t, BC + t, t % 2, "BC"[t // 4])
                if 1 <= t <= 4:
                    to_tokens(t - 1, (t - 1) % 2, t - 1)
            pe.wait_ge(w_lo, DT + 1)
            for k in range(8):
                w, sl = slice(64 * k, 64 * k + 64), DT % RING
                last = three(bank[4][0:64, :], wh[sl][:, w], wl[sl][:, w], H1h[:, k, :], H1l[:, k, :], k == 0, k == 7)
            last.then_inc(w_used, 1)
            conv_tile(8, XS, XS, 0, "x")
            pe.wait_ge(dt_cp, 1)
            for t in range(4):
                last = nc.tensor.transpose(bank[5][:, 64 * t:64 * t + 64], dtT[:, 128 * t:128 * t + 128], tab[0:64, 0:64])
            last.then_inc(dt_tr, 1)
            conv_tile(9, XS + 1, XS + 1, 1, "x")
            for u in range(2, 4):
                conv_tile(8 + u, XS + u, XS + u, u % 2, "x")
                to_tokens(6 + u, u % 2, 2 + u)
            with pe.Fori(1, 4) as i:
                for u in range(4):
                    conv_tile(8 + 4 * i + u, XS + 4 * i + u, XS + u, u % 2, "x")
                    to_tokens(6 + 4 * i + u, u % 2, 2 + 4 * i + u)
            pe.wait_ge(dt_dve, 1)
            pe.wait_ge(dt_dve, 12)
            F, B = slice(0, SH), slice(SH, 2 * SH)
            sums = (("gt", 0, F, 1), ("lt", 0, B, None), ("gt", 1, F, None), ("lt", 1, B, 0),
                    ("gt", 2, F, None), ("lt", 3, B, None), ("le", 2, F, None), ("ge", 2, B, None),
                    ("le", 3, F, None), ("ge", 3, B, None), (None, 2, F, None), (None, 3, B, None))
            for q, (name, tt, hs, whole) in enumerate(sums):
                o = bank[6][:, SH * q:SH * q + SH]
                last = mm(o, tabv(name) if name else ones[:, :], dtA[:, tt, hs], start=True, stop=whole is None)
                if whole is not None:
                    last = mm(o, ones[:, :], dtA[:, whole, hs], start=False, stop=True)
            last.then_inc(cum_mm, 1)
            pe.wait_ge(ct_lo, 8)
            pe.wait_ge(conv_up, 23)
            for c in range(2):
                cs = slice(128 * c, 128 * c + 128)
                for g in range(GROUPS):
                    last = three(bank[CB_BANK[c]][:, 128 * g:128 * g + 128], BTh[:, g, cs], BTl[:, g, cs], CTh[:, g, cs], CTl[:, g, cs], True, True)
                last.then_inc(cb_mm, 1)

            def z_tile(t, u):
                tile(ZS + t, ZS + u, bank[4 + u % 2][:, 0:LAT], lambda k: H1h[:, k, CTX:TOK],
                     lambda k: H1l[:, k, CTX:TOK], 0, 8, True, True).then_inc(w_used, 1)

            z_tile(0, 0)
            to_tokens(22, 0, 18)
            to_tokens(23, 1, 19)
            z_tile(1, 1)
            for u in range(2, 4):
                pe.wait_ge(conv_y, 23 + u)
                z_tile(u, u)
            with pe.Fori(1, 4) as i:
                for u in range(4):
                    pe.wait_ge(conv_y, 23 + 4 * i + u)
                    z_tile(4 * i + u, u)

            def decay(m, d_):
                i = 2 * m + d_
                pe.wait_ge(mk_hi, i + 1)
                pe.wait_ge(mk_lo, i + 1)
                if d_ == 0 and m >= 1:
                    pe.wait_ge(dec_exp, 2 * m)
                for b in range(2):
                    for part in (mh, ml):
                        last = mm(bank[6 + b][:, :], maskr[:, d_, :], part[:, 4 * b:4 * b + 4, :].rearrange("p h q -> p (h q)"),
                                  start=d_ == 0 and part is mh, stop=d_ == 1 and part is ml)
                last.then_inc(dec_mm, 1)

            def states(e):
                g, d_ = divmod(e, 2)
                if e:
                    pe.wait_ge(st_sum, e)
                for s, (tt, _row) in enumerate(STATE_TILES[d_]):
                    i = 3 * e + s
                    pe.wait_ge(xs_lo, i + 1)
                    three(bank[s // 2][:, :], Bth[:, tt, g, :], Btl[:, tt, g, :], xsh[:, s, :], xsl[:, s, :],
                          s != 1, s != 0).then_inc(st_mm, 1)

            def carried(e):
                g, d_ = divmod(e, 2)
                for z in range(2):
                    c = z if d_ == 0 else 1 - z
                    pe.wait_ge(st_lo, 2 * e + z + 1)
                    if e:
                        pe.wait_ge(off_rd, 2 * e + z - 1)
                    cs = slice(128 * c, 128 * c + 128)
                    three(bank[2 + z][:, :], CTh[:, g, cs], CTl[:, g, cs], hh[:, z, :], hl[:, z, :], True, True).then_inc(off_mm, 1)

            def diagonal(m):
                g, c = divmod(m, 2)
                pe.wait_ge(xg_lo, g + 1)
                pe.wait_ge(W_lo, m + 1)
                if m:
                    pe.wait_ge(y_done, m)
                for h in range(GH):
                    xs = slice(64 * h, 64 * h + 64)
                    last = three(bank[4][:, xs], Wh[:, h, :], Wl[:, h, :], xgh[:, c, xs], xgl[:, c, xs], True, True)
                last.then_inc(dg_mm, 1)

            def to_features(m):
                g, c = divmod(m, 2)
                pe.wait_ge(y_done, m + 1)
                if m:
                    pe.wait_ge(yt_done, m)
                for f in range(4):
                    last = nc.tensor.transpose(bank[5][:, 128 * f:128 * f + 128], Y[:, 2 * (g % 2) + c, 128 * f:128 * f + 128], tabv("ident"))
                last.then_inc(yt_mm, 1)

            pe.wait_ge(masks_r, 2)
            pe.wait_ge(cum_exp, 1)
            pe.wait_ge(cb_done, 4)
            decay(0, 0)
            states(0)
            decay(0, 1)
            carried(0)
            states(1)
            decay(1, 0)
            decay(1, 1)
            carried(1)
            for m in range(8):
                if m < 6:
                    states(m + 2)
                    decay(m + 2, 0)
                diagonal(m)
                if m < 6:
                    decay(m + 2, 1)
                to_features(m)
                if m < 6:
                    carried(m + 2)
            pe.wait_ge(root, 5)
            pe.wait_ge(gate_acc, 2)
            for g in (0, 3):
                if g:
                    pe.wait_ge(gate_sq, GROUPS)
                for f in range(4):
                    last = mm(bank[6][:, 0:LAT], ones[:, :], squared(g)[:, f // 2, 256 * (f % 2):256 * (f % 2) + 256],
                              start=g + f == 0, stop=g + f == 6)
            last.then_inc(sum_done, 1)
            pair(SO, (bank[0][:, 0:LAT], bank[1][:, 0:LAT]), lambda k: Hyh[:, k, :], lambda k: Hyl[:, k, :], KI, 2, NB[5])
            for m in range(2, 8):
                pe.wait_ge(added, 15 + m)
                for r in range(2):
                    tile(SO + 2 * m + r, SO + 2 * m + r, bank[m % 2][:, 0:LAT], lambda k: Hyh[:, k, :], lambda k: Hyl[:, k, :],
                         8 * r, 8, r == 0, r == 1).then_inc(w_used, 1)
            norm_sum(6, LAT)
            h2 = (lambda k: H2h[:, k, :]), (lambda k: H2l[:, k, :])
            for j in range(2):
                ffn(j, KH + j, j, LAT, *h2, F1 + 2 * j, F1 + 2 * j, NB[6] if j == 0 else None)
            with pe.Fori(1, KH // 2) as i:
                for u in range(2):
                    ffn(2 * i + u, KH + 2 * i + u, u, LAT, *h2, F1 + 4 * i + 2 * u, F1 + 2 * u, None)
            pe.wait_ge(hid_lo, 2 * KH)
            for m in range(8):
                w2(24, m, G1 + 3 * m, LAT, lambda k: U1h[:, k, :], lambda k: U1l[:, k, :])
            norm_sum(7, LAT)


def tiles(w, cols=128):
    k, m = w.shape
    return np.ascontiguousarray(w.reshape(k // 128, 128, m // cols, cols).transpose(2, 1, 0, 3).reshape(m // cols, 128, -1))


def columns(v):
    return v.reshape(-1, 128).T


def swap_halves():
    return np.concatenate([np.arange(8, 16), np.arange(0, 8), np.arange(24, 32), np.arange(16, 24)])


def shape_tables():
    i = np.arange(128)
    r, c = i[:, None], i[None, :]
    t = np.zeros((128, NTAB), np.float32)
    for name, m in (("ident", r == c), ("gt", r > c), ("lt", r < c), ("le", r <= c), ("ge", r >= c)):
        t[:, TAB[name]:TAB[name] + 128] = m
    tok = np.arange(LAT)
    inv = (10000.0 ** (-np.arange(8, dtype=np.float32) * 2.0 / 16)).astype(np.float32)
    for axis, pos in ((0, tok // GRID_W), (1, tok % GRID_W)):
        ang = (pos.astype(np.float32)[None, :] * inv[:, None]).astype(np.float32)
        for half, sign in ((0, -1.0), (1, 1.0)):
            at = 16 * axis + 8 * half
            t[64 + at:72 + at, TAB["cos"]:TAB["cos"] + LAT] = np.cos(ang)
            t[96 + at:104 + at, TAB["sin"]:TAB["sin"] + LAT] = sign * np.sin(ang)
    return t


def lay_out(i):
    o = {}
    o["xT"] = np.concatenate([i["ctx"][0], i["x"][0]], axis=0).T.reshape(KD, 128, TOK).transpose(1, 0, 2)
    cw, cbias = i["ssd_conv_w"][0], i["ssd_conv_b"][0]
    order = np.concatenate([np.arange(INNER, INNER + 1024), np.arange(INNER)])
    cwt = cw[:, order].reshape(5, 24, 128).transpose(2, 1, 0).reshape(128, 120)
    o["par"] = np.concatenate([
        columns(i["c"][0]), columns(i["c_ctx"]), columns(i["ada_b"].reshape(-1)), columns(i["norm_mix"].reshape(-1)),
        columns(i["norm_ffn"].reshape(-1)), columns(i["mla_q_norm"][0]), columns(i["mla_kv_norm"][0]), cwt,
        columns(cbias[order]), columns(i["ssd_norm"][0]), columns(i["final_norm"])], axis=1)
    r = np.concatenate([i["ssd_dt_bias"][0].reshape(-1), i["ssd_a_log"][0].reshape(-1), i["ssd_d"][0]])
    o["rows"] = np.broadcast_to(r, (128, 160))
    o["tab"] = shape_tables()
    o["ada_w"] = np.concatenate([tiles(w, 256) for w in i["ada_w"]]).reshape(48, 128, 2, 1024).transpose(0, 2, 1, 3).reshape(96, 128, 1024)
    w = i["mla_w_in"][0]
    o["w_in"] = tiles(np.concatenate([w[:, 512:768], w[:, 704:800], w[:, 768 + swap_halves()], w[:, 0:512]], axis=1))
    q = i["mla_w_uq"][0].reshape(512, HEADS, QKD)
    o["w_uq"] = tiles(np.concatenate([q, q[:, :, 64 + swap_halves()]], axis=2).reshape(512, -1))
    kv = i["mla_w_ukv"][0].reshape(256, HEADS, 2, 64)
    o["w_uk"] = tiles(kv[:, :, 0].reshape(256, -1), 64)
    o["w_uv"] = kv[:, :, 1].reshape(2, 128, 1024)
    o["w_o"] = tiles(i["mla_w_o"][0])
    for n in ("w1", "w3", "w2"):
        o[n] = np.concatenate([tiles(w) for w in i["ffn_" + n]])
    w = i["ssd_w_in"][0]
    o["w_z"] = tiles(w[:, 0:INNER])
    xbc = w[:, INNER:INNER + 3072]
    o["w_xbc"] = tiles(xbc[:, order])
    o["w_dt"] = tiles(w[:, INNER + 3072:], 64)[0]
    o["w_so"] = tiles(i["ssd_w_o"][0]).reshape(8, 128, 2, 1024).transpose(0, 2, 1, 3).reshape(16, 128, 1024)
    return {k: np.ascontiguousarray(v) for k, v in o.items()}


def kernel(**inputs):
    import concourse.bacc as bacc
    from concourse import mybir
    from concourse.bass_utils import run_bass_kernel_spmd

    nc = bacc.Bacc("TRN2", target_bir_lowering=False, num_devices=1, dynamic_dma_scratch_size=1024)
    arrays = lay_out({k: np.asarray(v) for k, v in inputs.items()})
    aps = {k: nc.dram_tensor("in_" + k, v.shape, mybir.dt.from_np(v.dtype), kind="ExternalInput").ap() for k, v in arrays.items()}
    out = nc.dram_tensor("out", (128, KD, LAT), mybir.dt.float32, kind="ExternalOutput").ap()
    program(nc, aps, out)
    r = run_bass_kernel_spmd(nc, [{"in_" + k: v for k, v in arrays.items()}], core_ids=[0])
    got = r.results[0]["out"]
    return np.ascontiguousarray(got.transpose(2, 1, 0).reshape(1, LAT, D))
```
